# Optimizing a Trainium2 kernel written in Bass

```python
import jax, jax.numpy as jnp
from jax import lax
import numpy as np
import math

D_MODEL = 1024
BATCH = 1
SEQ = 256
DEPTH = 1

N_MIXERS = 4
EPS = 1e-6
CONV_WIDTH = 31
HGRN_EXPAND = 128
HGRN_HEADS = D_MODEL // HGRN_EXPAND
HGRN_CHUNK = 64
POOL_WINDOWS = (2, 4, 8, 16)
POOL_GROUPS = len(POOL_WINDOWS)
POOL_DIM = D_MODEL // POOL_GROUPS
SB_HEADS = 16
SB_HEAD_DIM = D_MODEL // SB_HEADS
SB_BLOCK = 128
MOE_GROUPS = 4
MOE_EXPERTS_PER_GROUP = 8
MOE_EXPERTS = MOE_GROUPS * MOE_EXPERTS_PER_GROUP
MOE_TOP_K = 2
MOE_HIDDEN = D_MODEL // 2
MOE_BLOCK = 128


def _n_layers_of(m):
    return (DEPTH - m + N_MIXERS - 1) // N_MIXERS

def rmsnorm(x, g):
    xf = x.astype(jnp.float32)
    y = xf * lax.rsqrt(jnp.mean(xf * xf, axis=-1, keepdims=True) + EPS) * g.astype(jnp.float32)
    return y.astype(x.dtype)

def layernorm(x, g, b):
    xf = x.astype(jnp.float32)
    mu = jnp.mean(xf, axis=-1, keepdims=True)
    xc = xf - mu
    y = xc * lax.rsqrt(jnp.mean(xc * xc, axis=-1, keepdims=True) + EPS) * g + b
    return y.astype(x.dtype)

def conformer_conv(h, w_in, b_in, w_dw, b_dw, ln_g, ln_b, w_out):
    u = h @ w_in + b_in
    a, gt = jnp.split(u, 2, axis=-1)
    u = a * jax.nn.sigmoid(gt)
    y = lax.conv_general_dilated(
        u, w_dw[:, None, :], window_strides=(1,),
        padding=[(CONV_WIDTH - 1, 0)],
        dimension_numbers=('NWC', 'WIO', 'NWC'),
        feature_group_count=D_MODEL) + b_dw
    y = jax.nn.silu(layernorm(y, ln_g, ln_b))
    return (y @ w_out).astype(h.dtype)

def hgrn_lower_bounds(logits):
    p = jax.nn.softmax(logits.astype(jnp.float32), axis=0)
    cum = jnp.cumsum(p, axis=0)
    return cum - cum[0:1]

def hgrn2(h, w_in, lb, norm_g, w_out):
    B, S, _ = h.shape
    H, dh, C = HGRN_HEADS, HGRN_EXPAND, HGRN_CHUNK
    n_chunk = S // C
    q, f, i_in, g = jnp.split((h @ w_in).astype(jnp.float32), 4, axis=-1)
    q = jax.nn.silu(q)
    forget = lb + (1.0 - lb) * jax.nn.sigmoid(f)
    log_f = jnp.log(forget)
    k = (1.0 - lb) * jax.nn.sigmoid(-f)

    def chunks(t):
        return t.reshape(B, n_chunk, C, H, dh).transpose(1, 0, 3, 2, 4)

    causal = jnp.tril(jnp.ones((C, C), bool))[:, :, None]

    def step(state, inp):
        qc, kc, vc, lfc = inp
        b = jnp.cumsum(lfc, axis=2)
        o_inter = jnp.einsum('bhtk,bhkv->bhtv', qc * jnp.exp(b), state)
        rel = jnp.where(causal, b[:, :, :, None, :] - b[:, :, None, :, :], -jnp.inf)
        scores = jnp.einsum('bhtk,bhsk,bhtsk->bhts', qc, kc, jnp.exp(rel))
        o_intra = jnp.einsum('bhts,bhsv->bhtv', scores, vc)
        b_end = b[:, :, -1:, :]
        state = (jnp.exp(b_end[:, :, 0, :, None]) * state
                 + jnp.einsum('bhsk,bhsv->bhkv', kc * jnp.exp(b_end - b), vc))
        return state, o_inter + o_intra

    state0 = jnp.zeros((B, H, dh, dh), jnp.float32)
    _, o = lax.scan(step, state0, (chunks(q), chunks(k), chunks(i_in), chunks(log_f)))
    o = o.transpose(1, 0, 3, 2, 4).reshape(B, S, H, dh)
    o = o * lax.rsqrt(jnp.mean(o * o, axis=-1, keepdims=True) + EPS) * norm_g.reshape(H, dh)
    o = o.reshape(B, S, D_MODEL) * jax.nn.silu(g)
    return (o.astype(h.dtype) @ w_out).astype(h.dtype)

def multiscale_pool(h, w_grp, b_grp, ls):
    B, S, _ = h.shape
    hf = h.astype(jnp.float32).reshape(B, S, POOL_GROUPS, POOL_DIM)
    cs0 = jnp.pad(jnp.cumsum(hf, axis=1), ((0, 0), (1, 0), (0, 0), (0, 0)))
    pos = jnp.arange(S)
    outs = []
    for gi, w in enumerate(POOL_WINDOWS):
        c_g = cs0[:, :, gi]
        upper = c_g[:, 1:]
        lower = jnp.pad(c_g, ((0, 0), (w - 1, 0), (0, 0)))[:, :S]
        count = jnp.minimum(pos + 1, w).astype(jnp.float32)[None, :, None]
        outs.append((upper - lower) / count - hf[:, :, gi])
    pooled = jnp.stack(outs, axis=2)
    y = jnp.einsum('bsgc,gcd->bsgd', pooled, w_grp.astype(jnp.float32))
    y = y.reshape(B, S, D_MODEL) + b_grp
    return (y * ls).astype(h.dtype)

def stick_breaking_attention(h, w_qkv, w_out):
    B, S, _ = h.shape
    qkv = (h @ w_qkv).reshape(B, S, 3, SB_HEADS, SB_HEAD_DIM)
    q = qkv[:, :, 0].transpose(0, 2, 1, 3)
    k = qkv[:, :, 1].transpose(0, 2, 1, 3)
    v = qkv[:, :, 2].transpose(0, 2, 1, 3)
    n_blk = S // SB_BLOCK
    q_blocks = q.reshape(B, SB_HEADS, n_blk, SB_BLOCK, SB_HEAD_DIM).transpose(2, 0, 1, 3, 4)
    key_pos = jnp.arange(S)
    scale = SB_HEAD_DIM ** -0.5

    def one_block(args):
        qb, bi = args
        z = jnp.einsum('bhtd,bhsd->bhts', qb, k).astype(jnp.float32) * scale
        q_pos = bi * SB_BLOCK + jnp.arange(SB_BLOCK)
        strict = key_pos[None, :] < q_pos[:, None]
        log_keep = jnp.where(strict, jax.nn.log_sigmoid(-z), 0.0)
        later = lax.cumsum(log_keep, axis=3, reverse=True) - log_keep
        weights = jnp.where(strict, jnp.exp(jax.nn.log_sigmoid(z) + later), 0.0)
        return jnp.einsum('bhts,bhsd->bhtd', weights.astype(v.dtype), v)

    o = lax.map(one_block, (q_blocks, jnp.arange(n_blk)))
    o = o.transpose(1, 0, 3, 2, 4).reshape(B, S, D_MODEL)
    return (o @ w_out).astype(h.dtype)

def hier_moe(h, w_rg, b_rg, w_re, b_re, w_gate, w_up, w_down):
    B, S, D = h.shape
    T = B * S
    xt = h.reshape(T, D)
    grp_logits = (xt @ w_rg + b_rg).astype(jnp.float32)
    grp = jnp.argmax(grp_logits, axis=-1)
    grp_p = jnp.take_along_axis(jax.nn.softmax(grp_logits, axis=-1), grp[:, None], axis=1)[:, 0]
    exp_logits = (xt @ w_re + b_re).astype(jnp.float32).reshape(T, MOE_GROUPS, MOE_EXPERTS_PER_GROUP)
    in_grp = jnp.take_along_axis(exp_logits, grp[:, None, None], axis=1)[:, 0]
    top_val, top_idx = lax.top_k(in_grp, MOE_TOP_K)
    gate = grp_p[:, None] * jax.nn.softmax(top_val, axis=-1)
    expert = grp[:, None] * MOE_EXPERTS_PER_GROUP + top_idx

    n_assign = T * MOE_TOP_K
    e_flat = expert.reshape(n_assign).astype(jnp.int32)
    g_flat = gate.reshape(n_assign)
    t_flat = jnp.repeat(jnp.arange(T, dtype=jnp.int32), MOE_TOP_K)
    order = jnp.argsort(e_flat)
    e_s, t_s, g_s = e_flat[order], t_flat[order], g_flat[order]
    counts = jnp.bincount(e_flat, length=MOE_EXPERTS).astype(jnp.int32)
    padded = ((counts + MOE_BLOCK - 1) // MOE_BLOCK) * MOE_BLOCK
    seg_start = jnp.cumsum(counts) - counts
    pad_end = jnp.cumsum(padded)
    pad_start = pad_end - padded
    dest = pad_start[e_s] + (jnp.arange(n_assign, dtype=jnp.int32) - seg_start[e_s])
    n_slots = n_assign + MOE_EXPERTS * MOE_BLOCK
    n_blk = n_slots // MOE_BLOCK
    slot_tok = jnp.full((n_slots,), T, jnp.int32).at[dest].set(t_s)
    slot_gate = jnp.zeros((n_slots,), jnp.float32).at[dest].set(g_s)
    blk_start = jnp.arange(n_blk, dtype=jnp.int32) * MOE_BLOCK
    blk_expert = jnp.minimum(jnp.searchsorted(pad_end, blk_start, side='right'),
                             MOE_EXPERTS - 1).astype(jnp.int32)
    x_pad = jnp.concatenate([xt, jnp.zeros((1, D), xt.dtype)], axis=0)
    xs = x_pad[slot_tok].reshape(n_blk, MOE_BLOCK, D)

    def run_block(args):
        xb, e = args
        hid = jax.nn.silu(xb @ w_gate[e]) * (xb @ w_up[e])
        return hid @ w_down[e]

    ys = lax.map(run_block, (xs, blk_expert)).reshape(n_slots, D)
    out = jnp.zeros((T + 1, D), jnp.float32).at[slot_tok].add(
        ys.astype(jnp.float32) * slot_gate[:, None])[:T]
    return out.reshape(B, S, D).astype(h.dtype)

def first_inputs(seed: int = 0) -> dict:
    key = jax.random.key(seed)
    ks = iter(jax.random.split(key, 40))

    def nrm(shape, scale):
        return jax.random.normal(next(ks), shape, jnp.float32) * scale

    D = D_MODEL
    NA, NB, NC, ND = (_n_layers_of(m) for m in range(N_MIXERS))
    inv = D ** -0.5
    E, F = MOE_EXPERTS, MOE_HIDDEN
    return {
        "x": nrm((BATCH, SEQ, D), 1.0),
        "c": nrm((BATCH, D), 1.0),
        "ada_w": nrm((DEPTH, D, 6 * D), 0.5 * inv),
        "ada_b": nrm((DEPTH, 6 * D), 0.02),
        "norm_mix_g": 1.0 + nrm((DEPTH, D), 0.05),
        "norm_ffn_g": 1.0 + nrm((DEPTH, D), 0.05),
        "final_g": 1.0 + nrm((D,), 0.05),
        "conv_w_in": nrm((NA, D, 2 * D), inv),
        "conv_b_in": nrm((NA, 2 * D), 0.02),
        "conv_w_dw": nrm((NA, CONV_WIDTH, D), CONV_WIDTH ** -0.5),
        "conv_b_dw": nrm((NA, D), 0.02),
        "conv_ln_g": 1.0 + nrm((NA, D), 0.05),
        "conv_ln_b": nrm((NA, D), 0.02),
        "conv_w_out": nrm((NA, D, D), inv),
        "hgrn_w_in": nrm((NB, D, 4 * D), inv),
        "hgrn_lb_logits": nrm((DEPTH, D), 0.5),
        "hgrn_norm_g": 1.0 + nrm((NB, D), 0.05),
        "hgrn_w_out": nrm((NB, D, D), inv),
        "pool_w": nrm((NC, POOL_GROUPS, POOL_DIM, POOL_DIM), POOL_DIM ** -0.5),
        "pool_b": nrm((NC, D), 0.02),
        "pool_scale": 1.0 + nrm((NC, D), 0.1),
        "sb_w_qkv": nrm((ND, D, 3 * D), inv),
        "sb_w_out": nrm((ND, D, D), inv),
        "moe_w_rg": nrm((DEPTH, D, MOE_GROUPS), inv),
        "moe_b_rg": nrm((DEPTH, MOE_GROUPS), 0.01),
        "moe_w_re": nrm((DEPTH, D, E), inv),
        "moe_b_re": nrm((DEPTH, E), 0.01),
        "moe_w_gate": nrm((DEPTH, E, D, F), inv),
        "moe_w_up": nrm((DEPTH, E, D, F), inv),
        "moe_w_down": nrm((DEPTH, E, F, D), F ** -0.5),
    }

def first_block(x, c, ada_w, ada_b, norm_mix_g, norm_ffn_g, final_g,
              conv_w_in, conv_b_in, conv_w_dw, conv_b_dw, conv_ln_g, conv_ln_b, conv_w_out,
              hgrn_w_in, hgrn_lb_logits, hgrn_norm_g, hgrn_w_out,
              pool_w, pool_b, pool_scale,
              sb_w_qkv, sb_w_out,
              moe_w_rg, moe_b_rg, moe_w_re, moe_b_re, moe_w_gate, moe_w_up, moe_w_down):
    c_act = jax.nn.silu(c)
    lb_all = hgrn_lower_bounds(hgrn_lb_logits)
    for i in range(DEPTH):
        m, j = i % N_MIXERS, i // N_MIXERS
        mod = c_act @ ada_w[i] + ada_b[i]
        sh1, sc1, g1, sh2, sc2, g2 = [t[:, None, :] for t in jnp.split(mod, 6, axis=-1)]
        h = rmsnorm(x, norm_mix_g[i]) * (1 + sc1) + sh1
        if m == 0:
            y = conformer_conv(h, conv_w_in[j], conv_b_in[j], conv_w_dw[j], conv_b_dw[j],
                               conv_ln_g[j], conv_ln_b[j], conv_w_out[j])
        elif m == 1:
            y = hgrn2(h, hgrn_w_in[j], lb_all[i], hgrn_norm_g[j], hgrn_w_out[j])
        elif m == 2:
            y = multiscale_pool(h, pool_w[j], pool_b[j], pool_scale[j])
        else:
            y = stick_breaking_attention(h, sb_w_qkv[j], sb_w_out[j])
        x = x + g1 * y
        h = rmsnorm(x, norm_ffn_g[i]) * (1 + sc2) + sh2
        x = x + g2 * hier_moe(h, moe_w_rg[i], moe_b_rg[i], moe_w_re[i], moe_b_re[i],
                              moe_w_gate[i], moe_w_up[i], moe_w_down[i])
    return rmsnorm(x, final_g)


DEPTH_2 = 2

N_A = DEPTH_2 // 2
N_B = DEPTH_2 - N_A

H_A = 16
NOPE_A = 64
ROPE_A = 32
V_A = 64
Q_LORA = 768
KV_LORA = 256
WIDTH_A = H_A * V_A
QBLOCK = 128

H_B = 16
HD_B = 64
WIDTH_B = H_B * HD_B
MOBA_BLOCK = 256
MOBA_TOPK = 3
QCHUNK = 8

THETA = 10000.0
LN_EPS = 1e-5
RMS_EPS = 1e-6
ALPHA = (2 * DEPTH_2) ** 0.25
BETA = (8 * DEPTH_2) ** (-0.25)


def rope_tables(seq, dim):
    inv = THETA ** (-jnp.arange(0, dim, 2, dtype=jnp.float32) / dim)
    ang = jnp.arange(seq, dtype=jnp.float32)[:, None] * inv[None, :]
    ang = jnp.concatenate([ang, ang], axis=-1)
    return jnp.cos(ang), jnp.sin(ang)

def apply_rope(x, cos, sin):
    x1, x2 = jnp.split(x, 2, axis=-1)
    rot = jnp.concatenate([-x2, x1], axis=-1)
    return (x * cos + rot * sin).astype(x.dtype)

def layer_norm(x, g, b):
    xf = x.astype(jnp.float32)
    mu = jnp.mean(xf, axis=-1, keepdims=True)
    var = jnp.mean(jnp.square(xf - mu), axis=-1, keepdims=True)
    return ((xf - mu) * lax.rsqrt(var + LN_EPS) * g + b).astype(x.dtype)

def rms_norm(x, g):
    xf = x.astype(jnp.float32)
    return (xf * lax.rsqrt(jnp.mean(jnp.square(xf), axis=-1, keepdims=True) + RMS_EPS) * g).astype(x.dtype)

def mla_mixer(x, w_in, q_norm, kv_norm, w_uq, w_ukv, w_o, cos, sin):
    B, S, _ = x.shape
    h = x @ w_in
    c_q, c_kv, k_rope, gate = jnp.split(h, [Q_LORA, Q_LORA + KV_LORA, Q_LORA + KV_LORA + ROPE_A], axis=-1)
    q = (rms_norm(c_q, q_norm) @ w_uq).reshape(B, S, H_A, NOPE_A + ROPE_A)
    q_nope = q[..., :NOPE_A]
    q_rope = apply_rope(q[..., NOPE_A:], cos[None, :, None, :], sin[None, :, None, :])
    kv = (rms_norm(c_kv, kv_norm) @ w_ukv).reshape(B, S, H_A, NOPE_A + V_A)
    k_nope, v = kv[..., :NOPE_A], kv[..., NOPE_A:]
    k_rope = apply_rope(k_rope, cos[None], sin[None])
    scale = (NOPE_A + ROPE_A) ** -0.5
    outs = []
    for i in range(S // QBLOCK):
        q0, kend = i * QBLOCK, (i + 1) * QBLOCK
        s = (jnp.einsum('bqhd,bkhd->bhqk', q_nope[:, q0:kend], k_nope[:, :kend])
             + jnp.einsum('bqhr,bkr->bhqk', q_rope[:, q0:kend], k_rope[:, :kend])).astype(jnp.float32) * scale
        q_pos = q0 + jnp.arange(QBLOCK)
        mask = jnp.arange(kend)[None, :] <= q_pos[:, None]
        p = jax.nn.softmax(jnp.where(mask, s, -jnp.inf), axis=-1).astype(v.dtype)
        outs.append(jnp.einsum('bhqk,bkhd->bqhd', p, v[:, :kend]))
    o = jnp.concatenate(outs, axis=1).reshape(B, S, WIDTH_A)
    return (o * jax.nn.silu(gate)) @ w_o

def moba_shared_kv(x, w_kv, cos, sin):
    B, S, _ = x.shape
    kv = x @ w_kv
    k = kv[..., :WIDTH_B].reshape(B, S, H_B, HD_B)
    v = kv[..., WIDTH_B:].reshape(B, S, H_B, HD_B)
    k = apply_rope(k, cos[None, :, None, :], sin[None, :, None, :])
    nb = -(-S // MOBA_BLOCK)
    pad = nb * MOBA_BLOCK - S
    k = jnp.pad(k, ((0, 0), (0, pad), (0, 0), (0, 0)))
    v = jnp.pad(v, ((0, 0), (0, pad), (0, 0), (0, 0)))
    k_blocks = k.reshape(B, nb, MOBA_BLOCK, H_B, HD_B).transpose(0, 3, 1, 2, 4)
    v_blocks = v.reshape(B, nb, MOBA_BLOCK, H_B, HD_B).transpose(0, 3, 1, 2, 4)
    cnt = jnp.clip(S - jnp.arange(nb) * MOBA_BLOCK, 1, MOBA_BLOCK).astype(jnp.float32)
    k_mean = (jnp.sum(k_blocks.astype(jnp.float32), axis=3) / cnt[:, None]).astype(k.dtype)
    return k_blocks, v_blocks, k_mean

def moba_mixer(x, k_blocks, v_blocks, k_mean, w_in, w_o, cos, sin):
    B, S, _ = x.shape
    nb = k_blocks.shape[2]
    h = x @ w_in
    q, gate = h[..., :WIDTH_B], h[..., WIDTH_B:]
    q = apply_rope(q.reshape(B, S, H_B, HD_B), cos[None, :, None, :], sin[None, :, None, :])
    q = q.transpose(0, 2, 1, 3)
    gs = jnp.einsum('bhsd,bhnd->bhsn', q, k_mean).astype(jnp.float32)
    q_blk = jnp.arange(S) // MOBA_BLOCK
    past = jnp.arange(nb)[None, :] < q_blk[:, None]
    gs = jnp.where(past, gs, -jnp.inf)
    topk = min(MOBA_TOPK, nb)
    _, idx = lax.top_k(gs, topk)
    valid = idx < q_blk[:, None]
    n_chunks = S // QCHUNK
    q_c = q.reshape(B, H_B, n_chunks, QCHUNK, HD_B).transpose(2, 0, 1, 3, 4)
    idx_c = idx.reshape(B, H_B, n_chunks, QCHUNK, topk).transpose(2, 0, 1, 3, 4)
    valid_c = valid.reshape(B, H_B, n_chunks, QCHUNK, topk).transpose(2, 0, 1, 3, 4)
    starts = jnp.arange(n_chunks, dtype=jnp.int32) * QCHUNK
    b_ix = jnp.arange(B)[:, None, None, None]
    h_ix = jnp.arange(H_B)[None, :, None, None]
    scale = HD_B ** -0.5

    def attend(args):
        qq, ii, vv, start = args
        k_sel = k_blocks[b_ix, h_ix, ii]
        v_sel = v_blocks[b_ix, h_ix, ii]
        qb = start // MOBA_BLOCK
        k_own = lax.dynamic_index_in_dim(k_blocks, qb, axis=2, keepdims=False)
        v_own = lax.dynamic_index_in_dim(v_blocks, qb, axis=2, keepdims=False)
        s_sel = jnp.einsum('bhcd,bhctkd->bhctk', qq, k_sel).astype(jnp.float32) * scale
        s_sel = jnp.where(vv[..., None], s_sel, -jnp.inf).reshape(B, H_B, QCHUNK, topk * MOBA_BLOCK)
        s_own = jnp.einsum('bhcd,bhkd->bhck', qq, k_own).astype(jnp.float32) * scale
        k_pos = qb * MOBA_BLOCK + jnp.arange(MOBA_BLOCK)
        q_pos = start + jnp.arange(QCHUNK)
        s_own = jnp.where(k_pos[None, :] <= q_pos[:, None], s_own, -jnp.inf)
        p = jax.nn.softmax(jnp.concatenate([s_sel, s_own], axis=-1), axis=-1).astype(qq.dtype)
        p_sel = p[..., :topk * MOBA_BLOCK].reshape(B, H_B, QCHUNK, topk, MOBA_BLOCK)
        p_own = p[..., topk * MOBA_BLOCK:]
        return (jnp.einsum('bhctk,bhctkd->bhcd', p_sel, v_sel)
                + jnp.einsum('bhck,bhkd->bhcd', p_own, v_own))

    o = lax.map(attend, (q_c, idx_c, valid_c, starts))
    o = o.transpose(1, 0, 3, 2, 4).reshape(B, S, WIDTH_B)
    return (o * jax.nn.silu(gate)) @ w_o

def second_inputs(seed: int = 0) -> dict:
    key = jax.random.key(seed)
    ks = jax.random.split(key, 14)

    def nrm(k, shape, fan_in, scale=1.0):
        return jax.random.normal(k, shape, jnp.float32) * (scale * fan_in ** -0.5)

    x = jax.random.normal(ks[0], (BATCH, SEQ, D_MODEL), jnp.float32)
    mla_w_in = nrm(ks[1], (N_A, D_MODEL, Q_LORA + KV_LORA + ROPE_A + WIDTH_A), D_MODEL)
    mla_q_norm = 1.0 + 0.02 * jax.random.normal(ks[2], (N_A, Q_LORA), jnp.float32)
    mla_kv_norm = 1.0 + 0.02 * jax.random.normal(ks[3], (N_A, KV_LORA), jnp.float32)
    mla_w_uq = nrm(ks[4], (N_A, Q_LORA, H_A * (NOPE_A + ROPE_A)), Q_LORA)
    mla_w_ukv = nrm(ks[5], (N_A, KV_LORA, H_A * (NOPE_A + V_A)), KV_LORA)
    mla_w_o = nrm(ks[6], (N_A, WIDTH_A, D_MODEL), WIDTH_A, BETA)
    moba_w_kv = nrm(ks[7], (D_MODEL, 2 * WIDTH_B), D_MODEL)
    moba_w_in = nrm(ks[8], (N_B, D_MODEL, 2 * WIDTH_B), D_MODEL)
    moba_w_o = nrm(ks[9], (N_B, WIDTH_B, D_MODEL), WIDTH_B, BETA)
    ln_g = 1.0 + 0.02 * jax.random.normal(ks[10], (DEPTH_2, D_MODEL), jnp.float32)
    ln_b = 0.02 * jax.random.normal(ks[11], (DEPTH_2, D_MODEL), jnp.float32)
    return {"x": x, "mla_w_in": mla_w_in, "mla_q_norm": mla_q_norm, "mla_kv_norm": mla_kv_norm,
            "mla_w_uq": mla_w_uq, "mla_w_ukv": mla_w_ukv, "mla_w_o": mla_w_o,
            "moba_w_kv": moba_w_kv, "moba_w_in": moba_w_in, "moba_w_o": moba_w_o,
            "ln_g": ln_g, "ln_b": ln_b}

def second_block(x, mla_w_in, mla_q_norm, mla_kv_norm, mla_w_uq, mla_w_ukv, mla_w_o,
              moba_w_kv, moba_w_in, moba_w_o, ln_g, ln_b):
    S = x.shape[1]
    cos_a, sin_a = rope_tables(S, ROPE_A)
    cos_b, sin_b = rope_tables(S, HD_B)
    shared = None
    for layer in range(DEPTH_2):
        if layer < N_A:
            y = mla_mixer(x, mla_w_in[layer], mla_q_norm[layer], mla_kv_norm[layer],
                          mla_w_uq[layer], mla_w_ukv[layer], mla_w_o[layer], cos_a, sin_a)
        else:
            if shared is None:
                shared = moba_shared_kv(x, moba_w_kv, cos_b, sin_b)
            j = layer - N_A
            y = moba_mixer(x, shared[0], shared[1], shared[2], moba_w_in[j], moba_w_o[j], cos_b, sin_b)
        x = layer_norm(ALPHA * x + y, ln_g[layer], ln_b[layer])
    return x


def setup_inputs(seed=0):
    out = dict(first_inputs(seed))
    for name, value in second_inputs(seed + 1).items():
        if name != "x":
            out[name + "_2"] = value
    return out


def reference(
    x, c, ada_w, ada_b, norm_mix_g, norm_ffn_g, final_g, conv_w_in, conv_b_in, conv_w_dw,
    conv_b_dw, conv_ln_g, conv_ln_b, conv_w_out, hgrn_w_in, hgrn_lb_logits, hgrn_norm_g,
    hgrn_w_out, pool_w, pool_b, pool_scale, sb_w_qkv, sb_w_out, moe_w_rg, moe_b_rg, moe_w_re,
    moe_b_re, moe_w_gate, moe_w_up, moe_w_down, mla_w_in_2, mla_q_norm_2, mla_kv_norm_2,
    mla_w_uq_2, mla_w_ukv_2, mla_w_o_2, moba_w_kv_2, moba_w_in_2, moba_w_o_2, ln_g_2, ln_b_2,
):
    x = first_block(
        x, c, ada_w, ada_b, norm_mix_g, norm_ffn_g, final_g, conv_w_in, conv_b_in, conv_w_dw,
        conv_b_dw, conv_ln_g, conv_ln_b, conv_w_out, hgrn_w_in, hgrn_lb_logits, hgrn_norm_g,
        hgrn_w_out, pool_w, pool_b, pool_scale, sb_w_qkv, sb_w_out, moe_w_rg, moe_b_rg,
        moe_w_re, moe_b_re, moe_w_gate, moe_w_up, moe_w_down,
    )
    return second_block(
        x, mla_w_in_2, mla_q_norm_2, mla_kv_norm_2, mla_w_uq_2, mla_w_ukv_2, mla_w_o_2,
        moba_w_kv_2, moba_w_in_2, moba_w_o_2, ln_g_2, ln_b_2,
    )


_drawn_inputs = setup_inputs


def setup_inputs(seed=0):
    import zlib

    import numpy as np

    out = dict(_drawn_inputs(seed))
    spreads = {}
    factors = {'ada_b': 3.007,
     'norm_mix_g': 5.403,
     'conv_b_in': 8.0,
     'conv_b_dw': 7.356,
     'conv_ln_g': 4.909,
     'conv_ln_b': 6.692,
     'moe_b_rg': 8.0,
     'moe_b_re': 8.0,
     'mla_q_norm_2': 8.0,
     'mla_kv_norm_2': 8.0}
    for name, (base, spread) in spreads.items():
        noise = np.random.default_rng([zlib.crc32(name.encode()), seed]).standard_normal(out[name].shape)
        drawn = base * np.exp(spread * noise) if base else spread * noise
        out[name] = __import__('jax').numpy.asarray(drawn.astype(out[name].dtype))
    for name, factor in factors.items():
        out[name] = (out[name] * factor).astype(out[name].dtype)
    return out
```

```python
from contextlib import ExitStack

import numpy as np
import concourse.bass as bass
from concourse import mybir

ALU = mybir.AluOpType
ACT = mybir.ActivationFunctionType
F32 = mybir.dt.float32
I32 = mybir.dt.int32
AX = mybir.AxisListType

P = 128
T = 256
NT = T // P
D = 1024
KD = D // P
TAPS = 31
EXPERTS = 32
GROUPS = 4
PER_GROUP = EXPERTS // GROUPS
HIDDEN = 512
KF = HIDDEN // P
SLOTS_A = 2 * T
WIN = 64
PADDED = SLOTS_A + WIN
NOWHERE = SLOTS_A
BIG = 1e30
EPS = 1e-6
LN_EPS = 1e-5
ALPHA = 4 ** 0.25

HEADS = 16
NOPE, ROPE = 64, 32
QK = NOPE + ROPE
HD = 64
KQ = 768 // P
KKV = 256 // P
SCALE_A = QK ** -0.5
SCALE_B = HD ** -0.5

SLOT = 4096
RING = 9
RING_C = 7
BODY = 3
LOOPS = EXPERTS // BODY
PEELED = EXPERTS - LOOPS * BODY
PE_TAPS = 13
DIAGS = 8

C_IDENT, C_ONES = 0, P
R_STRICT, R_IOTA, R_IOTA32 = 0, P, P + SLOTS_A
R_COLS = P + SLOTS_A + EXPERTS
A_MASK, A_COS, A_SIN = 0, T, 2 * T
A_COLS = 3 * T
B_COS, B_SIN, B_ROT = 0, T, 2 * T
B_COLS = 2 * T + P

LOT0 = [("ada_b", 48), ("conv_b_in", 16), ("norm_mix_g", 8), ("norm_ffn_g", 8), ("final_g", 8),
        ("conv_b_dw", 8), ("conv_ln_g", 8), ("conv_ln_b", 8), ("c", 8)]
LOT1 = [("mla_q_norm_2", 6), ("mla_kv_norm_2", 2), ("ln_g_2", 16), ("ln_b_2", 16)]
COL = {}
_at = 0
for _name, _n in LOT0 + LOT1:
    COL[_name] = _at
    _at += _n
LOT0_ROWS = sum(n for _, n in LOT0)
LOT1_ROWS = sum(n for _, n in LOT1)
COL["dw"] = _at
PAR = _at + TAPS * KD
DW_ROWS = TAPS * KD // 2


def two_blocks(nc, A, out):
    with ExitStack() as ctx:
        def sb(name, shape, dt=F32):
            return ctx.enter_context(nc.sbuf_tensor(name, shape, dt))

        sems = {}

        def sem(name):
            if name not in sems:
                sems[name] = ctx.enter_context(nc.semaphore(name))
            return sems[name]

        R0 = RING * SLOT
        R = R0 + KD * T
        arena = sb("arena", [P, R + 13312])
        consts = sb("consts", [P, 2 * P])
        par = sb("par", [P, PAR])
        mod = sb("mod", [P, 48])
        der = sb("der", [P, 40])
        brow = sb("brow", [1, GROUPS + EXPERTS])
        table = sb("table", [1, 4 * EXPERTS + 4], I32)
        ps = [ctx.enter_context(nc.psum_tensor(f"bank{i}", [P, 512], F32)) for i in range(8)]

        def area(off, k, n):
            return arena[:, off:off + k * n].rearrange("p (k n) -> p k n", k=k)

        ident = consts[:, C_IDENT:C_IDENT + P]
        ones = consts[:, C_ONES:C_ONES + P]

        def col(name, j=0):
            return par[:, COL[name] + j:COL[name] + j + 1]

        cact = der[:, 0:8]
        a1, a2 = der[:, 8:16], der[:, 16:24]
        eps6, eps5 = der[:, 24:25], der[:, 25:26]

        xT = area(R0, KD, T)
        x_tok = area(R, NT, D)
        sq = area(R + 2048, KD, T)
        h = area(R + 4096, KD, T)
        u = area(R + 6144, KD, TAPS - 1 + T)
        y = area(R + 8432, KD, T)
        sg = area(R + 10480, 4, T)
        diag = area(R + 11504, DIAGS, P)
        rows = area(R + 12528, 4, P)
        std = arena[:, R + 6144:R + 6144 + T]
        scaled = x_tok.rearrange("p a b -> p (a b)").rearrange("p (k n) -> p k n", k=KD)
        h2 = area(R + 4608, KD, T)
        h2_tok = area(R + 6656, NT, D)
        small = arena[:, R + 9216:R + 10240]
        sel = area(R + 10240, NT, SLOTS_A)
        selw = area(R + 11264, NT, SLOTS_A)
        rc = arena[:, R + 12640:R + 12640 + R_COLS]
        wr = arena[:, R + 8704:R + 8704 + KD * 36].rearrange("p (k n) -> p k n", k=KD)
        xg = area(R, KD, PADDED)
        yT = area(R + 4608, KD, PADDED)
        comb = area(R + 9216, SLOTS_A // P, T)
        xw = [area(R + 10240 + b * KD * WIN, KD, WIN) for b in range(BODY)]
        silu_g = area(R + 11776, KF, WIN)
        hid = area(R + 12544, KF, WIN)
        y_tok = area(R, SLOTS_A // P, D)
        qh = area(RING_C * SLOT, HEADS, T)
        kh = area((RING_C + 1) * SLOT, HEADS, T)
        cq = area(R, KQ + KKV, T)
        gate = area(R + 2048, KD, T)
        v = area(R + 4096, NT, D)
        o = area(R + 6144, KD, T)
        sq2 = o
        raw = area(R + 6144, 4, 2 * T)
        prob = area(R + 8192, 4, 3 * P)
        prob_t = area(R + 9728, 4, 3 * P)
        ac = arena[:, R + 11264:R + 11264 + A_COLS]
        std2 = arena[:, R + 12032:R + 12288]
        smin = area(R + 12288, 4, 2)
        ssum = area(R + 12296, 4, 2)
        srec = area(R + 12304, 4, 2)
        wrope = area(R + 12352, KD, ROPE)
        qb = area(RING_C * SLOT, KD, T)
        kb = area(RING_C * SLOT + 2048, KD, T)
        raw_b = area((RING_C + 1) * SLOT, KD, T)
        turned = area((RING_C + 1) * SLOT + 2048, KD, T)
        bc = arena[:, R:R + B_COLS]
        out_tok = area(R, NT, D)
        final = area(R + 6144, KD, T)

        def slot(s, k=KD, n=512):
            return arena[:, s * SLOT:s * SLOT + k * n].rearrange("p (k n) -> p k n", k=k)

        use, fills, reads = {}, [0] * 8, [0] * 8

        def plan(name, b, readers=1, counted=1):
            use[name] = (b, fills[b], reads[b], reads[b] + readers)
            fills[b] += counted
            reads[b] += readers

        for j in range(KD):
            plan(("x", j), j % 4)
        plan("par", 4)
        plan("ms1", 7)
        plan("mod_a", 6)
        for j in range(KD):
            plan(("glu_a", j), 2 * (j % 2))
            plan(("glu_g", j), 2 * (j % 2) + 1)
        plan("mod_b", 6)
        for j in range(KD):
            plan(("conv", j), [4, 5, 0, 1][j % 4], counted=0)
        plan("mean1", 2, readers=0)
        plan("var1", 7)
        for j in range(KD):
            plan(("proj1", j), j % 4)
        plan("ms2", 7)
        plan("logit", 5)
        for t in range(NT):
            for half in range(2):
                plan(("h2tok", t, half), 2 * t + half)
        plan("rank", 4, 1)
        for j in range(KD):
            plan(("gather", j), j % 4)
        for n in range(2):
            plan(("comb", n), 4 + n)
        BEFORE_EXPERTS = list(reads)
        for s in range(4):
            for half in range(2):
                plan(("ytok", s, half), (2 * s + half) % 4)
        for j in range(KD):
            plan(("moe", j), 4 + j % 3)
        plan("ms3", 7)
        for j in range(KQ + KKV):
            plan(("cq", j), j % 4)
        plan("msq", 7)
        plan("mskv", 6)
        plan("krope", 4)
        for j in range(KD):
            plan(("gate1", j), j % 4)
        for t in range(NT):
            for n in range(2):
                plan(("v1", t, n), 2 * t + n)
        for p in range(HEADS // 2):
            plan(("kn", p), p % 4)
        for p in range(HEADS // 2):
            plan(("q", p), p % 4)
        for layer in (0, 1):
            if layer:
                for n in range(2):
                    for j in range(KD):
                        plan(("raw", n, j), j % 4)
                        if j:
                            plan(("rot", n, j - 1), 4 + (j - 1) % 2)
                    plan(("rot", n, KD - 1), 4 + (KD - 1) % 2)
                    for w in range(KD if n else 4):
                        plan(("gate2", w) if n else ("v2", w // 2, w % 2), w % 4)
            for i in range(HEADS + 3):
                if i < HEADS:
                    plan(("s", layer, i), i % 2)
                if 0 <= i - 2 < HEADS:
                    plan(("pt", layer, i - 2), 2 + i % 2)
                if 0 <= i - 3 and (i - 3) % 2 == 0:
                    plan(("o", layer, (i - 3) // 2), 4 + (i - 3) // 2 % 2)
            for j in range(KD):
                plan(("proj2", layer, j), j % 4)
            plan(("mean2", layer), 6, readers=0)
            plan(("var2", layer), 7)
        for t in range(NT):
            for half in range(2):
                plan(("out", t, half), 2 * t + half)

        def may_fill(pe, name):
            b, _, before, _ = use[name]
            if before:
                pe.wait_ge(sem(f"bank{b}_read"), before)
            return ps[b]

        def filled(eng, name):
            b, n, _, _ = use[name]
            eng.wait_ge(sem(f"bank{b}_full"), n + 1)
            return ps[b]

        def full(name):
            return sem(f"bank{use[name][0]}_full")

        def read(name):
            return sem(f"bank{use[name][0]}_read")

        def moved(eng, name):
            b, _, _, after = use[name]
            eng.wait_ge(sem(f"bank{b}_read"), after)

        def cols(w, lo, n, k=KD):
            return w[:, lo:lo + n].rearrange("(k p) n -> p k n", p=P)

        chunks = []

        def chunk(name, s, parts, last):
            chunks.append((name, s, parts, last))

        aw = A["ada_w"][0]
        win = A["conv_w_in"][0]
        order = [("ada", i) for i in range(4)] + [("glu", i) for i in range(4)] \
            + [("ada", i) for i in range(4, 12)] + [("proj1", 0), ("proj1", 1)]
        for i, (kind, n) in enumerate(order):
            s = i % RING
            if kind == "ada":
                chunk((kind, n), s, [(slot(s), cols(aw, 512 * n, 512))], "mod_a" if n < 4 else "mod_b")
            elif kind == "glu":
                w = arena[:, s * SLOT:(s + 1) * SLOT].rearrange("p (k n) -> p k n", k=KD)
                chunk((kind, n), s, [(w[:, :, 0:256], cols(win, 256 * n, 256)),
                                     (w[:, :, 256:512], cols(win, D + 256 * n, 256))], ("glu_g", 2 * n + 1))
            else:
                chunk((kind, n), s, [(slot(s), cols(A["conv_w_out"][0], 512 * n, 512))], ("proj1", 4 * n + 3))
        CHUNKS_A = len(chunks)
        assert CHUNKS_A % RING == 0

        def next_c():
            return (RING_C - 1 + len(chunks) - CHUNKS_A) % RING_C

        mw = A["mla_w_in_2"][0]
        for n in range(2):
            s = next_c()
            chunk(("cq", n), s, [(slot(s), cols(mw, 512 * n, 512))], ("cq", 4 * n + 3))
        for n in range(2):
            s = next_c()
            chunk(("gate1", n), s, [(slot(s), cols(mw, D + ROPE + 512 * n, 512))], ("gate1", 4 * n + 3))
        s = next_c()
        chunk("ukv", s, [(slot(s, KKV, 2048), cols(A["mla_w_ukv_2"][0], 0, 2048))], ("kn", HEADS // 2 - 1))
        for n in range(4):
            s = next_c()
            chunk(("uq", n), s, [(slot(s, KQ, 384), cols(A["mla_w_uq_2"][0], 384 * n, 384))], ("q", 2 * n + 1))
        for n in range(2):
            s = next_c()
            chunk(("wo", 0, n), s, [(slot(s), cols(A["mla_w_o_2"][0], 512 * n, 512))], ("proj2", 0, 4 * n + 3))
        for kind, w in (("kv", A["moba_w_kv_2"]), ("in", A["moba_w_in_2"][0])):
            for n in range(4):
                s = next_c()
                if n < 2:
                    last = ("raw", int(kind == "in"), 4 * n + 3)
                else:
                    last = ("v2", 1, n - 2) if kind == "kv" else ("gate2", 4 * n - 5)
                chunk((kind, n), s, [(slot(s), cols(w, 512 * n, 512))], last)
        for n in range(2):
            s = next_c()
            chunk(("wo", 1, n), s, [(slot(s), cols(A["moba_w_o_2"][0], 512 * n, 512))], ("proj2", 1, 4 * n + 3))

        landed, place, count = {}, {}, [0] * RING
        for i, (name, s, parts, _) in enumerate(chunks):
            if i == CHUNKS_A:
                EXPERT_BASE = list(count)
                for e in range(EXPERTS):
                    for m in range(3):
                        count[3 * (e % BODY) + m] += 16
            count[s] += 16 * len(parts)
            landed[name], place[name] = count[s], s

        def arrived(eng, name):
            eng.wait_ge(sem(f"slot{place[name]}"), landed[name])
            return place[name]

        gate_full, up_full, y_full = sem("gate_full"), sem("up_full"), sem("down_full")
        silu_done, hid_ready = sem("silu_done"), sem("hidden_ready")
        y_moved, win_ready = sem("expert_moved"), sem("window_ready")
        G_BANK, U_BANK, Y_BANK = ps[0], ps[1], ps[2]
        C_UP, C_MOVED = BODY, 1

        expert_w = [A["moe_w_gate"][0], A["moe_w_up"][0], A["moe_w_down"][0]]

        def overflow(eng):
            eng.wait_ge(sem("table_ready"), 1)
            most = eng.value_load(table[0:1, EXPERTS:EXPERTS + 1], min_val=0, max_val=T)
            return most > WIN

        S_P1, S_P2, S_W1, S_W2 = 1000, 1002, 1004, 1006

        block = ctx.enter_context(nc.Block())

        @block.sync
        def _(sp):
            sp.dma_start(x_tok, A["x"][0].rearrange("(t p) n -> p t n", p=P)).then_inc(sem("x_in"), 16)

            def load(i):
                _, s, parts, _ = chunks[i]
                for dst, src in parts:
                    sp.dma_start(dst, src).then_inc(sem(f"slot{s}"), 16)

            for i in range(CHUNKS_A):
                if i >= RING:
                    filled(sp, chunks[i - RING][3])
                load(i)

            def load_matrix(e, b, m):
                s = 3 * b + m
                dst = slot(s) if m < 2 else slot(s, KF, D)
                src = expert_w[m][bass.ds(e, 1)].rearrange("e (k p) n -> p (e k) n", p=P)
                sp.dma_start(dst, src).then_inc(sem(f"slot{s}"), 16)

            for e in range(BODY):
                for m in range(3):
                    filled(sp, chunks[CHUNKS_A - RING + 3 * e + m][3])
                    load_matrix(e, e, m)
            with sp.Fori(0, LOOPS - 1) as it:
                for b in range(BODY):
                    sp.wait_ge(gate_full, it * BODY + (b + 1))
                    load_matrix(it * BODY + (BODY + b), b, 0)
                    sp.wait_ge(up_full, it * BODY + (C_UP + b + 1))
                    load_matrix(it * BODY + (BODY + b), b, 1)
                    sp.wait_ge(y_full, it * BODY + (b + 1))
                    load_matrix(it * BODY + (BODY + b), b, 2)
            for b in range(PEELED):
                e = LOOPS * BODY + b
                sp.wait_ge(gate_full, e - BODY + 1)
                load_matrix(e, b, 0)
                sp.wait_ge(up_full, C_UP + e - BODY + 1)
                load_matrix(e, b, 1)
                sp.wait_ge(y_full, e - BODY + 1)
                load_matrix(e, b, 2)
            with sp.If(overflow(sp)):
                sp.wait_ge(y_full, EXPERTS)
                with sp.Fori(0, EXPERTS) as e:
                    sp.wait_ge(sem("over_moved"), e * 3 + 1)
                    for m in range(3):
                        dst = slot(m) if m < 2 else slot(m, KF, D)
                        sp.dma_start(dst, expert_w[m][bass.ds(e, 1)].rearrange("e (k p) n -> p (e k) n", p=P)) \
                            .then_inc(sem("over_in"), 16)
                sp.wait_ge(sem("over_moved"), 3 * EXPERTS + 1)
            for i in range(CHUNKS_A, len(chunks)):
                n = i - CHUNKS_A
                s = chunks[i][1]
                if n >= RING_C:
                    filled(sp, chunks[i - RING_C][3])
                elif s == RING_C - 1:
                    sp.wait_ge(gate_full, LOOPS * BODY)
                elif s < 3 * PEELED:
                    e = LOOPS * BODY + s // 3
                    used = ((gate_full, 0), (up_full, C_UP), (y_full, 0))[s % 3]
                    sp.wait_ge(used[0], used[1] + e + 1)
                load(i)
            for t in range(NT):
                sp.wait_ge(sem(f"out_ready{t}"), 2)
                sp.dma_start(out[0, t * P:(t + 1) * P, :], out_tok[:, t, :]).then_inc(sem("out_done"), 16)
            sp.wait_ge(sem("out_done"), 16 * NT)

        @block.gpsimd
        def _(pool):
            pool.wait_ge(sem("consts_in"), 16)
            moved(pool, "par")
            made = 0
            for j in range(KD):
                for w in range(PE_TAPS):
                    if made >= DIAGS:
                        pool.wait_ge(sem("diag_used"), made - DIAGS + 1)
                    pool.tensor_scalar(diag[:, made % DIAGS, :], ident, col("dw", w * KD + j), 0.0,
                                       ALU.mult, ALU.add).then_inc(sem("diag_ready"), 1)
                    made += 1

            pool.wait_ge(sem("slots_known"), 1)
            iota = rc[:, R_IOTA:R_IOTA + SLOTS_A]
            for t in range(NT):
                other = h2[:, 0:2, :].rearrange("p k n -> p (k n)")
                if t == 0:
                    moved(pool, ("h2tok", 1, 1))
                    filled(pool, "logit")
                if t:
                    pool.wait_ge(sem("selw_ready"), t)
                pool.tensor_scalar(selw[:, t, :], iota, small[:, S_P1 + t:S_P1 + t + 1],
                                   small[:, S_W1 + t:S_W1 + t + 1], ALU.is_equal, ALU.mult) \
                    .then_inc(sem("selw_part"), 1)
                pool.tensor_scalar(other, iota, small[:, S_P2 + t:S_P2 + t + 1],
                                   small[:, S_W2 + t:S_W2 + t + 1], ALU.is_equal, ALU.mult) \
                    .then_inc(sem("selw_part"), 1)
                pool.wait_ge(sem("selw_part"), 2 * (t + 1))
                pool.tensor_tensor(selw[:, t, :], selw[:, t, :], other, ALU.add).then_inc(sem("selw_ready"), 1)
            pool.memset(xg[:, :, SLOTS_A:PADDED], 0.0).then_inc(sem("pad_ready"), 1)
            pool.wait_ge(sem("pad_ready"), 1)
            pool.wait_ge(sem("table_ready"), 1)
            for j in range(KD):
                moved(pool, ("gather", j))
            moved(pool, ("comb", 1))

            def window(e, b):
                at = pool.value_load(table[0:1, bass.ds(e, 1)], min_val=0, max_val=SLOTS_A)
                pool.tensor_copy(xw[b], xg[:, :, bass.ds(at, WIN)]).then_inc(win_ready, 1)

            with pool.Fori(0, LOOPS) as it:
                for b in range(BODY):
                    pool.wait_ge(up_full, it * BODY + (b + 1))
                    window(it * BODY + b, b)
            for b in range(PEELED):
                pool.wait_ge(up_full, LOOPS * BODY + b + 1)
                window(LOOPS * BODY + b, b)
            with pool.If(overflow(pool)):
                pool.wait_ge(up_full, C_UP + EXPERTS)
                with pool.Fori(0, EXPERTS) as e:
                    for r in range(3):
                        pool.wait_ge(sem("over_moved"), e * 3 + (r + 1))
                        at = pool.value_load(table[0:1, bass.ds(e + (EXPERTS + 4 + EXPERTS * r), 1)],
                                             min_val=0, max_val=SLOTS_A)
                        pool.tensor_copy(xw[0], xg[:, :, bass.ds(at, WIN)]).then_inc(sem("over_window"), 1)

            pool.wait_ge(sem("krope_ready"), 1)
            src = raw[NOPE:QK, 3, 0:T].unsqueeze(1).broadcast_to((ROPE, HEADS, T))
            pool.tensor_copy(kh[NOPE:QK, :, :], src).then_inc(sem("krope_spread"), 1)
            cosA = ac[NOPE:QK, A_COS:A_COS + T].unsqueeze(1).broadcast_to((ROPE, 2, T))
            for p in range(HEADS // 2):
                pool.wait_ge(sem("q_shuffled"), p + 1)
                pool.tensor_tensor(qh[NOPE:QK, 2 * p:2 * p + 2, :], qh[NOPE:QK, 2 * p:2 * p + 2, :], cosA,
                                   ALU.mult).then_inc(sem("q_cos"), 1)

            def scale_probs(n):
                pool.wait_ge(sem("sum_inverse"), n + 1)
                b = n % 4
                pool.tensor_scalar(prob[:, b, 0:P], prob[:, b, 0:P], srec[:, b, 0:1], 0.0, ALU.mult, ALU.add)
                pool.tensor_scalar(prob[:, b, P:3 * P], prob[:, b, P:3 * P], srec[:, b, 1:2], 0.0,
                                   ALU.mult, ALU.add).then_inc(sem("probs_ready"), 1)

            for i in range(HEADS):
                scale_probs(i)
            for n in range(2):
                for j in range(KD):
                    moved(pool, ("raw", n, j))
                    filled(pool, ("rot", n, j))
                    pool.tensor_tensor(raw_b[:, j, :], raw_b[:, j, :], bc[:, B_COS:B_COS + T], ALU.mult) \
                        .then_inc(sem("raw_cos"), 1)
            for i in range(HEADS):
                scale_probs(HEADS + i)

        @block.scalar
        def _(act):
            def rows_of(name):
                a = A[name]
                n = len(a.shape)
                flat = a if n == 1 else a.rearrange("a b -> (a b)")
                return flat.rearrange("(r n) -> r n", n=P)

            act.dma_start(consts[:, :], A["k_base"]).then_inc(sem("consts_in"), 16)
            for lot, names in ((0, LOT0), (1, LOT1)):
                at = 0
                for name, n in names:
                    act.dma_start(rows[at:at + n, lot, :], rows_of(name)).then_inc(sem("rows_in"), 16)
                    at += n
            dwr = A["conv_w_dw"][0].rearrange("w (k n) -> (w k) n", n=P)
            for half in range(2):
                act.dma_start(rows[0:DW_ROWS, 2 + half, :], dwr[half * DW_ROWS:(half + 1) * DW_ROWS, :]) \
                    .then_inc(sem("rows_in"), 16)
            act.dma_start(brow[:, 0:GROUPS], A["moe_b_rg"]).then_inc(sem("router_in"), 16)
            act.dma_start(brow[:, GROUPS:GROUPS + EXPERTS], A["moe_b_re"]).then_inc(sem("router_in"), 16)

            def norm_std(name, n, eps):
                bank = filled(act, name)
                to = std if name in ("ms1", "var1", "ms2") else std2
                act.activation(to, bank[:, 0:T], ACT.Sqrt, bias=eps, scale=1.0 / n).then_inc(read(name), 1)

            for j in range(KD):
                moved(act, ("x", j))
                act.activation(sq[:, j, :], xT[:, j, :], ACT.Square).then_inc(sem("squared0"), 1)
            moved(act, "par")
            act.activation(cact, par[:, COL["c"]:COL["c"] + 8], ACT.Silu).then_inc(sem("c_ready"), 1)
            act.wait_ge(sem("eps_ready"), 2)
            norm_std("ms1", D, eps6)
            moved(act, "mod_a")
            for j in range(KD):
                act.wait_ge(sem("h_scaled"), j + 1)
                act.activation(h[:, j, :], h[:, j, :], ACT.Identity, bias=mod[:, j:j + 1]) \
                    .then_inc(sem("h_ready"), 1)
            for j in range(KD):
                bank = filled(act, ("glu_g", j))
                if j >= 4:
                    moved(act, ("glu_a", j - 4))
                act.activation(sg[:, j % 4, :], bank[:, 0:T], ACT.Sigmoid, bias=col("conv_b_in", KD + j)) \
                    .then_inc(read(("glu_g", j)), 1)
            for j in range(KD):
                act.wait_ge(sem("conv_done"), j + 1)
                bank = ps[use[("conv", j)][0]]
                act.activation(y[:, j, :], bank[:, 0:T], ACT.Identity, bias=col("conv_b_dw", j)) \
                    .then_inc(read(("conv", j)), 1)
            for j in range(KD):
                act.wait_ge(sem("centred1"), j + 1)
                act.activation(sq[:, j, :], y[:, j, :], ACT.Square).then_inc(sem("squared1"), 1)
            norm_std("var1", D, eps6)
            for j in range(KD):
                act.wait_ge(sem("normed1"), j + 1)
                act.activation(h[:, j, :], y[:, j, :], ACT.Silu, bias=col("conv_ln_b", j)) \
                    .then_inc(sem("act_ready"), 1)
            for j in range(KD):
                moved(act, ("proj1", j))
                act.activation(sq[:, j, :], xT[:, j, :], ACT.Square).then_inc(sem("squared2"), 1)
                if j == 0:
                    act.dma_start(rc, A["k_route"]).then_inc(sem("route_in"), 16)
                    act.dma_start(wr[:, :, 0:GROUPS], cols(A["moe_w_rg"][0], 0, GROUPS)) \
                        .then_inc(sem("router_in"), 16)
                    act.dma_start(wr[:, :, GROUPS:36], cols(A["moe_w_re"][0], 0, EXPERTS)) \
                        .then_inc(sem("router_in"), 16)
            norm_std("ms2", D, eps6)
            for j in range(KD):
                act.wait_ge(sem("h2_scaled"), j + 1)
                act.activation(h2[:, j, :], scaled[:, j, :], ACT.Identity, bias=mod[:, 24 + j:25 + j]) \
                    .then_inc(sem("h2_ready"), 1)
            for t in range(NT):
                for half in range(2):
                    name = ("h2tok", t, half)
                    bank = filled(act, name)
                    act.activation(h2_tok[:, t, half * 512:(half + 1) * 512], bank[:, :], ACT.Copy) \
                        .then_inc(read(name), 1)
            act.wait_ge(sem("group_shifted"), 1)
            act.activation(small[:, 80:88], small[:, 80:88], ACT.Exp).then_inc(sem("group_exp"), 1)
            act.wait_ge(sem("pair_shifted"), 1)
            act.activation(small[:, 88:90], small[:, 88:90], ACT.Exp).then_inc(sem("pair_exp"), 1)
            for j in range(0, KD, 2):
                bank = filled(act, ("gather", j))
                act.activation(xg[:, j, 0:SLOTS_A], bank[:, :], ACT.Copy).then_inc(read(("gather", j)), 1)

            def silu(full_sem, n, done):
                act.wait_ge(full_sem, n)
                act.activation(silu_g.rearrange("p k n -> p (k n)"), G_BANK[:, 0:KF * WIN], ACT.Silu) \
                    .then_inc(done, 1)

            with act.Fori(0, EXPERTS) as e:
                silu(gate_full, e + 1, silu_done)
            with act.If(overflow(act)):
                with act.Fori(0, 3 * EXPERTS) as n:
                    silu(sem("over_gate"), n + 1, sem("over_silu"))

            act.wait_ge(hid_ready, EXPERTS)
            act.wait_ge(y_full, EXPERTS)
            act.wait_ge(sem("over_end"), 1)
            act.dma_start(ac, A["k_mla"]).then_inc(sem("mla_in"), 16)
            act.dma_start(wrope, cols(mw, D, ROPE)).then_inc(sem("wrope_in"), 16)
            for s in range(4):
                name = ("ytok", s, 0)
                bank = filled(act, name)
                act.activation(y_tok[:, s, 0:512], bank[:, :], ACT.Copy).then_inc(read(name), 1)
            for j in range(KD):
                moved(act, ("moe", j))
                if j == 0:
                    filled(act, ("ytok", 3, 1))
                act.activation(sq2[:, j, :], xT[:, j, :], ACT.Square).then_inc(sem("squared3"), 1)
            norm_std("ms3", D, eps6)
            for j in range(KQ + KKV):
                moved(act, ("cq", j))
                act.activation(sq2[:, j, :], cq[:, j, :], ACT.Square).then_inc(sem("squared5"), 1)
            norm_std("msq", KQ * P, eps6)
            act.wait_ge(sem("rstd_ready"), 5)
            norm_std("mskv", KKV * P, eps6)
            bank = filled(act, "krope")
            act.activation(raw[NOPE:QK, 3, 0:T], bank[NOPE:QK, 0:T], ACT.Copy).then_inc(read("krope"), 1)
            for j in range(KD):
                name = ("gate1", j)
                bank = filled(act, name)
                act.activation(gate[:, j, :], bank[:, 0:T], ACT.Silu).then_inc(read(name), 1)
            for t in range(NT):
                name = ("v1", t, 0)
                bank = filled(act, name)
                act.activation(v[:, t, 0:512], bank[:, :], ACT.Copy).then_inc(read(name), 1)
            for p in range(HEADS // 2):
                if p % 2:
                    continue
                name = ("kn", p)
                bank = filled(act, name)
                act.activation(kh[0:NOPE, 2 * p:2 * p + 2, :], bank[0:NOPE, :].rearrange("p (h n) -> p h n", h=2),
                               ACT.Copy).then_inc(read(name), 1)
            for p in range(HEADS // 2):
                name = ("q", p)
                bank = filled(act, name)
                act.activation(qh[0:QK, 2 * p:2 * p + 2, :], bank[0:QK, :].rearrange("p (h n) -> p h n", h=2),
                               ACT.Copy).then_inc(read(name), 1)

            def attention(layer):
                for i in range(HEADS + 2):
                    if i < HEADS:
                        b = i % 4
                        moved(act, ("s", layer, i))
                        act.activation(prob[:, b, 0:P], prob[:, b, 0:P], ACT.Exp, bias=smin[:, b, 0:1],
                                       scale=-1.0, accum_out=ssum[:, b, 0:1]).then_inc(sem("exp_done"), 1)
                        act.activation(prob[:, b, P:3 * P], prob[:, b, P:3 * P], ACT.Exp, bias=smin[:, b, 1:2],
                                       scale=-1.0, accum_out=ssum[:, b, 1:2]).then_inc(sem("exp_done"), 1)
                    if i >= 2:
                        n = i - 2
                        name = ("pt", layer, n)
                        bank = filled(act, name)
                        if n >= 4:
                            filled(act, ("o", layer, (n - 4) // 2))
                        act.activation(prob_t[:, n % 4, :], bank[:, 0:3 * P], ACT.Copy).then_inc(read(name), 1)

            def out_norm(layer):
                for j in range(KD):
                    act.wait_ge(sem("centred2"), KD * layer + j + 1)
                    act.activation(sq2[:, j, :], xT[:, j, :], ACT.Square).then_inc(sem("squared4"), 1)
                norm_std(("var2", layer), D, eps5)
                for j in range(KD):
                    act.wait_ge(sem("normed2"), KD * layer + j + 1)
                    to = final if layer else xT
                    act.activation(to[:, j, :], xT[:, j, :], ACT.Identity, bias=col("ln_b_2", KD * layer + j)) \
                        .then_inc(sem("layer_ready"), 1)

            attention(0)
            out_norm(0)
            act.dma_start(bc, A["k_moba"]).then_inc(sem("moba_in"), 16)
            for n in range(2):
                for j in range(KD):
                    name = ("raw", n, j)
                    bank = filled(act, name)
                    if n:
                        act.wait_ge(sem("turned"), j + 1)
                    act.activation(raw_b[:, j, :], bank[:, 0:T], ACT.Copy).then_inc(read(name), 1)
                for w in range(KD if n else 4):
                    name = ("gate2", w) if n else ("v2", w // 2, w % 2)
                    bank = filled(act, name)
                    if n:
                        act.activation(gate[:, w, :], bank[:, 0:T], ACT.Silu).then_inc(read(name), 1)
                    else:
                        act.activation(v[:, w // 2, (w % 2) * 512:(w % 2 + 1) * 512], bank[:, :], ACT.Copy) \
                            .then_inc(read(name), 1)
            attention(1)
            out_norm(1)
            for t in range(NT):
                name = ("out", t, 1)
                bank = filled(act, name)
                act.activation(out_tok[:, t, 512:D], bank[:, :], ACT.Copy).then_inc(sem(f"out_ready{t}"), 1)

        @block.tensor
        def _(pe):
            pe.sem_inc(up_full, C_UP)
            pe.wait_ge(sem("consts_in"), 16)
            pe.wait_ge(sem("x_in"), 16)
            for j in range(KD):
                bank = may_fill(pe, ("x", j))
                for t in range(NT):
                    mm = pe.transpose(bank[:, t * P:(t + 1) * P], x_tok[:, t, j * P:(j + 1) * P], ident)
                mm.then_inc(full(("x", j)), 1)
            pe.wait_ge(sem("rows_in"), 16 * (len(LOT0) + len(LOT1) + 2))
            bank = may_fill(pe, "par")
            for lot, n, at in ((0, LOT0_ROWS, 0), (1, LOT1_ROWS, LOT0_ROWS), (2, DW_ROWS, COL["dw"]),
                               (3, DW_ROWS, COL["dw"] + DW_ROWS)):
                mm = pe.transpose(bank[:, at:at + n], rows[0:n, lot, :], ident[0:n, 0:n])
            mm.then_inc(full("par"), 1)

            def total(name, src, tiles, ready):
                bank = may_fill(pe, name)
                for k in range(tiles):
                    ready(k)
                    mm = pe.matmul(bank[:, 0:T], ones, src[:, k, :], start=(k == 0), stop=(k == tiles - 1))
                mm.then_inc(full(name), 1)

            def project(name, w, lo, m, rhs, k0=0, n=T, at=0, part=0, tiles=KD, done=True, ready=None):
                bank = ps[use[name][0]]
                for k in range(tiles):
                    if ready:
                        ready(k)
                    mm = pe.matmul(bank[part:part + m, at:at + n], w[:, k, lo:lo + m], rhs[:, k0 + k, :],
                                   start=(k == 0), stop=(k == tiles - 1))
                if done:
                    mm.then_inc(full(name), 1)

            total("ms1", sq, KD, lambda k: pe.wait_ge(sem("squared0"), k + 1))

            def ada(first, n, name):
                pe.wait_ge(sem("c_ready"), 1)
                bank = may_fill(pe, name)
                for i in range(first, first + n):
                    w = slot(arrived(pe, ("ada", i)))
                    for j in range(4):
                        for k in range(KD):
                            mm = pe.matmul(bank[:, 4 * i + j:4 * i + j + 1], w[:, k, j * P:(j + 1) * P],
                                           cact[:, k:k + 1], start=(k == 0), stop=(k == KD - 1))
                mm.then_inc(full(name), 1)

            ada(0, 4, "mod_a")
            for n in range(4):
                w = slot(arrived(pe, ("glu", n)))
                for jj in range(2):
                    j = 2 * n + jj
                    may_fill(pe, ("glu_a", j))
                    project(("glu_a", j), w, jj * P, P, h,
                            ready=(lambda k: pe.wait_ge(sem("h_ready"), k + 1)) if j == 0 else None)
                    may_fill(pe, ("glu_g", j))
                    project(("glu_g", j), w, 256 + jj * P, P, h)
            made = 0
            for j in range(KD):
                name = ("conv", j)
                bank = may_fill(pe, name)
                pe.wait_ge(sem("u_edge"), 1)
                moved(pe, ("glu_a", j))
                for w in range(PE_TAPS):
                    pe.wait_ge(sem("diag_ready"), made + 1)
                    mm = pe.matmul(bank[:, 0:T], diag[:, made % DIAGS, :], u[:, j, w:w + T],
                                   start=(w == 0), stop=(w == PE_TAPS - 1))
                    mm.then_inc(sem("diag_used"), 1)
                    made += 1
            ada(4, 8, "mod_b")
            total("mean1", y, KD, lambda k: moved(pe, ("conv", k)))
            total("var1", sq, KD, lambda k: pe.wait_ge(sem("squared1"), k + 1))
            for n in range(2):
                w = slot(arrived(pe, ("proj1", n)))
                for j in range(4 * n, 4 * n + 4):
                    may_fill(pe, ("proj1", j))
                    project(("proj1", j), w, (j % 4) * P, P, h,
                            ready=(lambda k: pe.wait_ge(sem("act_ready"), k + 1)) if j == 0 else None)
            total("ms2", sq, KD, lambda k: pe.wait_ge(sem("squared2"), k + 1))

            pe.wait_ge(sem("router_in"), 64)
            bank = may_fill(pe, "logit")
            for t in range(NT):
                for k in range(KD):
                    pe.wait_ge(sem("h2_ready"), k + 1)
                    pe.matmul(bank[:, t * 64:t * 64 + 36], h2[:, k, t * P:(t + 1) * P], wr[:, k, :],
                              start=(k == 0), stop=False)
                mm = pe.matmul(bank[:, t * 64:t * 64 + 36], ones[0:1, :], brow[0:1, :], start=False, stop=True)
            mm.then_inc(full("logit"), 1)
            for t in range(NT):
                for half in range(2):
                    name = ("h2tok", t, half)
                    bank = may_fill(pe, name)
                    for j in range(4):
                        mm = pe.transpose(bank[:, j * P:(j + 1) * P], h2[:, 4 * half + j, t * P:(t + 1) * P], ident)
                    mm.then_inc(full(name), 1)
            pe.wait_ge(sem("chosen"), 1)
            pe.wait_ge(sem("route_in"), 16)
            bank = may_fill(pe, "rank")
            strict = rc[:, R_STRICT:R_STRICT + P]
            picked = small[:, 384:448].rearrange("p (t e) -> p t e", t=NT)
            pe.matmul(bank[:, 0:32], strict, picked[:, 0, :], start=True, stop=True)
            pe.matmul(bank[:, 32:64], ones, picked[:, 0, :], start=True, stop=False)
            pe.matmul(bank[:, 32:64], strict, picked[:, 1, :], start=False, stop=True)
            pe.matmul(bank[:, 64:96], ones, picked[:, 0, :], start=True, stop=False)
            pe.matmul(bank[:, 64:96], ones, picked[:, 1, :], start=False, stop=True).then_inc(full("rank"), 1)
            for j in range(KD):
                name = ("gather", j)
                bank = may_fill(pe, name)
                for t in range(NT):
                    pe.wait_ge(sem("sel_ready"), t + 1)
                    moved(pe, ("h2tok", t, j // 4))
                    mm = pe.matmul(bank[:, :], h2_tok[:, t, j * P:(j + 1) * P], sel[:, t, :],
                                   start=(t == 0), stop=(t == NT - 1))
                mm.then_inc(full(name), 1)
            for n in range(2):
                name = ("comb", n)
                bank = may_fill(pe, name)
                for half in range(2):
                    for t in range(NT):
                        pe.wait_ge(sem("selw_ready"), t + 1)
                        s = 2 * n + half
                        mm = pe.transpose(bank[:, half * T + t * P:half * T + (t + 1) * P],
                                          selw[:, t, s * P:(s + 1) * P], ident)
                mm.then_inc(full(name), 1)
            for b in range(8):
                if BEFORE_EXPERTS[b]:
                    pe.wait_ge(sem(f"bank{b}_read"), BEFORE_EXPERTS[b])

            def into_hidden(w, window, bank):
                for f in range(KF):
                    for k in range(KD):
                        mm = pe.matmul(bank[:, f * WIN:(f + 1) * WIN], w[:, k, f * P:(f + 1) * P], window[:, k, :],
                                       start=(k == 0), stop=(k == KD - 1))
                return mm

            def down(w):
                for j in range(KD):
                    for f in range(KF):
                        mm = pe.matmul(Y_BANK[:, j * WIN:(j + 1) * WIN], w[:, f, j * P:(j + 1) * P], hid[:, f, :],
                                       start=(f == 0), stop=(f == KF - 1))
                return mm

            def expert(e, b, uses):
                pe.wait_ge(win_ready, e + 1)
                pe.wait_ge(sem(f"slot{3 * b}"), uses(3 * b))
                into_hidden(slot(3 * b), xw[b], G_BANK).then_inc(gate_full, 1)
                pe.wait_ge(sem(f"slot{3 * b + 1}"), uses(3 * b + 1))
                into_hidden(slot(3 * b + 1), xw[b], U_BANK).then_inc(up_full, 1)
                pe.wait_ge(sem(f"slot{3 * b + 2}"), uses(3 * b + 2))
                pe.wait_ge(hid_ready, e + 1)
                pe.wait_ge(y_moved, e + 1)
                down(slot(3 * b + 2, KF, D)).then_inc(y_full, 1)

            with pe.Fori(0, LOOPS) as it:
                for b in range(BODY):
                    expert(it * BODY + b, b, lambda s: it * 16 + (EXPERT_BASE[s] + 16))
            for b in range(PEELED):
                expert(LOOPS * BODY + b, b, lambda s: LOOPS * 16 + EXPERT_BASE[s] + 16)
            with pe.If(overflow(pe)):
                with pe.Fori(0, EXPERTS) as e:
                    pe.wait_ge(sem("over_in"), e * 48 + 48)
                    for r in range(3):
                        pe.wait_ge(sem("over_window"), e * 3 + (r + 1))
                        into_hidden(slot(0), xw[0], G_BANK).then_inc(sem("over_gate"), 1)
                        into_hidden(slot(1), xw[0], U_BANK).then_inc(sem("over_up"), 1)
                        pe.wait_ge(sem("over_hidden"), e * 3 + (r + 1))
                        down(slot(2, KF, D)).then_inc(sem("over_down"), 1)

            pe.wait_ge(y_moved, C_MOVED + EXPERTS)
            pe.wait_ge(sem("over_end"), 1)
            for s in range(4):
                for half in range(2):
                    name = ("ytok", s, half)
                    bank = may_fill(pe, name)
                    for j in range(4):
                        mm = pe.transpose(bank[:, j * P:(j + 1) * P], yT[:, 4 * half + j, s * P:(s + 1) * P], ident)
                    mm.then_inc(full(name), 1)
            for j in range(KD):
                name = ("moe", j)
                bank = may_fill(pe, name)
                for s in range(4):
                    moved(pe, ("ytok", s, j // 4))
                    mm = pe.matmul(bank[:, 0:T], y_tok[:, s, j * P:(j + 1) * P], comb[:, s, :],
                                   start=(s == 0), stop=(s == 3))
                mm.then_inc(full(name), 1)
            total("ms3", sq2, KD, lambda k: pe.wait_ge(sem("squared3"), k + 1))
            for n in range(2):
                w = slot(arrived(pe, ("cq", n)))
                for j in range(4 * n, 4 * n + 4):
                    may_fill(pe, ("cq", j))
                    project(("cq", j), w, (j % 4) * P, P, xT,
                            ready=(lambda k: pe.wait_ge(sem("x_normed"), k + 1)) if j == 0 else None)
            total("msq", sq2, KQ, lambda k: pe.wait_ge(sem("squared5"), k + 1))
            bank = may_fill(pe, "mskv")
            for k in range(KKV):
                pe.wait_ge(sem("squared5"), KQ + k + 1)
                mm = pe.matmul(bank[:, 0:T], ones, sq2[:, KQ + k, :], start=(k == 0), stop=(k == KKV - 1))
            mm.then_inc(full("mskv"), 1)
            pe.wait_ge(sem("wrope_in"), 16)
            may_fill(pe, "krope")
            project("krope", wrope, 0, ROPE, xT, part=NOPE)
            for n in range(2):
                w = slot(arrived(pe, ("gate1", n)))
                for j in range(4 * n, 4 * n + 4):
                    may_fill(pe, ("gate1", j))
                    project(("gate1", j), w, (j % 4) * P, P, xT)
            w = slot(arrived(pe, "ukv"), KKV, 2048)
            wv = w.rearrange("p k (h c) -> p k h c", c=P)
            for t in range(NT):
                for n in range(2):
                    name = ("v1", t, n)
                    bank = may_fill(pe, name)
                    for k in range(KKV):
                        pe.wait_ge(sem("latent_ready"), KQ + k + 1)
                        mm = pe.matmul(bank[:, :].rearrange("p (h c) -> p h c", c=HD), cq[:, KQ + k, t * P:(t + 1) * P], wv[:, k, 8 * n:8 * n + 8, NOPE:P],
                                       start=(k == 0), stop=(k == KKV - 1))
                    mm.then_inc(full(name), 1)
            for p in range(HEADS // 2):
                name = ("kn", p)
                may_fill(pe, name)
                for half in range(2):
                    project(name, w, (2 * p + half) * P, NOPE, cq, k0=KQ, at=half * T, tiles=KKV, done=half == 1)
            for n in range(4):
                w = slot(arrived(pe, ("uq", n)), KQ, 384)
                for p in (2 * n, 2 * n + 1):
                    name = ("q", p)
                    may_fill(pe, name)
                    for half in range(2):
                        project(name, w, ((2 * p + half) % 4) * QK, QK, cq, at=half * T, tiles=KQ, done=half == 1)

            def attention(layer, q_of, k_of, ready):
                for i in range(HEADS + 3):
                    if i < HEADS:
                        ready(i)
                        name = ("s", layer, i)
                        bank = may_fill(pe, name)
                        q, k = q_of(i), k_of(i)
                        pe.matmul(bank[:, 0:P], q[:, 0:P], k[:, 0:P], start=True, stop=True)
                        pe.matmul(bank[:, P:3 * P], q[:, P:T], k[:, 0:T], start=True, stop=True) \
                            .then_inc(full(name), 1)
                    if 0 <= i - 2 < HEADS:
                        n = i - 2
                        name = ("pt", layer, n)
                        bank = may_fill(pe, name)
                        pe.wait_ge(sem("probs_ready"), HEADS * layer + n + 1)
                        for c in range(3):
                            mm = pe.transpose(bank[:, c * P:(c + 1) * P], prob[:, n % 4, c * P:(c + 1) * P], ident)
                        mm.then_inc(full(name), 1)
                    if i >= 3:
                        n = i - 3
                        name = ("o", layer, n // 2)
                        at = HD * (n % 2)
                        bank = may_fill(pe, name) if n % 2 == 0 else ps[use[name][0]]
                        moved(pe, ("pt", layer, n))
                        pe.matmul(bank[at:at + HD, 0:T], v[:, 0, n * HD:(n + 1) * HD], prob_t[:, n % 4, 0:T],
                                  start=True, stop=False, skip_group_check=True)
                        mm = pe.matmul(bank[at:at + HD, P:T], v[:, 1, n * HD:(n + 1) * HD],
                                       prob_t[:, n % 4, T:3 * P], start=False, stop=True, skip_group_check=True)
                        if n % 2:
                            mm.then_inc(full(name), 1)

            def out_layer(layer):
                for n in range(2):
                    w = slot(arrived(pe, ("wo", layer, n)))
                    for j in range(4 * n, 4 * n + 4):
                        may_fill(pe, ("proj2", layer, j))
                        project(("proj2", layer, j), w, (j % 4) * P, P, o,
                                ready=(lambda k: moved(pe, ("o", layer, k))) if j == 0 else None)
                total(("mean2", layer), xT, KD, lambda k: moved(pe, ("proj2", layer, k)))
                total(("var2", layer), sq2, KD, lambda k: pe.wait_ge(sem("squared4"), KD * layer + k + 1))

            def ready_a(i):
                if i == 0:
                    pe.wait_ge(sem("krope_spread"), 1)
                    for p in range(HEADS // 2 - 4, HEADS // 2):
                        moved(pe, ("kn", p))
                    pe.wait_ge(sem("mla_in"), 16)
                    for t in range(NT):
                        for n in range(2):
                            moved(pe, ("v1", t, n))
                pe.wait_ge(sem("q_ready"), i // 2 + 1)

            attention(0, lambda i: qh[0:QK, i, :], lambda i: kh[0:QK, i, :], ready_a)
            out_layer(0)

            def rotate(n, j):
                name = ("rot", n, j)
                bank = may_fill(pe, name)
                moved(pe, ("raw", n, j))
                pe.matmul(bank[:, 0:T], bc[:, B_ROT:B_ROT + P], raw_b[:, j, :], start=True, stop=True) \
                    .then_inc(full(name), 1)

            for n, kind in enumerate(("kv", "in")):
                for j in range(KD):
                    if j % 4 == 0:
                        w = slot(arrived(pe, (kind, j // 4)))
                    may_fill(pe, ("raw", n, j))
                    project(("raw", n, j), w, (j % 4) * P, P, xT,
                            ready=(lambda k: pe.wait_ge(sem("layer_ready"), k + 1)) if n == j == 0 else None)
                    if j == 1 and n == 0:
                        pe.wait_ge(sem("moba_in"), 16)
                    if j:
                        rotate(n, j - 1)
                rotate(n, KD - 1)
                if n == 0:
                    ws = [slot(arrived(pe, (kind, 2))), slot(arrived(pe, (kind, 3)))]
                    for t in range(NT):
                        for half in range(2):
                            name = ("v2", t, half)
                            bank = may_fill(pe, name)
                            for k in range(KD):
                                mm = pe.matmul(bank[:, :], xT[:, k, t * P:(t + 1) * P], ws[half][:, k, :],
                                               start=(k == 0), stop=(k == KD - 1))
                            mm.then_inc(full(name), 1)
                else:
                    for j in range(KD):
                        if j % 4 == 0:
                            w = slot(arrived(pe, (kind, 2 + j // 4)))
                        may_fill(pe, ("gate2", j))
                        project(("gate2", j), w, (j % 4) * P, P, xT)

            def ready_b(i):
                if i == 0:
                    for t in range(NT):
                        for n in range(2):
                            moved(pe, ("v2", t, n))
                pe.wait_ge(sem("turned"), KD + i // 2 + 1)

            attention(1, lambda i: qb[HD * (i % 2):HD * (i % 2) + HD, i // 2, :],
                      lambda i: kb[HD * (i % 2):HD * (i % 2) + HD, i // 2, :], ready_b)
            out_layer(1)
            for t in range(NT):
                for half in range(2):
                    name = ("out", t, half)
                    bank = may_fill(pe, name)
                    for j in range(4):
                        pe.wait_ge(sem("layer_ready"), KD + 4 * half + j + 1)
                        mm = pe.transpose(bank[:, j * P:(j + 1) * P], final[:, 4 * half + j, t * P:(t + 1) * P], ident)
                    mm.then_inc(full(name), 1)

        @block.vector
        def _(dve):
            steps = [0]

            def then(ins):
                steps[0] += 1
                ins.then_inc(sem("vector_step"), 1)
                dve.wait_ge(sem("vector_step"), steps[0])

            rstd_count = [0]

            def inverse(name, parked):
                moved(dve, name)
                dve.reciprocal(parked, std if name in ("ms1", "var1", "ms2") else std2) \
                    .then_inc(sem("rstd_ready"), 1)
                rstd_count[0] += 1
                dve.wait_ge(sem("rstd_ready"), rstd_count[0])
                return parked

            def rstd_of(name):
                return inverse(name, ps[use[name][0]][:, T:2 * T])

            dve.sem_inc(y_moved, C_MOVED)
            dve.memset(eps6, EPS).then_inc(sem("eps_ready"), 1)
            dve.memset(eps5, LN_EPS).then_inc(sem("eps_ready"), 1)
            for j in range(KD):
                bank = filled(dve, ("x", j))
                dve.tensor_copy(xT[:, j, :], bank[:, 0:T]).then_inc(read(("x", j)), 1)
            bank = filled(dve, "par")
            dve.tensor_copy(par[:, :], bank[:, 0:PAR]).then_inc(read("par"), 1)
            rstd = rstd_of("ms1")
            dve.memset(u[:, :, 0:TAPS - 1], 0.0).then_inc(sem("u_edge"), 1)
            bank = filled(dve, "mod_a")
            moved(dve, "par")
            dve.tensor_tensor(mod[:, 0:16], bank[:, 0:16], par[:, 0:16], ALU.add).then_inc(read("mod_a"), 1)
            moved(dve, "mod_a")
            then(dve.scalar_tensor_tensor(out=a1, in0=mod[:, 8:16], scalar=1.0,
                                          in1=par[:, COL["norm_mix_g"]:COL["norm_mix_g"] + 8],
                                          op0=ALU.add, op1=ALU.mult))
            for j in range(KD):
                moved(dve, ("x", j))
                dve.scalar_tensor_tensor(out=h[:, j, :], in0=xT[:, j, :], scalar=a1[:, j:j + 1], in1=rstd,
                                         op0=ALU.mult, op1=ALU.mult).then_inc(sem("h_scaled"), 1)
            for j in range(KD):
                bank = filled(dve, ("glu_a", j))
                moved(dve, ("glu_g", j))
                dve.scalar_tensor_tensor(out=u[:, j, TAPS - 1:], in0=bank[:, 0:T], scalar=col("conv_b_in", j),
                                         in1=sg[:, j % 4, :], op0=ALU.add, op1=ALU.mult) \
                    .then_inc(read(("glu_a", j)), 1)
            dve.wait_ge(sem("u_edge"), 1)
            taps = TAPS - PE_TAPS
            for j in range(0, KD, 2):
                for w in range(taps):
                    for c in range(2):
                        name = ("conv", j + c)
                        bank = ps[use[name][0]]
                        if w == 0:
                            moved(dve, ("glu_a", j + c))
                            dve.wait_ge(sem("diag_used"), PE_TAPS * (j + c + 1))
                        else:
                            dve.wait_ge(sem("tap_done"), (j // 2) * 2 * (taps - 1) + 2 * (w - 1) + c + 1)
                        done = sem("conv_done") if w == taps - 1 else sem("tap_done")
                        dve.scalar_tensor_tensor(out=bank[:, 0:T], in0=u[:, j + c, PE_TAPS + w:PE_TAPS + w + T],
                                                 scalar=col("dw", (PE_TAPS + w) * KD + j + c), in1=bank[:, 0:T],
                                                 op0=ALU.mult, op1=ALU.add).then_inc(done, 1)
            bank = filled(dve, "mod_b")
            dve.tensor_tensor(mod[:, 16:48], bank[:, 16:48], par[:, 16:48], ALU.add).then_inc(read("mod_b"), 1)
            moved(dve, "mod_b")
            then(dve.scalar_tensor_tensor(out=a2, in0=mod[:, 32:40], scalar=1.0,
                                          in1=par[:, COL["norm_ffn_g"]:COL["norm_ffn_g"] + 8],
                                          op0=ALU.add, op1=ALU.mult))
            bank = filled(dve, "mean1")
            for j in range(KD):
                moved(dve, ("conv", j))
                dve.scalar_tensor_tensor(out=y[:, j, :], in0=bank[:, 0:T], scalar=-1.0 / D, in1=y[:, j, :],
                                         op0=ALU.mult, op1=ALU.add).then_inc(sem("centred1"), 1)
            dve.wait_ge(sem("centred1"), KD)
            rstd = rstd_of("var1")
            for j in range(KD):
                dve.scalar_tensor_tensor(out=y[:, j, :], in0=y[:, j, :], scalar=col("conv_ln_g", j), in1=rstd,
                                         op0=ALU.mult, op1=ALU.mult).then_inc(sem("normed1"), 1)
            for j in range(KD):
                bank = filled(dve, ("proj1", j))
                dve.scalar_tensor_tensor(out=xT[:, j, :], in0=bank[:, 0:T], scalar=mod[:, 16 + j:17 + j],
                                         in1=xT[:, j, :], op0=ALU.mult, op1=ALU.add) \
                    .then_inc(read(("proj1", j)), 1)
            rstd = rstd_of("ms2")
            for j in range(KD):
                moved(dve, ("proj1", j))
                dve.scalar_tensor_tensor(out=scaled[:, j, :], in0=xT[:, j, :], scalar=a2[:, j:j + 1], in1=rstd,
                                         op0=ALU.mult, op1=ALU.mult).then_inc(sem("h2_scaled"), 1)

            def tmp(at, n, e):
                return small[:, at:at + n * e].rearrange("p (t e) -> p t e", t=n)

            def wide(a, n):
                return a.unsqueeze(2).broadcast_to((P, NT, n))

            iota32 = rc[:, R_IOTA32:R_IOTA32 + EXPERTS]
            bank = filled(dve, "logit")
            dve.wait_ge(sem("route_in"), 16)
            logit = tmp(0, NT, 36)
            dve.tensor_copy(logit, bank[:, 0:128].rearrange("p (t e) -> p t e", t=NT)[:, :, 0:36]) \
                .then_inc(read("logit"), 1)
            moved(dve, "logit")
            gmax, m1, m2, mn = small[:, 72:74], small[:, 74:76], small[:, 76:78], small[:, 78:80]

            def first_max(values, n, most, flags, cand, picked):
                then(dve.tensor_reduce(most, values, AX.X, ALU.max))
                then(dve.tensor_tensor(flags, values, wide(most, n), ALU.is_equal))
                for t in range(NT):
                    ins = dve.scalar_tensor_tensor(out=cand[:, t, :], in0=flags[:, t, :], scalar=-64.0,
                                                   in1=iota32[:, 0:n], op0=ALU.mult, op1=ALU.add)
                    if t < NT - 1:
                        ins.then_inc(sem("first_half"), 1)
                        first[0] += 1
                then(ins)
                dve.wait_ge(sem("first_half"), first[0])
                then(dve.tensor_reduce(mn, cand, AX.X, ALU.min))
                then(dve.tensor_tensor(picked, cand, wide(mn, n), ALU.is_equal))

            first = [0]
            flags, cand = tmp(128, NT, 32), tmp(192, NT, 32)
            oh1, oh2, picked, em = tmp(256, NT, 32), tmp(320, NT, 32), tmp(384, NT, 32), tmp(448, NT, 32)
            glog, elog = logit[:, :, 0:GROUPS], logit[:, :, GROUPS:36]
            ohg, gflag, gcand = tmp(96, NT, 4), tmp(104, NT, 4), tmp(112, NT, 4)
            first_max(glog, GROUPS, gmax, gflag, gcand, ohg)
            dve.tensor_tensor(tmp(80, NT, 4), glog, wide(gmax, 4), ALU.subtract).then_inc(sem("group_shifted"), 1)
            pen = tmp(120, NT, 4)
            then(dve.tensor_scalar(pen, ohg, BIG, -BIG, ALU.mult, ALU.add))
            for t in range(NT):
                then(dve.tensor_tensor(em[:, t, :].rearrange("p (g e) -> p g e", g=GROUPS),
                                       elog[:, t, :].rearrange("p (g e) -> p g e", g=GROUPS),
                                       pen[:, t, :].unsqueeze(2).broadcast_to((P, GROUPS, PER_GROUP)), ALU.add))
            first_max(em, EXPERTS, m1, flags, cand, oh1)
            then(dve.scalar_tensor_tensor(out=em.rearrange("p t e -> p (t e)"),
                                          in0=oh1.rearrange("p t e -> p (t e)"), scalar=-3 * BIG,
                                          in1=em.rearrange("p t e -> p (t e)"), op0=ALU.mult, op1=ALU.add))
            first_max(em, EXPERTS, m2, flags, cand, oh2)
            dve.tensor_tensor(picked, oh1, oh2, ALU.add).then_inc(sem("chosen"), 1)
            dve.tensor_tensor(small[:, 88:90], m2, m1, ALU.subtract).then_inc(sem("pair_shifted"), 1)
            dve.wait_ge(sem("group_exp"), 1)
            gsum, gp, es, w1, w2 = (small[:, 520:522], small[:, 522:524], small[:, 524:526],
                                    small[:, S_W1:S_W1 + 2], small[:, S_W2:S_W2 + 2])
            then(dve.tensor_reduce(gsum, tmp(80, NT, 4), AX.X, ALU.add))
            then(dve.reciprocal(gp, gsum))
            dve.wait_ge(sem("pair_exp"), 1)
            then(dve.tensor_scalar(es, small[:, 88:90], 1.0, None, ALU.add))
            then(dve.reciprocal(es, es))
            then(dve.tensor_tensor(w1, es, gp, ALU.mult))
            then(dve.tensor_tensor(w2, w1, small[:, 88:90], ALU.mult))
            bank = filled(dve, "rank")
            cnt = small[:, 530:562]
            incl, start = small[:, 562:594], small[:, 594:626]
            then(dve.tensor_copy(cnt, bank[:, 64:96]))
            then(dve.tensor_tensor_scan(incl, ones[:, 0:EXPERTS], cnt, 0.0, ALU.mult, ALU.add))
            then(dve.tensor_tensor(start, incl, cnt, ALU.subtract))
            pos = tmp(640, NT, 32)
            dve.tensor_tensor(pos, bank[:, 0:64].rearrange("p (t e) -> p t e", t=NT),
                              start.unsqueeze(1).broadcast_to((P, NT, EXPERTS)), ALU.add).then_inc(read("rank"), 1)
            moved(dve, "rank")
            then(dve.tensor_tensor(flags, oh1, pos, ALU.mult))
            then(dve.tensor_reduce(small[:, S_P1:S_P1 + 2], flags, AX.X, ALU.add))
            then(dve.tensor_tensor(flags, oh2, pos, ALU.mult))
            dve.tensor_reduce(small[:, S_P2:S_P2 + 2], flags, AX.X, ALU.add).then_inc(sem("slots_known"), 1)
            dve.wait_ge(sem("slots_known"), 1)
            iota = rc[:, R_IOTA:R_IOTA + SLOTS_A]
            for t in range(NT):
                then(dve.tensor_scalar(sel[:, t, :], iota, small[:, S_P1 + t:S_P1 + t + 1], None, ALU.is_equal))
                dve.scalar_tensor_tensor(out=sel[:, t, :], in0=iota, scalar=small[:, S_P2 + t:S_P2 + t + 1],
                                         in1=sel[:, t, :], op0=ALU.is_equal, op1=ALU.add) \
                    .then_inc(sem("sel_ready"), 1)
            row = tmp(740, 1, 132)[0:1, 0, :]
            over, at_, end = small[0:1, 880:912], small[0:1, 912:944], small[0:1, 944:976]
            then(dve.tensor_copy(row[:, 0:EXPERTS], start[0:1, :]))
            then(dve.memset(row[:, EXPERTS:EXPERTS + 4], 0.0))
            then(dve.tensor_reduce(row[:, EXPERTS:EXPERTS + 1], cnt[0:1, :], AX.X, ALU.max))
            then(dve.tensor_scalar(end, incl[0:1, :], float(-WIN), None, ALU.add))
            for r in range(1, 4):
                then(dve.tensor_scalar(over, cnt[0:1, :], float(WIN * r), None, ALU.is_gt))
                then(dve.scalar_tensor_tensor(out=at_, in0=start[0:1, :], scalar=float(WIN * r), in1=end,
                                              op0=ALU.add, op1=ALU.min))
                then(dve.scalar_tensor_tensor(out=at_, in0=at_, scalar=float(-NOWHERE), in1=over,
                                              op0=ALU.add, op1=ALU.mult))
                lo = EXPERTS + 4 + EXPERTS * (r - 1)
                then(dve.tensor_scalar(row[:, lo:lo + EXPERTS], at_, float(NOWHERE), None, ALU.add))
            dve.tensor_copy(table[0:1, :], row).then_inc(sem("table_ready"), 1)
            for j in range(1, KD, 2):
                bank = filled(dve, ("gather", j))
                dve.tensor_copy(xg[:, j, 0:SLOTS_A], bank[:, :]).then_inc(read(("gather", j)), 1)
            for n in range(2):
                bank = filled(dve, ("comb", n))
                if n == 0:
                    dve.wait_ge(sem("table_ready"), 1)
                    filled(dve, ("comb", 1))
                dve.tensor_copy(comb[:, 2 * n:2 * n + 2, :], bank[:, :].rearrange("p (s n) -> p s n", s=2)) \
                    .then_inc(read(("comb", n)), 1)

            def gated():
                return dve.tensor_tensor(hid.rearrange("p k n -> p (k n)"), U_BANK[:, 0:KF * WIN],
                                         silu_g.rearrange("p k n -> p (k n)"), ALU.mult)

            def place_result(place):
                at = dve.value_load(table[0:1, bass.ds(place, 1)], min_val=0, max_val=SLOTS_A)
                return dve.tensor_copy(yT[:, :, bass.ds(at, WIN)], Y_BANK[:, :].rearrange("p (k n) -> p k n", k=KD))

            with dve.Fori(0, EXPERTS) as e:
                dve.wait_ge(silu_done, e + 1)
                dve.wait_ge(up_full, e + (C_UP + 1))
                gated().then_inc(hid_ready, 1)
                dve.wait_ge(y_moved, e + C_MOVED)
                dve.wait_ge(y_full, e + 1)
                place_result(e).then_inc(y_moved, 1)
            dve.wait_ge(y_moved, C_MOVED + EXPERTS)
            dve.sem_inc(sem("over_moved"), 1)
            with dve.If(overflow(dve)):
                with dve.Fori(0, EXPERTS) as e:
                    for r in range(3):
                        dve.wait_ge(sem("over_silu"), e * 3 + (r + 1))
                        dve.wait_ge(sem("over_up"), e * 3 + (r + 1))
                        gated().then_inc(sem("over_hidden"), 1)
                        dve.wait_ge(sem("over_moved"), e * 3 + (r + 1))
                        dve.wait_ge(sem("over_down"), e * 3 + (r + 1))
                        place_result(e + (EXPERTS + 4 + EXPERTS * r)).then_inc(sem("over_moved"), 1)
                dve.wait_ge(sem("over_moved"), 3 * EXPERTS + 1)
            dve.sem_inc(sem("over_end"), 1)

            for s in range(4):
                name = ("ytok", s, 1)
                bank = filled(dve, name)
                dve.tensor_copy(y_tok[:, s, 512:D], bank[:, :]).then_inc(read(name), 1)
            for j in range(KD):
                bank = filled(dve, ("moe", j))
                dve.scalar_tensor_tensor(out=xT[:, j, :], in0=bank[:, 0:T], scalar=mod[:, 40 + j:41 + j],
                                         in1=xT[:, j, :], op0=ALU.mult, op1=ALU.add).then_inc(read(("moe", j)), 1)
            rstd = rstd_of("ms3")
            for j in range(KD):
                moved(dve, ("moe", j))
                dve.scalar_tensor_tensor(out=xT[:, j, :], in0=xT[:, j, :], scalar=col("final_g", j), in1=rstd,
                                         op0=ALU.mult, op1=ALU.mult).then_inc(sem("x_normed"), 1)

            for j in range(KQ + KKV):
                bank = filled(dve, ("cq", j))
                dve.tensor_copy(cq[:, j, :], bank[:, 0:T]).then_inc(read(("cq", j)), 1)
            rq = rstd_of("msq")
            for j in range(KQ):
                moved(dve, ("cq", j))
                dve.scalar_tensor_tensor(out=cq[:, j, :], in0=cq[:, j, :], scalar=col("mla_q_norm_2", j), in1=rq,
                                         op0=ALU.mult, op1=ALU.mult).then_inc(sem("latent_ready"), 1)
            rkv = rstd_of("mskv")
            for j in range(KKV):
                moved(dve, ("cq", KQ + j))
                dve.scalar_tensor_tensor(out=cq[:, KQ + j, :], in0=cq[:, KQ + j, :],
                                         scalar=col("mla_kv_norm_2", j), in1=rkv,
                                         op0=ALU.mult, op1=ALU.mult).then_inc(sem("latent_ready"), 1)
            swap = [(i + ROPE // 2) % ROPE for i in range(ROPE)]
            cosA = ac[NOPE:QK, A_COS:A_COS + T]
            sinA = ac[NOPE:QK, A_SIN:A_SIN + T]
            dve.wait_ge(sem("mla_in"), 16)
            moved(dve, "krope")
            k_raw, k_turn = raw[NOPE:QK, 3, 0:T], raw[NOPE:QK, 3, T:2 * T]
            then(dve.stream_shuffle(k_turn, k_raw, swap))
            then(dve.tensor_tensor(k_turn, k_turn, sinA, ALU.mult))
            then(dve.tensor_tensor(k_raw, k_raw, cosA, ALU.mult))
            dve.tensor_tensor(k_raw, k_raw, k_turn, ALU.add).then_inc(sem("krope_ready"), 1)
            for t in range(NT):
                name = ("v1", t, 1)
                bank = filled(dve, name)
                dve.tensor_copy(v[:, t, 512:D], bank[:, :]).then_inc(read(name), 1)
            for p in range(1, HEADS // 2, 2):
                name = ("kn", p)
                bank = filled(dve, name)
                dve.tensor_copy(kh[0:NOPE, 2 * p:2 * p + 2, :], bank[0:NOPE, :].rearrange("p (h n) -> p h n", h=2)) \
                    .then_inc(read(name), 1)
            sin2 = sinA.unsqueeze(1).broadcast_to((ROPE, 2, T))
            for p in range(HEADS // 2):
                moved(dve, ("q", p))
                turn = raw[NOPE:QK, p % 2, :].rearrange("p (h n) -> p h n", h=2)
                q = qh[NOPE:QK, 2 * p:2 * p + 2, :]
                dve.stream_shuffle(turn, q, swap).then_inc(sem("q_shuffled"), 1)
                dve.wait_ge(sem("q_shuffled"), p + 1)
                then(dve.tensor_tensor(turn, turn, sin2, ALU.mult))
                dve.wait_ge(sem("q_cos"), p + 1)
                dve.tensor_tensor(q, q, turn, ALU.add).then_inc(sem("q_ready"), 1)

            mask = ac[:, A_MASK:A_MASK + T]

            def attention(layer, scale):
                for i in range(HEADS + 4):
                    if i < HEADS:
                        b = i % 4
                        name = ("s", layer, i)
                        bank = filled(dve, name)
                        if i >= 4:
                            filled(dve, ("pt", layer, i - 4))
                        dve.tensor_tensor_reduce(out=prob[:, b, 0:P], in0=bank[:, 0:P], in1=mask[:, P:T],
                                                 scale=-scale, scalar=3e38, op0=ALU.add, op1=ALU.min,
                                                 accum_out=smin[:, b, 0:1]).then_inc(sem("scores_part"), 1)
                        dve.wait_ge(sem("scores_part"), HEADS * layer + i + 1)
                        dve.tensor_tensor_reduce(out=prob[:, b, P:3 * P], in0=bank[:, P:3 * P], in1=mask,
                                                 scale=-scale, scalar=3e38, op0=ALU.add, op1=ALU.min,
                                                 accum_out=smin[:, b, 1:2]).then_inc(read(name), 1)
                    if 1 <= i <= HEADS:
                        b = (i - 1) % 4
                        dve.wait_ge(sem("exp_done"), 2 * (HEADS * layer + i))
                        dve.reciprocal(srec[:, b, :], ssum[:, b, :]).then_inc(sem("sum_inverse"), 1)
                    if i >= 5 and (i - 5) % 2 == 0 and (i - 5) // 2 < HEADS // 2:
                        merge(layer, (i - 5) // 2)

            def merge(layer, p):
                name = ("o", layer, p)
                bank = filled(dve, name)
                dve.tensor_tensor(o[:, p, :], bank[:, 0:T], gate[:, p, :], ALU.mult).then_inc(read(name), 1)

            def out_norm(layer):
                for j in range(KD):
                    name = ("proj2", layer, j)
                    bank = filled(dve, name)
                    dve.scalar_tensor_tensor(out=xT[:, j, :], in0=xT[:, j, :], scalar=ALPHA, in1=bank[:, 0:T],
                                             op0=ALU.mult, op1=ALU.add).then_inc(read(name), 1)
                name = ("mean2", layer)
                bank = filled(dve, name)
                for j in range(KD):
                    dve.scalar_tensor_tensor(out=xT[:, j, :], in0=bank[:, 0:T], scalar=-1.0 / D, in1=xT[:, j, :],
                                             op0=ALU.mult, op1=ALU.add).then_inc(sem("centred2"), 1)
                dve.wait_ge(sem("centred2"), KD * (layer + 1))
                rs = rstd_of(("var2", layer))
                for j in range(KD):
                    dve.scalar_tensor_tensor(out=xT[:, j, :], in0=xT[:, j, :], scalar=col("ln_g_2", KD * layer + j),
                                             in1=rs, op0=ALU.mult, op1=ALU.mult).then_inc(sem("normed2"), 1)

            attention(0, SCALE_A)
            out_norm(0)
            dve.wait_ge(sem("moba_in"), 16)
            for n in range(2):
                for j in range(KD):
                    name = ("rot", n, j)
                    bank = filled(dve, name)
                    dve.tensor_tensor(turned[:, j, :], bank[:, 0:T], bc[:, B_SIN:B_SIN + T], ALU.mult) \
                        .then_inc(read(name), 1)
                    moved(dve, name)
                    dve.wait_ge(sem("raw_cos"), KD * n + j + 1)
                    to = qb if n else kb
                    dve.tensor_tensor(to[:, j, :], raw_b[:, j, :], turned[:, j, :], ALU.add) \
                        .then_inc(sem("turned"), 1)
            attention(1, SCALE_B)
            out_norm(1)
            for t in range(NT):
                name = ("out", t, 0)
                bank = filled(dve, name)
                dve.tensor_copy(out_tok[:, t, 0:512], bank[:, :]).then_inc(sem(f"out_ready{t}"), 1)


_USED = ["x", "c", "ada_w", "ada_b", "norm_mix_g", "norm_ffn_g", "final_g", "conv_w_in", "conv_b_in",
         "conv_w_dw", "conv_b_dw", "conv_ln_g", "conv_ln_b", "conv_w_out", "moe_w_rg", "moe_b_rg",
         "moe_w_re", "moe_b_re", "moe_w_gate", "moe_w_up", "moe_w_down", "mla_w_in_2", "mla_q_norm_2",
         "mla_kv_norm_2", "mla_w_uq_2", "mla_w_ukv_2", "mla_w_o_2", "moba_w_kv_2", "moba_w_in_2",
         "moba_w_o_2", "ln_g_2", "ln_b_2"]


def shape_constants():
    base = np.concatenate([np.eye(P), np.ones((P, P))], 1)
    i = np.arange(P)
    route = np.concatenate([i[:, None] < i[None, :],
                            np.broadcast_to(np.arange(SLOTS_A), (P, SLOTS_A)),
                            np.broadcast_to(np.arange(EXPERTS), (P, EXPERTS))], 1)
    mask = np.concatenate([np.zeros((P, P)), np.where(i[None, :] <= i[:, None], 0.0, -BIG)], 1)

    def tables(dim):
        inv = np.float32(10000.0) ** (-np.arange(0, dim, 2, dtype=np.float32) / np.float32(dim))
        ang = np.arange(T, dtype=np.float32)[None, :] * inv.astype(np.float32)[:, None]
        ang = np.concatenate([ang, ang], 0)
        return np.cos(ang), np.sin(ang)

    cos, sin = tables(ROPE)
    sign = np.where(np.arange(ROPE) < ROPE // 2, -1.0, 1.0)[:, None]
    mla = np.zeros((P, A_COLS))
    mla[:, 0:T] = mask
    mla[NOPE:QK, A_COS:A_COS + T] = cos
    mla[NOPE:QK, A_SIN:A_SIN + T] = sin * sign
    cos, sin = tables(HD)
    rot = np.zeros((P, P))
    for m in range(P):
        if m % HD < HD // 2:
            rot[m + HD // 2, m] = -1.0
        else:
            rot[m - HD // 2, m] = 1.0
    moba = np.concatenate([np.tile(cos, (2, 1)), np.tile(sin, (2, 1)), rot], 1)
    return {"k_base": base, "k_route": route, "k_mla": mla, "k_moba": moba}


def kernel(**inputs):
    import concourse.bacc as bacc
    from concourse.bass_utils import run_bass_kernel_spmd

    nc = bacc.Bacc("TRN2", target_bir_lowering=False, num_devices=1)
    arrays, A = {}, {}
    given = {name: np.ascontiguousarray(inputs[name]) for name in _USED}
    for name, a in shape_constants().items():
        given[name] = np.ascontiguousarray(a.astype(np.float32))
    for name, a in given.items():
        arrays[f"in_{name}"] = a
        A[name] = nc.dram_tensor(f"in_{name}", a.shape, mybir.dt.from_np(a.dtype), kind="ExternalInput").ap()
    out = nc.dram_tensor("out_0", (1, T, D), F32, kind="ExternalOutput").ap()
    two_blocks(nc, A, out)
    r = run_bass_kernel_spmd(nc, [arrays], core_ids=[0])
    return r.results[0]["out_0"]
```

```python
from contextlib import ExitStack

import numpy as np
import concourse.bass as bass
from concourse import mybir

ALU = mybir.AluOpType
ACT = mybir.ActivationFunctionType
F32 = mybir.dt.float32
I32 = mybir.dt.int32
AX = mybir.AxisListType

P = 128
T = 256
NT = T // P
D = 1024
KD = D // P
TAPS = 31
EXPERTS = 32
GROUPS = 4
PER_GROUP = EXPERTS // GROUPS
HIDDEN = 512
KF = HIDDEN // P
SLOTS_A = 2 * T
WIN = 64
PADDED = SLOTS_A + WIN
NOWHERE = SLOTS_A
BIG = 1e30
EPS = 1e-6
LN_EPS = 1e-5
ALPHA = 4 ** 0.25

HEADS = 16
NOPE, ROPE = 64, 32
QK = NOPE + ROPE
HD = 64
KQ = 768 // P
KKV = 256 // P
SCALE_A = QK ** -0.5
SCALE_B = HD ** -0.5

SLOT = 4096
RING = 9
RING_C = 7
BODY = 3
LOOPS = EXPERTS // BODY
PEELED = EXPERTS - LOOPS * BODY
PE_TAPS = 13
DIAGS = 8

C_IDENT, C_ONES = 0, P
R_STRICT, R_IOTA = 0, P
R_IOTA32 = R_IOTA
R_IOTA2 = P + SLOTS_A
R_COLS = 2 * P + SLOTS_A
A_MASK, A_COS, A_SIN = 0, T, 2 * T
A_COLS = 3 * T
B_COS, B_SIN, B_ROT = 0, T, 2 * T
B_COLS = 2 * T + P

LOT0 = [("ada_b", 48), ("conv_b_in", 16), ("norm_mix_g", 8), ("norm_ffn_g", 8), ("final_g", 8),
        ("conv_b_dw", 8), ("conv_ln_g", 8), ("conv_ln_b", 8), ("c", 8)]
LOT1 = [("mla_q_norm_2", 6), ("mla_kv_norm_2", 2), ("ln_g_2", 16), ("ln_b_2", 16)]
COL = {}
_at = 0
for _name, _n in LOT0 + LOT1:
    COL[_name] = _at
    _at += _n
LOT0_ROWS = sum(n for _, n in LOT0)
LOT1_ROWS = sum(n for _, n in LOT1)
COL["dw"] = _at
PAR = _at + TAPS * KD
DW_ROWS = TAPS * KD // 2


def two_blocks(nc, A, out):
    with ExitStack() as ctx:
        def sb(name, shape, dt=F32):
            return ctx.enter_context(nc.sbuf_tensor(name, shape, dt))

        sems = {}

        def sem(name):
            if name not in sems:
                sems[name] = ctx.enter_context(nc.semaphore(name))
            return sems[name]

        R0 = RING * SLOT
        R = R0 + KD * T
        arena = sb("arena", [P, R + 13312])
        consts = sb("consts", [P, 2 * P])
        par = sb("par", [P, PAR])
        mod = sb("mod", [P, 48])
        der = sb("der", [P, 40])
        brow = sb("brow", [1, GROUPS + EXPERTS])
        table = sb("table", [1, 4 * EXPERTS + 4], I32)
        ps = [ctx.enter_context(nc.psum_tensor(f"bank{i}", [P, 512], F32)) for i in range(8)]

        def area(off, k, n):
            return arena[:, off:off + k * n].rearrange("p (k n) -> p k n", k=k)

        ident = consts[:, C_IDENT:C_IDENT + P]
        ones = consts[:, C_ONES:C_ONES + P]

        def col(name, j=0):
            return par[:, COL[name] + j:COL[name] + j + 1]

        a1, a2 = der[:, 8:16], der[:, 16:24]
        own = der[:, 28:40].rearrange("p (b q) -> p b q", b=BODY)
        eps6, eps5 = der[:, 24:25], der[:, 25:26]

        xT = area(R0, KD, T)
        x_tok = area(R, NT, D)
        sq = area(R + 2048, KD, T)
        h = area(R + 4096, KD, T)
        u = area(R + 6144, KD, TAPS - 1 + T)
        y = area(R + 8432, KD, T)
        sg = area(R + 10480, 4, T)
        diag = area(R + 11504, DIAGS, P)
        rows = area(R + 12528, 4, P)
        cact = area(R + 13040, KD, 32)
        ada_rows = arena[:, R + 12528:R + 13040]
        std = arena[:, R + 6144:R + 6144 + T]
        scaled = x_tok.rearrange("p a b -> p (a b)").rearrange("p (k n) -> p k n", k=KD)
        h2 = area(R + 4608, KD, T)
        h2_tok = area(R + 6656, NT, D)
        small = arena[:, R + 9216:R + 10240]
        sel = area(R + 10240, NT, SLOTS_A)
        rc = arena[:, R + 12528:R + 12528 + R_COLS]
        wr = arena[:, R + 8704:R + 8704 + KD * 36].rearrange("p (k n) -> p k n", k=KD)
        xg = area(R, KD, PADDED)
        xw = [area(R + 4608 + b * KD * WIN, KD, WIN) for b in range(BODY)]
        weighted = [area(R + 6144 + b * NT * P, NT, P) for b in range(BODY)]
        silu_g = arena[0:WIN, R + 6912:R + 6912 + HIDDEN]
        hid = arena[0:WIN, R + 7424:R + 7424 + HIDDEN]
        turned_e = [arena[:, R + 10240 + b * 512:R + 10752 + b * 512] for b in range(BODY)]
        hid_t = [a[:, 0:KF * WIN].rearrange("p (f n) -> p f n", f=KF) for a in turned_e]
        comb = [a[:, KF * WIN:512] for a in turned_e]
        y_e = arena[:, R + 11776:R + 12288]
        qh = area(RING_C * SLOT, HEADS, T)
        kh = area((RING_C + 1) * SLOT, HEADS, T)
        cq = area(R, KQ + KKV, T)
        gate = area(R + 2048, KD, T)
        v = area(R + 4096, NT, D)
        o = area(R + 6144, KD, T)
        sq2 = o
        raw = area(R + 6144, 4, 2 * T)
        prob = area(R + 8192, 4, 3 * P)
        prob_t = area(R + 9728, 4, 3 * P)
        ac = arena[:, R + 11264:R + 11264 + A_COLS]
        std2 = arena[:, R + 12032:R + 12288]
        smin = area(R + 12288, 4, 2)
        ssum = area(R + 12296, 4, 2)
        srec = area(R + 12304, 4, 2)
        wrope = area(R + 12352, KD, ROPE)
        qb = area(RING_C * SLOT, KD, T)
        kb = area(RING_C * SLOT + 2048, KD, T)
        raw_b = area((RING_C + 1) * SLOT, KD, T)
        turned = area((RING_C + 1) * SLOT + 2048, KD, T)
        bc = arena[:, R:R + B_COLS]
        out_tok = area(R, NT, D)
        final = area(R + 6144, KD, T)

        def slot(s, k=KD, n=512):
            return arena[:, s * SLOT:s * SLOT + k * n].rearrange("p (k n) -> p k n", k=k)

        use, fills, reads = {}, [0] * 8, [0] * 8

        def plan(name, b, readers=1, counted=1):
            use[name] = (b, fills[b], reads[b], reads[b] + readers)
            fills[b] += counted
            reads[b] += readers

        for j in range(KD):
            plan(("x", j), j % 4)
        plan("par", 4)
        plan("ms1", 7)
        plan(("ada", 0), 6)
        plan(("mod", 0), 5)
        for j in range(KD):
            plan(("glu_a", j), 2 * (j % 2))
            plan(("glu_g", j), 2 * (j % 2) + 1)
        for j in range(KD):
            plan(("conv", j), [4, 5, 0, 1][j % 4], counted=0)
        for g in (1, 2):
            plan(("ada", g), 6)
            plan(("mod", g), 3)
        plan("mean1", 2, readers=0)
        plan("var1", 7)
        for j in range(KD):
            plan(("proj1", j), j % 4)
        plan("ms2", 7)
        plan("logit", 5)
        for t in range(NT):
            for half in range(2):
                plan(("h2tok", t, half), 2 * t + half)
        plan("rank", 4, 1)
        for j in range(KD):
            plan(("gather", j), j % 4)
        BEFORE_EXPERTS = list(reads)
        for n in range(4):
            plan(("acc", n), 4 + n, readers=2, counted=0)
        plan("ms3", 7)
        for j in range(KQ + KKV):
            plan(("cq", j), j % 4)
        plan("msq", 7)
        plan("mskv", 6)
        plan("krope", 4)
        for j in range(KD):
            plan(("gate1", j), j % 4)
        for t in range(NT):
            for n in range(2):
                plan(("v1", t, n), 2 * t + n)
        for p in range(HEADS // 2):
            plan(("kn", p), p % 4)
        for p in range(HEADS // 2):
            plan(("q", p), p % 4)
        for layer in (0, 1):
            if layer:
                for n in range(2):
                    for j in range(KD):
                        plan(("raw", n, j), j % 4)
                        if j:
                            plan(("rot", n, j - 1), 4 + (j - 1) % 2)
                    plan(("rot", n, KD - 1), 4 + (KD - 1) % 2)
                    for w in range(KD if n else 4):
                        plan(("gate2", w) if n else ("v2", w // 2, w % 2), w % 4)
            for i in range(HEADS + 3):
                if i < HEADS:
                    plan(("s", layer, i), i % 2)
                if 0 <= i - 2 < HEADS:
                    plan(("pt", layer, i - 2), 2 + i % 2)
                if 0 <= i - 3 and (i - 3) % 2 == 0:
                    plan(("o", layer, (i - 3) // 2), 4 + (i - 3) // 2 % 2)
            for j in range(KD):
                plan(("proj2", layer, j), j % 4)
            plan(("mean2", layer), 6, readers=0)
            plan(("var2", layer), 7)
        for t in range(NT):
            for half in range(2):
                plan(("out", t, half), 2 * t + half)

        def may_fill(pe, name):
            b, _, before, _ = use[name]
            if before:
                pe.wait_ge(sem(f"bank{b}_read"), before)
            return ps[b]

        def filled(eng, name):
            b, n, _, _ = use[name]
            eng.wait_ge(sem(f"bank{b}_full"), n + 1)
            return ps[b]

        def full(name):
            return sem(f"bank{use[name][0]}_full")

        def read(name):
            return sem(f"bank{use[name][0]}_read")

        def moved(eng, name):
            b, _, _, after = use[name]
            eng.wait_ge(sem(f"bank{b}_read"), after)

        def cols(w, lo, n, k=KD):
            return w[:, lo:lo + n].rearrange("(k p) n -> p k n", p=P)

        chunks = []

        def chunk(name, s, parts, last):
            chunks.append((name, s, parts, last))

        aw = A["ada_w"][0]
        win = A["conv_w_in"][0]
        order = [("ada", i) for i in range(4)] + [("glu", i) for i in range(4)] \
            + [("ada", i) for i in range(4, 12)] + [("proj1", 0), ("proj1", 1)]
        for i, (kind, n) in enumerate(order):
            s = i % RING
            if kind == "ada":
                chunk((kind, n), s, [(slot(s), cols(aw, 512 * n, 512))], ("ada", n // 4))
            elif kind == "glu":
                w = arena[:, s * SLOT:(s + 1) * SLOT].rearrange("p (k n) -> p k n", k=KD)
                chunk((kind, n), s, [(w[:, :, 0:256], cols(win, 256 * n, 256)),
                                     (w[:, :, 256:512], cols(win, D + 256 * n, 256))], ("glu_g", 2 * n + 1))
            else:
                chunk((kind, n), s, [(slot(s), cols(A["conv_w_out"][0], 512 * n, 512))], ("proj1", 4 * n + 3))
        CHUNKS_A = len(chunks)
        assert CHUNKS_A % RING == 0

        def next_c():
            return (RING_C - 1 + len(chunks) - CHUNKS_A) % RING_C

        mw = A["mla_w_in_2"][0]
        for n in range(2):
            s = next_c()
            chunk(("cq", n), s, [(slot(s), cols(mw, 512 * n, 512))], ("cq", 4 * n + 3))
        for n in range(2):
            s = next_c()
            chunk(("gate1", n), s, [(slot(s), cols(mw, D + ROPE + 512 * n, 512))], ("gate1", 4 * n + 3))
        s = next_c()
        chunk("ukv", s, [(slot(s, KKV, 2048), cols(A["mla_w_ukv_2"][0], 0, 2048))], ("kn", HEADS // 2 - 1))
        for n in range(4):
            s = next_c()
            chunk(("uq", n), s, [(slot(s, KQ, 384), cols(A["mla_w_uq_2"][0], 384 * n, 384))], ("q", 2 * n + 1))
        for n in range(2):
            s = next_c()
            chunk(("wo", 0, n), s, [(slot(s), cols(A["mla_w_o_2"][0], 512 * n, 512))], ("proj2", 0, 4 * n + 3))
        for kind, w in (("kv", A["moba_w_kv_2"]), ("in", A["moba_w_in_2"][0])):
            for n in range(4):
                s = next_c()
                if n < 2:
                    last = ("raw", int(kind == "in"), 4 * n + 3)
                else:
                    last = ("v2", 1, n - 2) if kind == "kv" else ("gate2", 4 * n - 5)
                chunk((kind, n), s, [(slot(s), cols(w, 512 * n, 512))], last)
        for n in range(2):
            s = next_c()
            chunk(("wo", 1, n), s, [(slot(s), cols(A["moba_w_o_2"][0], 512 * n, 512))], ("proj2", 1, 4 * n + 3))

        landed, place, count = {}, {}, [0] * RING
        for i, (name, s, parts, _) in enumerate(chunks):
            if i == CHUNKS_A:
                EXPERT_BASE = list(count)
                for e in range(EXPERTS):
                    for m in range(3):
                        count[3 * (e % BODY) + m] += 16
            count[s] += 16 * len(parts)
            landed[name], place[name] = count[s], s

        def arrived(eng, name):
            eng.wait_ge(sem(f"slot{place[name]}"), landed[name])
            return place[name]

        gu_full, silu_done, hid_ready = sem("gate_up_full"), sem("silu_done"), sem("hidden_ready")
        t_full, t_moved = sem("turned_full"), sem("turned_moved")
        y_full, y_moved, win_ready = sem("down_full"), sem("down_moved"), sem("window_ready")
        GU_BANK, Y_BANK, T_BANK = ps[0], ps[1], ps[2]
        ACC = ps[4:8]
        C_T = BODY

        expert_w = [A["moe_w_gate"][0], A["moe_w_up"][0], A["moe_w_down"][0]]

        def overflow(eng):
            eng.wait_ge(sem("table_ready"), 1)
            most = eng.value_load(table[0:1, EXPERTS:EXPERTS + 1], min_val=0, max_val=T)
            return most > WIN

        S_P1, S_P2, S_W1, S_W2 = 1000, 1002, 1004, 1006

        block = ctx.enter_context(nc.Block())

        @block.sync
        def _(sp):
            sp.dma_start(x_tok, A["x"][0].rearrange("(t p) n -> p t n", p=P)).then_inc(sem("x_in"), 16)

            def load(i):
                _, s, parts, _ = chunks[i]
                for dst, src in parts:
                    sp.dma_start(dst, src).then_inc(sem(f"slot{s}"), 16)

            for i in range(CHUNKS_A):
                if i >= RING:
                    filled(sp, chunks[i - RING][3])
                load(i)

            def load_matrix(e, b, m):
                s = 3 * b + m
                dst = slot(s) if m < 2 else slot(s, KF, D)
                src = expert_w[m][bass.ds(e, 1)].rearrange("e (k p) n -> p (e k) n", p=P)
                sp.dma_start(dst, src).then_inc(sem(f"slot{s}"), 16)

            for e in range(BODY):
                for m in range(3):
                    filled(sp, chunks[CHUNKS_A - RING + 3 * e + m][3])
                    load_matrix(e, e, m)
            with sp.Fori(0, LOOPS - 1) as it:
                for b in range(BODY):
                    sp.wait_ge(gu_full, it * BODY + (b + 1))
                    load_matrix(it * BODY + (BODY + b), b, 0)
                    load_matrix(it * BODY + (BODY + b), b, 1)
                    sp.wait_ge(y_full, it * BODY + (b + 1))
                    load_matrix(it * BODY + (BODY + b), b, 2)
            for b in range(PEELED):
                e = LOOPS * BODY + b
                sp.wait_ge(gu_full, e - BODY + 1)
                load_matrix(e, b, 0)
                load_matrix(e, b, 1)
                sp.wait_ge(y_full, e - BODY + 1)
                load_matrix(e, b, 2)
            with sp.If(overflow(sp)):
                sp.wait_ge(y_full, EXPERTS)
                with sp.Fori(0, EXPERTS) as e:
                    sp.wait_ge(sem("over_done"), e * 3 + 1)
                    for m in range(3):
                        dst = slot(m) if m < 2 else slot(m, KF, D)
                        sp.dma_start(dst, expert_w[m][bass.ds(e, 1)].rearrange("e (k p) n -> p (e k) n", p=P)) \
                            .then_inc(sem("over_in"), 16)
                sp.wait_ge(sem("over_done"), 3 * EXPERTS + 1)
            for i in range(CHUNKS_A, len(chunks)):
                n = i - CHUNKS_A
                s = chunks[i][1]
                if n >= RING_C:
                    filled(sp, chunks[i - RING_C][3])
                elif s == RING_C - 1:
                    sp.wait_ge(gu_full, LOOPS * BODY)
                elif s < 3 * PEELED:
                    e = LOOPS * BODY + s // 3
                    sp.wait_ge(gu_full if s % 3 < 2 else y_full, e + 1)
                load(i)
            for t in range(NT):
                sp.wait_ge(sem(f"out_ready{t}"), 2)
                sp.dma_start(out[0, t * P:(t + 1) * P, :], out_tok[:, t, :]).then_inc(sem("out_done"), 16)
            sp.wait_ge(sem("out_done"), 16 * NT)

        @block.gpsimd
        def _(pool):
            pool.wait_ge(sem("consts_in"), 16)
            moved(pool, "par")
            made = 0
            for j in range(KD):
                for w in range(PE_TAPS):
                    if made >= DIAGS:
                        pool.wait_ge(sem("diag_used"), made - DIAGS + 1)
                    pool.tensor_scalar(diag[:, made % DIAGS, :], ident, col("dw", w * KD + j), 0.0,
                                       ALU.mult, ALU.add).then_inc(sem("diag_ready"), 1)
                    made += 1

            pool.wait_ge(sem("h2_ready"), KD)
            pool.memset(xg[:, :, SLOTS_A:PADDED], 0.0).then_inc(sem("pad_ready"), 1)
            for j in range(KD):
                moved(pool, ("gather", j))
            pool.memset(y_e, 0.0).then_inc(sem("zeros_ready"), 1)
            pool.wait_ge(sem("pad_ready"), 1)
            pool.wait_ge(sem("table_ready"), 1)

            def window(e, r, b, ready):
                place = e if r == 0 else e + (4 + EXPERTS * r)
                ranks = small[:, P * r:P * (r + 1)].rearrange("p (q e) -> p q e", q=2 * NT)
                pool.tensor_copy(own[:, b, :].unsqueeze(2), ranks[:, :, bass.ds(e, 1)]).then_inc(sem("own_ready"), 1)
                pool.wait_ge(sem("own_ready"), e + 1 if r == 0 else e * 3 + (EXPERTS + r))
                at = pool.value_load(table[0:1, bass.ds(place, 1)], min_val=0, max_val=SLOTS_A)
                pool.tensor_copy(xw[b], xg[:, :, bass.ds(at, WIN)])
                for t in range(NT):
                    ins = pool.tensor_scalar(weighted[b][:, t, :], rc[:, R_IOTA2:R_IOTA2 + P], own[:, b, t:t + 1],
                                             own[:, b, NT + t:NT + t + 1], ALU.is_equal, ALU.mult)
                ins.then_inc(ready, 1)

            with pool.Fori(0, LOOPS) as it:
                for b in range(BODY):
                    pool.wait_ge(t_full, it * BODY + (b + 1))
                    window(it * BODY + b, 0, b, win_ready)
            for b in range(PEELED):
                pool.wait_ge(t_full, LOOPS * BODY + b + 1)
                window(LOOPS * BODY + b, 0, b, win_ready)
            pool.sem_inc(sem("over_done"), 1)
            with pool.If(overflow(pool)):
                pool.wait_ge(sem("combined"), 1)
                with pool.Fori(0, EXPERTS) as e:
                    for r in range(1, 4):
                        pool.wait_ge(sem("over_done"), e * 3 + r)
                        window(e, r, 0, sem("over_window"))

            pool.wait_ge(sem("krope_ready"), 1)
            src = raw[NOPE:QK, 3, 0:T].unsqueeze(1).broadcast_to((ROPE, HEADS, T))
            pool.tensor_copy(kh[NOPE:QK, :, :], src).then_inc(sem("krope_spread"), 1)
            cosA = ac[NOPE:QK, A_COS:A_COS + T].unsqueeze(1).broadcast_to((ROPE, 2, T))
            for p in range(HEADS // 2):
                pool.wait_ge(sem("q_shuffled"), p + 1)
                pool.tensor_tensor(qh[NOPE:QK, 2 * p:2 * p + 2, :], qh[NOPE:QK, 2 * p:2 * p + 2, :], cosA,
                                   ALU.mult).then_inc(sem("q_cos"), 1)

            def scale_probs(n):
                pool.wait_ge(sem("sum_inverse"), n + 1)
                b = n % 4
                pool.tensor_scalar(prob[:, b, 0:P], prob[:, b, 0:P], srec[:, b, 0:1], 0.0, ALU.mult, ALU.add)
                pool.tensor_scalar(prob[:, b, P:3 * P], prob[:, b, P:3 * P], srec[:, b, 1:2], 0.0,
                                   ALU.mult, ALU.add).then_inc(sem("probs_ready"), 1)

            for i in range(HEADS):
                scale_probs(i)
            for n in range(2):
                for j in range(KD):
                    moved(pool, ("raw", n, j))
                    filled(pool, ("rot", n, j))
                    pool.tensor_tensor(raw_b[:, j, :], raw_b[:, j, :], bc[:, B_COS:B_COS + T], ALU.mult) \
                        .then_inc(sem("raw_cos"), 1)
            for i in range(HEADS):
                scale_probs(HEADS + i)

        @block.scalar
        def _(act):
            def rows_of(name):
                a = A[name]
                n = len(a.shape)
                flat = a if n == 1 else a.rearrange("a b -> (a b)")
                return flat.rearrange("(r n) -> r n", n=P)

            act.dma_start(consts[:, :], A["k_base"]).then_inc(sem("consts_in"), 16)
            for lot, names in ((0, LOT0), (1, LOT1)):
                at = 0
                for name, n in names:
                    act.dma_start(rows[at:at + n, lot, :], rows_of(name)).then_inc(sem("rows_in"), 16)
                    at += n
            dwr = A["conv_w_dw"][0].rearrange("w (k n) -> (w k) n", n=P)
            for half in range(2):
                act.dma_start(rows[0:DW_ROWS, 2 + half, :], dwr[half * DW_ROWS:(half + 1) * DW_ROWS, :]) \
                    .then_inc(sem("rows_in"), 16)
            act.dma_start(brow[:, 0:GROUPS], A["moe_b_rg"]).then_inc(sem("router_in"), 16)
            act.dma_start(brow[:, GROUPS:GROUPS + EXPERTS], A["moe_b_re"]).then_inc(sem("router_in"), 16)

            def norm_std(name, n, eps):
                bank = filled(act, name)
                to = std if name in ("ms1", "var1", "ms2") else std2
                act.activation(to, bank[:, 0:T], ACT.Sqrt, bias=eps, scale=1.0 / n).then_inc(read(name), 1)

            for j in range(KD):
                moved(act, ("x", j))
                act.activation(sq[:, j, :], xT[:, j, :], ACT.Square).then_inc(sem("squared0"), 1)
            moved(act, "par")
            act.activation(cact[:, :, :], par[:, COL["c"]:COL["c"] + 8].unsqueeze(2).broadcast_to((P, KD, 32)),
                           ACT.Silu).then_inc(sem("c_ready"), 1)
            act.wait_ge(sem("eps_ready"), 2)
            norm_std("ms1", D, eps6)
            moved(act, ("mod", 0))
            for j in range(KD):
                act.wait_ge(sem("h_scaled"), j + 1)
                act.activation(h[:, j, :], h[:, j, :], ACT.Identity, bias=mod[:, j:j + 1]) \
                    .then_inc(sem("h_ready"), 1)
            for j in range(KD):
                bank = filled(act, ("glu_g", j))
                if j >= 4:
                    moved(act, ("glu_a", j - 4))
                act.activation(sg[:, j % 4, :], bank[:, 0:T], ACT.Sigmoid, bias=col("conv_b_in", KD + j)) \
                    .then_inc(read(("glu_g", j)), 1)
            for j in range(KD):
                act.wait_ge(sem("conv_done"), j + 1)
                bank = ps[use[("conv", j)][0]]
                act.activation(y[:, j, :], bank[:, 0:T], ACT.Identity, bias=col("conv_b_dw", j)) \
                    .then_inc(read(("conv", j)), 1)
            for j in range(KD):
                act.wait_ge(sem("centred1"), j + 1)
                act.activation(sq[:, j, :], y[:, j, :], ACT.Square).then_inc(sem("squared1"), 1)
            norm_std("var1", D, eps6)
            for j in range(KD):
                act.wait_ge(sem("normed1"), j + 1)
                act.activation(h[:, j, :], y[:, j, :], ACT.Silu, bias=col("conv_ln_b", j)) \
                    .then_inc(sem("act_ready"), 1)
            for j in range(KD):
                moved(act, ("proj1", j))
                act.activation(sq[:, j, :], xT[:, j, :], ACT.Square).then_inc(sem("squared2"), 1)
                if j == 0:
                    act.dma_start(rc, A["k_route"]).then_inc(sem("route_in"), 16)
                    act.dma_start(wr[:, :, 0:GROUPS], cols(A["moe_w_rg"][0], 0, GROUPS)) \
                        .then_inc(sem("router_in"), 16)
                    act.dma_start(wr[:, :, GROUPS:36], cols(A["moe_w_re"][0], 0, EXPERTS)) \
                        .then_inc(sem("router_in"), 16)
            norm_std("ms2", D, eps6)
            for j in range(KD):
                act.wait_ge(sem("h2_scaled"), j + 1)
                act.activation(h2[:, j, :], scaled[:, j, :], ACT.Identity, bias=mod[:, 24 + j:25 + j]) \
                    .then_inc(sem("h2_ready"), 1)
            for t in range(NT):
                for half in range(2):
                    name = ("h2tok", t, half)
                    bank = filled(act, name)
                    act.activation(h2_tok[:, t, half * 512:(half + 1) * 512], bank[:, :], ACT.Copy) \
                        .then_inc(read(name), 1)
            act.wait_ge(sem("group_shifted"), 1)
            act.activation(small[:, 80:88], small[:, 80:88], ACT.Exp).then_inc(sem("group_exp"), 1)
            act.wait_ge(sem("pair_shifted"), 1)
            act.activation(small[:, 88:90], small[:, 88:90], ACT.Exp).then_inc(sem("pair_exp"), 1)
            for j in range(0, KD, 2):
                bank = filled(act, ("gather", j))
                act.activation(xg[:, j, 0:SLOTS_A], bank[:, :], ACT.Copy).then_inc(read(("gather", j)), 1)

            def silu(full_sem, n, done):
                act.wait_ge(full_sem, n)
                act.activation(silu_g, GU_BANK[WIN:2 * WIN, :], ACT.Silu).then_inc(done, 1)

            def move_turned(full_sem, n, b, done):
                act.wait_ge(full_sem, n)
                act.activation(turned_e[b], T_BANK[:, :], ACT.Copy).then_inc(done, 1)

            silu(gu_full, 1, silu_done)
            with act.Fori(0, LOOPS) as it:
                for b in range(BODY):
                    silu(gu_full, it * BODY + (b + 2), silu_done)
                    move_turned(t_full, it * BODY + (C_T + b + 1), b, t_moved)
            for e in range(LOOPS * BODY + 1, EXPERTS + 1):
                if e < EXPERTS:
                    silu(gu_full, e + 1, silu_done)
                move_turned(t_full, C_T + e, (e - 1) % BODY, t_moved)
            act.wait_ge(sem("combined"), 1)
            with act.If(overflow(act)):
                with act.Fori(0, 3 * EXPERTS) as n:
                    silu(sem("over_gate_up"), n + 1, sem("over_silu"))
                    move_turned(sem("over_turned"), n + 1, 0, sem("over_turned_moved"))
                act.wait_ge(sem("over_done"), 3 * EXPERTS + 1)
            act.dma_start(ac, A["k_mla"]).then_inc(sem("mla_in"), 16)
            act.dma_start(wrope, cols(mw, D, ROPE)).then_inc(sem("wrope_in"), 16)
            for j in range(KD):
                moved(act, ("acc", j // 2))
                act.activation(sq2[:, j, :], xT[:, j, :], ACT.Square).then_inc(sem("squared3"), 1)
            norm_std("ms3", D, eps6)
            for j in range(KQ + KKV):
                moved(act, ("cq", j))
                act.activation(sq2[:, j, :], cq[:, j, :], ACT.Square).then_inc(sem("squared5"), 1)
            norm_std("msq", KQ * P, eps6)
            act.wait_ge(sem("rstd_ready"), 5)
            norm_std("mskv", KKV * P, eps6)
            bank = filled(act, "krope")
            act.activation(raw[NOPE:QK, 3, 0:T], bank[NOPE:QK, 0:T], ACT.Copy).then_inc(read("krope"), 1)
            for j in range(KD):
                name = ("gate1", j)
                bank = filled(act, name)
                act.activation(gate[:, j, :], bank[:, 0:T], ACT.Silu).then_inc(read(name), 1)
            for t in range(NT):
                name = ("v1", t, 0)
                bank = filled(act, name)
                act.activation(v[:, t, 0:512], bank[:, :], ACT.Copy).then_inc(read(name), 1)
            for p in range(HEADS // 2):
                if p % 2:
                    continue
                name = ("kn", p)
                bank = filled(act, name)
                act.activation(kh[0:NOPE, 2 * p:2 * p + 2, :], bank[0:NOPE, :].rearrange("p (h n) -> p h n", h=2),
                               ACT.Copy).then_inc(read(name), 1)
            for p in range(HEADS // 2):
                name = ("q", p)
                bank = filled(act, name)
                act.activation(qh[0:QK, 2 * p:2 * p + 2, :], bank[0:QK, :].rearrange("p (h n) -> p h n", h=2),
                               ACT.Copy).then_inc(read(name), 1)

            def attention(layer):
                for i in range(HEADS + 2):
                    if i < HEADS:
                        b = i % 4
                        moved(act, ("s", layer, i))
                        act.activation(prob[:, b, 0:P], prob[:, b, 0:P], ACT.Exp, bias=smin[:, b, 0:1],
                                       scale=-1.0, accum_out=ssum[:, b, 0:1]).then_inc(sem("exp_done"), 1)
                        act.activation(prob[:, b, P:3 * P], prob[:, b, P:3 * P], ACT.Exp, bias=smin[:, b, 1:2],
                                       scale=-1.0, accum_out=ssum[:, b, 1:2]).then_inc(sem("exp_done"), 1)
                    if i >= 2:
                        n = i - 2
                        name = ("pt", layer, n)
                        bank = filled(act, name)
                        if n >= 4:
                            filled(act, ("o", layer, (n - 4) // 2))
                        act.activation(prob_t[:, n % 4, :], bank[:, 0:3 * P], ACT.Copy).then_inc(read(name), 1)

            def out_norm(layer):
                for j in range(KD):
                    act.wait_ge(sem("centred2"), KD * layer + j + 1)
                    act.activation(sq2[:, j, :], xT[:, j, :], ACT.Square).then_inc(sem("squared4"), 1)
                norm_std(("var2", layer), D, eps5)
                for j in range(KD):
                    act.wait_ge(sem("normed2"), KD * layer + j + 1)
                    to = final if layer else xT
                    act.activation(to[:, j, :], xT[:, j, :], ACT.Identity, bias=col("ln_b_2", KD * layer + j)) \
                        .then_inc(sem("layer_ready"), 1)

            attention(0)
            out_norm(0)
            act.dma_start(bc, A["k_moba"]).then_inc(sem("moba_in"), 16)
            for n in range(2):
                for j in range(KD):
                    name = ("raw", n, j)
                    bank = filled(act, name)
                    if n:
                        act.wait_ge(sem("turned"), j + 1)
                    act.activation(raw_b[:, j, :], bank[:, 0:T], ACT.Copy).then_inc(read(name), 1)
                for w in range(KD if n else 4):
                    name = ("gate2", w) if n else ("v2", w // 2, w % 2)
                    bank = filled(act, name)
                    if n:
                        act.activation(gate[:, w, :], bank[:, 0:T], ACT.Silu).then_inc(read(name), 1)
                    else:
                        act.activation(v[:, w // 2, (w % 2) * 512:(w % 2 + 1) * 512], bank[:, :], ACT.Copy) \
                            .then_inc(read(name), 1)
            attention(1)
            out_norm(1)
            for t in range(NT):
                name = ("out", t, 1)
                bank = filled(act, name)
                act.activation(out_tok[:, t, 512:D], bank[:, :], ACT.Copy).then_inc(sem(f"out_ready{t}"), 1)

        @block.tensor
        def _(pe):
            pe.sem_inc(t_full, C_T)
            pe.wait_ge(sem("consts_in"), 16)
            pe.wait_ge(sem("x_in"), 16)
            for j in range(KD):
                bank = may_fill(pe, ("x", j))
                for t in range(NT):
                    mm = pe.transpose(bank[:, t * P:(t + 1) * P], x_tok[:, t, j * P:(j + 1) * P], ident)
                mm.then_inc(full(("x", j)), 1)
            pe.wait_ge(sem("rows_in"), 16 * (len(LOT0) + len(LOT1) + 2))
            bank = may_fill(pe, "par")
            for lot, n, at in ((0, LOT0_ROWS, 0), (1, LOT1_ROWS, LOT0_ROWS), (2, DW_ROWS, COL["dw"]),
                               (3, DW_ROWS, COL["dw"] + DW_ROWS)):
                mm = pe.transpose(bank[:, at:at + n], rows[0:n, lot, :], ident[0:n, 0:n])
            mm.then_inc(full("par"), 1)

            def total(name, src, tiles, ready):
                bank = may_fill(pe, name)
                for k in range(tiles):
                    ready(k)
                    mm = pe.matmul(bank[:, 0:T], ones, src[:, k, :], start=(k == 0), stop=(k == tiles - 1))
                mm.then_inc(full(name), 1)

            def project(name, w, lo, m, rhs, k0=0, n=T, at=0, part=0, tiles=KD, done=True, ready=None):
                bank = ps[use[name][0]]
                for k in range(tiles):
                    if ready:
                        ready(k)
                    mm = pe.matmul(bank[part:part + m, at:at + n], w[:, k, lo:lo + m], rhs[:, k0 + k, :],
                                   start=(k == 0), stop=(k == tiles - 1))
                if done:
                    mm.then_inc(full(name), 1)

            total("ms1", sq, KD, lambda k: pe.wait_ge(sem("squared0"), k + 1))

            def ada(g):
                pe.wait_ge(sem("c_ready"), 1)
                bank = may_fill(pe, ("ada", g))
                for i in range(4):
                    w = slot(arrived(pe, ("ada", 4 * g + i)))
                    for k in range(KD):
                        for c in range(4):
                            mm = pe.matmul(bank[32 * c:32 * c + 32, i * P:(i + 1) * P], cact[:, k, :],
                                           w[:, k, c * P:(c + 1) * P], start=(k == 0), stop=(k == KD - 1),
                                           skip_group_check=True)
                mm.then_inc(full(("ada", g)), 1)

            def ada_columns(g):
                bank = may_fill(pe, ("mod", g))
                moved(pe, ("ada", g))
                for i in range(4):
                    mm = pe.transpose(bank[:, i * P:(i + 1) * P], ada_rows[:, i * P:(i + 1) * P], ident)
                mm.then_inc(full(("mod", g)), 1)

            ada(0)
            ada_columns(0)
            for n in range(4):
                w = slot(arrived(pe, ("glu", n)))
                for jj in range(2):
                    j = 2 * n + jj
                    may_fill(pe, ("glu_a", j))
                    project(("glu_a", j), w, jj * P, P, h,
                            ready=(lambda k: pe.wait_ge(sem("h_ready"), k + 1)) if j == 0 else None)
                    may_fill(pe, ("glu_g", j))
                    project(("glu_g", j), w, 256 + jj * P, P, h)
            made = 0
            for j in range(KD):
                name = ("conv", j)
                bank = may_fill(pe, name)
                pe.wait_ge(sem("u_edge"), 1)
                moved(pe, ("glu_a", j))
                for w in range(PE_TAPS):
                    pe.wait_ge(sem("diag_ready"), made + 1)
                    mm = pe.matmul(bank[:, 0:T], diag[:, made % DIAGS, :], u[:, j, w:w + T],
                                   start=(w == 0), stop=(w == PE_TAPS - 1))
                    mm.then_inc(sem("diag_used"), 1)
                    made += 1
            for g in (1, 2):
                ada(g)
                ada_columns(g)
            total("mean1", y, KD, lambda k: moved(pe, ("conv", k)))
            total("var1", sq, KD, lambda k: pe.wait_ge(sem("squared1"), k + 1))
            for n in range(2):
                w = slot(arrived(pe, ("proj1", n)))
                for j in range(4 * n, 4 * n + 4):
                    may_fill(pe, ("proj1", j))
                    project(("proj1", j), w, (j % 4) * P, P, h,
                            ready=(lambda k: pe.wait_ge(sem("act_ready"), k + 1)) if j == 0 else None)
            total("ms2", sq, KD, lambda k: pe.wait_ge(sem("squared2"), k + 1))

            pe.wait_ge(sem("router_in"), 64)
            bank = may_fill(pe, "logit")
            for t in range(NT):
                for k in range(KD):
                    pe.wait_ge(sem("h2_ready"), k + 1)
                    pe.matmul(bank[:, t * 64:t * 64 + 36], h2[:, k, t * P:(t + 1) * P], wr[:, k, :],
                              start=(k == 0), stop=False)
                mm = pe.matmul(bank[:, t * 64:t * 64 + 36], ones[0:1, :], brow[0:1, :], start=False, stop=True)
            mm.then_inc(full("logit"), 1)
            for t in range(NT):
                for half in range(2):
                    name = ("h2tok", t, half)
                    bank = may_fill(pe, name)
                    for j in range(4):
                        mm = pe.transpose(bank[:, j * P:(j + 1) * P], h2[:, 4 * half + j, t * P:(t + 1) * P], ident)
                    mm.then_inc(full(name), 1)
            pe.wait_ge(sem("chosen"), 1)
            pe.wait_ge(sem("route_in"), 16)
            bank = may_fill(pe, "rank")
            strict = rc[:, R_STRICT:R_STRICT + P]
            picked = small[:, 384:448].rearrange("p (t e) -> p t e", t=NT)
            pe.matmul(bank[:, 0:32], strict, picked[:, 0, :], start=True, stop=True)
            pe.matmul(bank[:, 32:64], ones, picked[:, 0, :], start=True, stop=False)
            pe.matmul(bank[:, 32:64], strict, picked[:, 1, :], start=False, stop=True)
            pe.matmul(bank[:, 64:96], ones, picked[:, 0, :], start=True, stop=False)
            pe.matmul(bank[:, 64:96], ones, picked[:, 1, :], start=False, stop=True).then_inc(full("rank"), 1)
            for j in range(KD):
                name = ("gather", j)
                bank = may_fill(pe, name)
                for t in range(NT):
                    pe.wait_ge(sem("sel_ready"), t + 1)
                    moved(pe, ("h2tok", t, j // 4))
                    mm = pe.matmul(bank[:, :], h2_tok[:, t, j * P:(j + 1) * P], sel[:, t, :],
                                   start=(t == 0), stop=(t == NT - 1))
                mm.then_inc(full(name), 1)
            for b in range(8):
                if BEFORE_EXPERTS[b]:
                    pe.wait_ge(sem(f"bank{b}_read"), BEFORE_EXPERTS[b])

            pe.wait_ge(sem("zeros_ready"), 1)
            for bank in ACC:
                pe.matmul(bank[:, :], ones[0:1, :], y_e[0:1, :], start=True, stop=False, skip_group_check=True)

            def gate_up(b, wu, wg):
                for k in range(KD):
                    for half, w in ((0, wu), (1, wg)):
                        mm = pe.matmul(GU_BANK[half * WIN:(half + 1) * WIN, :], xw[b][:, k, :], w[:, k, :],
                                       start=(k == 0), stop=(k == KD - 1), skip_group_check=True)
                return mm

            def turn(b):
                for t in range(NT):
                    lo = KF * WIN + t * P
                    pe.transpose(T_BANK[:, lo:lo + P], weighted[b][:, t, :], ident)
                for f in range(KF):
                    mm = pe.transpose(T_BANK[:, f * WIN:(f + 1) * WIN], hid[:, f * P:(f + 1) * P],
                                      ident[0:WIN, 0:WIN])
                return mm

            def down(b, w):
                for f in range(KF):
                    for half in range(2):
                        mm = pe.matmul(Y_BANK[half * WIN:(half + 1) * WIN, :], hid_t[b][:, f, :],
                                       w[:, f, half * 512:(half + 1) * 512], start=(f == 0), stop=(f == KF - 1),
                                       skip_group_check=True)
                return mm

            def combine(b):
                for j in range(4):
                    for half in range(2):
                        rows_ = slice(half * WIN, (half + 1) * WIN)
                        mm = pe.matmul(ACC[2 * half + j // 2][:, (j % 2) * T:(j % 2 + 1) * T],
                                       y_e[rows_, j * P:(j + 1) * P], comb[b][rows_, :],
                                       start=False, stop=False, skip_group_check=True)
                return mm

            def step(e, b, uses, first=0):
                b1, b2 = (b - 1) % BODY, (b - 2) % BODY
                if uses:
                    pe.wait_ge(win_ready, e + 1)
                    pe.wait_ge(sem(f"slot{3 * b}"), uses(3 * b, 0))
                    pe.wait_ge(sem(f"slot{3 * b + 1}"), uses(3 * b + 1, 0))
                    if first != 1:
                        pe.wait_ge(hid_ready, e)
                    gate_up(b, slot(3 * b + 1), slot(3 * b)).then_inc(gu_full, 1)
                if first == 1:
                    return
                pe.wait_ge(hid_ready, e)
                turn(b1).then_inc(t_full, 1)
                if first != 2:
                    pe.wait_ge(y_moved, e - 1)
                    combine(b2)
                pe.wait_ge(sem(f"slot{3 * b1 + 2}"), (uses or last_uses)(3 * b1 + 2, -1 if b == 0 else 0))
                pe.wait_ge(t_moved, e)
                down(b1, slot(3 * b1 + 2, KF, D)).then_inc(y_full, 1)

            def last_uses(s, back):
                return (LOOPS + 1 + back) * 16 + EXPERT_BASE[s]

            for e in range(BODY):
                step(e, e, lambda s, back: EXPERT_BASE[s] + 16, first=e + 1)
            with pe.Fori(1, LOOPS) as it:
                for b in range(BODY):
                    step(it * BODY + b, b, lambda s, back: it * 16 + (EXPERT_BASE[s] + 16 + 16 * back))
            for b in range(PEELED):
                step(LOOPS * BODY + b, b, last_uses)
            step(EXPERTS, EXPERTS % BODY, None)
            pe.wait_ge(y_moved, EXPERTS)
            combine((EXPERTS - 1) % BODY).then_inc(sem("combined"), 1)
            with pe.If(overflow(pe)):
                with pe.Fori(0, EXPERTS) as e:
                    pe.wait_ge(sem("over_in"), e * 48 + 48)
                    for r in range(3):
                        n = e * 3 + (r + 1)
                        pe.wait_ge(sem("over_window"), n)
                        gate_up(0, slot(1), slot(0)).then_inc(sem("over_gate_up"), 1)
                        pe.wait_ge(sem("over_hidden"), n)
                        turn(0).then_inc(sem("over_turned"), 1)
                        pe.wait_ge(sem("over_turned_moved"), n)
                        down(0, slot(2, KF, D)).then_inc(sem("over_down"), 1)
                        pe.wait_ge(sem("over_down_moved"), n)
                        combine(0).then_inc(sem("over_done"), 1)

            total("ms3", sq2, KD, lambda k: pe.wait_ge(sem("squared3"), k + 1))
            for n in range(2):
                w = slot(arrived(pe, ("cq", n)))
                for j in range(4 * n, 4 * n + 4):
                    may_fill(pe, ("cq", j))
                    project(("cq", j), w, (j % 4) * P, P, xT,
                            ready=(lambda k: pe.wait_ge(sem("x_normed"), k + 1)) if j == 0 else None)
            total("msq", sq2, KQ, lambda k: pe.wait_ge(sem("squared5"), k + 1))
            bank = may_fill(pe, "mskv")
            for k in range(KKV):
                pe.wait_ge(sem("squared5"), KQ + k + 1)
                mm = pe.matmul(bank[:, 0:T], ones, sq2[:, KQ + k, :], start=(k == 0), stop=(k == KKV - 1))
            mm.then_inc(full("mskv"), 1)
            pe.wait_ge(sem("wrope_in"), 16)
            may_fill(pe, "krope")
            project("krope", wrope, 0, ROPE, xT, part=NOPE)
            for n in range(2):
                w = slot(arrived(pe, ("gate1", n)))
                for j in range(4 * n, 4 * n + 4):
                    may_fill(pe, ("gate1", j))
                    project(("gate1", j), w, (j % 4) * P, P, xT)
            w = slot(arrived(pe, "ukv"), KKV, 2048)
            wv = w.rearrange("p k (h c) -> p k h c", c=P)
            for t in range(NT):
                for n in range(2):
                    name = ("v1", t, n)
                    bank = may_fill(pe, name)
                    for k in range(KKV):
                        pe.wait_ge(sem("latent_ready"), KQ + k + 1)
                        mm = pe.matmul(bank[:, :].rearrange("p (h c) -> p h c", c=HD), cq[:, KQ + k, t * P:(t + 1) * P], wv[:, k, 8 * n:8 * n + 8, NOPE:P],
                                       start=(k == 0), stop=(k == KKV - 1))
                    mm.then_inc(full(name), 1)
            for p in range(HEADS // 2):
                name = ("kn", p)
                may_fill(pe, name)
                for half in range(2):
                    project(name, w, (2 * p + half) * P, NOPE, cq, k0=KQ, at=half * T, tiles=KKV, done=half == 1)
            for n in range(4):
                w = slot(arrived(pe, ("uq", n)), KQ, 384)
                for p in (2 * n, 2 * n + 1):
                    name = ("q", p)
                    may_fill(pe, name)
                    for half in range(2):
                        project(name, w, ((2 * p + half) % 4) * QK, QK, cq, at=half * T, tiles=KQ, done=half == 1)

            def attention(layer, q_of, k_of, ready):
                for i in range(HEADS + 3):
                    if i < HEADS:
                        ready(i)
                        name = ("s", layer, i)
                        bank = may_fill(pe, name)
                        q, k = q_of(i), k_of(i)
                        pe.matmul(bank[:, 0:P], q[:, 0:P], k[:, 0:P], start=True, stop=True)
                        pe.matmul(bank[:, P:3 * P], q[:, P:T], k[:, 0:T], start=True, stop=True) \
                            .then_inc(full(name), 1)
                    if 0 <= i - 2 < HEADS:
                        n = i - 2
                        name = ("pt", layer, n)
                        bank = may_fill(pe, name)
                        pe.wait_ge(sem("probs_ready"), HEADS * layer + n + 1)
                        for c in range(3):
                            mm = pe.transpose(bank[:, c * P:(c + 1) * P], prob[:, n % 4, c * P:(c + 1) * P], ident)
                        mm.then_inc(full(name), 1)
                    if i >= 3:
                        n = i - 3
                        name = ("o", layer, n // 2)
                        at = HD * (n % 2)
                        bank = may_fill(pe, name) if n % 2 == 0 else ps[use[name][0]]
                        moved(pe, ("pt", layer, n))
                        pe.matmul(bank[at:at + HD, 0:T], v[:, 0, n * HD:(n + 1) * HD], prob_t[:, n % 4, 0:T],
                                  start=True, stop=False, skip_group_check=True)
                        mm = pe.matmul(bank[at:at + HD, P:T], v[:, 1, n * HD:(n + 1) * HD],
                                       prob_t[:, n % 4, T:3 * P], start=False, stop=True, skip_group_check=True)
                        if n % 2:
                            mm.then_inc(full(name), 1)

            def out_layer(layer):
                for n in range(2):
                    w = slot(arrived(pe, ("wo", layer, n)))
                    for j in range(4 * n, 4 * n + 4):
                        may_fill(pe, ("proj2", layer, j))
                        project(("proj2", layer, j), w, (j % 4) * P, P, o,
                                ready=(lambda k: moved(pe, ("o", layer, k))) if j == 0 else None)
                total(("mean2", layer), xT, KD, lambda k: moved(pe, ("proj2", layer, k)))
                total(("var2", layer), sq2, KD, lambda k: pe.wait_ge(sem("squared4"), KD * layer + k + 1))

            def ready_a(i):
                if i == 0:
                    pe.wait_ge(sem("krope_spread"), 1)
                    for p in range(HEADS // 2 - 4, HEADS // 2):
                        moved(pe, ("kn", p))
                    pe.wait_ge(sem("mla_in"), 16)
                    for t in range(NT):
                        for n in range(2):
                            moved(pe, ("v1", t, n))
                pe.wait_ge(sem("q_ready"), i // 2 + 1)

            attention(0, lambda i: qh[0:QK, i, :], lambda i: kh[0:QK, i, :], ready_a)
            out_layer(0)

            def rotate(n, j):
                name = ("rot", n, j)
                bank = may_fill(pe, name)
                moved(pe, ("raw", n, j))
                pe.matmul(bank[:, 0:T], bc[:, B_ROT:B_ROT + P], raw_b[:, j, :], start=True, stop=True) \
                    .then_inc(full(name), 1)

            for n, kind in enumerate(("kv", "in")):
                for j in range(KD):
                    if j % 4 == 0:
                        w = slot(arrived(pe, (kind, j // 4)))
                    may_fill(pe, ("raw", n, j))
                    project(("raw", n, j), w, (j % 4) * P, P, xT,
                            ready=(lambda k: pe.wait_ge(sem("layer_ready"), k + 1)) if n == j == 0 else None)
                    if j == 1 and n == 0:
                        pe.wait_ge(sem("moba_in"), 16)
                    if j:
                        rotate(n, j - 1)
                rotate(n, KD - 1)
                if n == 0:
                    ws = [slot(arrived(pe, (kind, 2))), slot(arrived(pe, (kind, 3)))]
                    for t in range(NT):
                        for half in range(2):
                            name = ("v2", t, half)
                            bank = may_fill(pe, name)
                            for k in range(KD):
                                mm = pe.matmul(bank[:, :], xT[:, k, t * P:(t + 1) * P], ws[half][:, k, :],
                                               start=(k == 0), stop=(k == KD - 1))
                            mm.then_inc(full(name), 1)
                else:
                    for j in range(KD):
                        if j % 4 == 0:
                            w = slot(arrived(pe, (kind, 2 + j // 4)))
                        may_fill(pe, ("gate2", j))
                        project(("gate2", j), w, (j % 4) * P, P, xT)

            def ready_b(i):
                if i == 0:
                    for t in range(NT):
                        for n in range(2):
                            moved(pe, ("v2", t, n))
                pe.wait_ge(sem("turned"), KD + i // 2 + 1)

            attention(1, lambda i: qb[HD * (i % 2):HD * (i % 2) + HD, i // 2, :],
                      lambda i: kb[HD * (i % 2):HD * (i % 2) + HD, i // 2, :], ready_b)
            out_layer(1)
            for t in range(NT):
                for half in range(2):
                    name = ("out", t, half)
                    bank = may_fill(pe, name)
                    for j in range(4):
                        pe.wait_ge(sem("layer_ready"), KD + 4 * half + j + 1)
                        mm = pe.transpose(bank[:, j * P:(j + 1) * P], final[:, 4 * half + j, t * P:(t + 1) * P], ident)
                    mm.then_inc(full(name), 1)

        @block.vector
        def _(dve):
            steps = [0]

            def then(ins):
                steps[0] += 1
                ins.then_inc(sem("vector_step"), 1)
                dve.wait_ge(sem("vector_step"), steps[0])

            rstd_count = [0]

            def inverse(name, parked):
                moved(dve, name)
                dve.reciprocal(parked, std if name in ("ms1", "var1", "ms2") else std2) \
                    .then_inc(sem("rstd_ready"), 1)
                rstd_count[0] += 1
                dve.wait_ge(sem("rstd_ready"), rstd_count[0])
                return parked

            def rstd_of(name):
                return inverse(name, ps[use[name][0]][:, T:2 * T])

            dve.memset(eps6, EPS).then_inc(sem("eps_ready"), 1)
            dve.memset(eps5, LN_EPS).then_inc(sem("eps_ready"), 1)
            for j in range(KD):
                bank = filled(dve, ("x", j))
                dve.tensor_copy(xT[:, j, :], bank[:, 0:T]).then_inc(read(("x", j)), 1)
            bank = filled(dve, "par")
            dve.tensor_copy(par[:, :], bank[:, 0:PAR]).then_inc(read("par"), 1)
            rstd = rstd_of("ms1")
            dve.memset(u[:, :, 0:TAPS - 1], 0.0).then_inc(sem("u_edge"), 1)
            moved(dve, "par")

            def modulation(g):
                bank = filled(dve, ("ada", g))
                dve.tensor_copy(ada_rows, bank[:, :]).then_inc(read(("ada", g)), 1)
                bank = filled(dve, ("mod", g))
                dve.tensor_tensor(mod[:, 16 * g:16 * g + 16].rearrange("p (i c) -> p i c", i=4),
                                  bank[:, :].rearrange("p (i c n) -> p i c n", i=4, c=4)[:, :, :, 0],
                                  par[:, 16 * g:16 * g + 16].rearrange("p (i c) -> p i c", i=4),
                                  ALU.add).then_inc(read(("mod", g)), 1)
                moved(dve, ("mod", g))

            modulation(0)
            then(dve.scalar_tensor_tensor(out=a1, in0=mod[:, 8:16], scalar=1.0,
                                          in1=par[:, COL["norm_mix_g"]:COL["norm_mix_g"] + 8],
                                          op0=ALU.add, op1=ALU.mult))
            for j in range(KD):
                moved(dve, ("x", j))
                dve.scalar_tensor_tensor(out=h[:, j, :], in0=xT[:, j, :], scalar=a1[:, j:j + 1], in1=rstd,
                                         op0=ALU.mult, op1=ALU.mult).then_inc(sem("h_scaled"), 1)
            for j in range(KD):
                bank = filled(dve, ("glu_a", j))
                moved(dve, ("glu_g", j))
                dve.scalar_tensor_tensor(out=u[:, j, TAPS - 1:], in0=bank[:, 0:T], scalar=col("conv_b_in", j),
                                         in1=sg[:, j % 4, :], op0=ALU.add, op1=ALU.mult) \
                    .then_inc(read(("glu_a", j)), 1)
            dve.wait_ge(sem("u_edge"), 1)
            taps = TAPS - PE_TAPS
            for j in range(0, KD, 2):
                for w in range(taps):
                    for c in range(2):
                        name = ("conv", j + c)
                        bank = ps[use[name][0]]
                        if w == 0:
                            moved(dve, ("glu_a", j + c))
                            dve.wait_ge(sem("diag_used"), PE_TAPS * (j + c + 1))
                        else:
                            dve.wait_ge(sem("tap_done"), (j // 2) * 2 * (taps - 1) + 2 * (w - 1) + c + 1)
                        done = sem("conv_done") if w == taps - 1 else sem("tap_done")
                        dve.scalar_tensor_tensor(out=bank[:, 0:T], in0=u[:, j + c, PE_TAPS + w:PE_TAPS + w + T],
                                                 scalar=col("dw", (PE_TAPS + w) * KD + j + c), in1=bank[:, 0:T],
                                                 op0=ALU.mult, op1=ALU.add).then_inc(done, 1)
            modulation(1)
            modulation(2)
            then(dve.scalar_tensor_tensor(out=a2, in0=mod[:, 32:40], scalar=1.0,
                                          in1=par[:, COL["norm_ffn_g"]:COL["norm_ffn_g"] + 8],
                                          op0=ALU.add, op1=ALU.mult))
            bank = filled(dve, "mean1")
            for j in range(KD):
                moved(dve, ("conv", j))
                dve.scalar_tensor_tensor(out=y[:, j, :], in0=bank[:, 0:T], scalar=-1.0 / D, in1=y[:, j, :],
                                         op0=ALU.mult, op1=ALU.add).then_inc(sem("centred1"), 1)
            dve.wait_ge(sem("centred1"), KD)
            rstd = rstd_of("var1")
            for j in range(KD):
                dve.scalar_tensor_tensor(out=y[:, j, :], in0=y[:, j, :], scalar=col("conv_ln_g", j), in1=rstd,
                                         op0=ALU.mult, op1=ALU.mult).then_inc(sem("normed1"), 1)
            for j in range(KD):
                bank = filled(dve, ("proj1", j))
                dve.scalar_tensor_tensor(out=xT[:, j, :], in0=bank[:, 0:T], scalar=mod[:, 16 + j:17 + j],
                                         in1=xT[:, j, :], op0=ALU.mult, op1=ALU.add) \
                    .then_inc(read(("proj1", j)), 1)
            rstd = rstd_of("ms2")
            for j in range(KD):
                moved(dve, ("proj1", j))
                dve.scalar_tensor_tensor(out=scaled[:, j, :], in0=xT[:, j, :], scalar=a2[:, j:j + 1], in1=rstd,
                                         op0=ALU.mult, op1=ALU.mult).then_inc(sem("h2_scaled"), 1)

            def tmp(at, n, e):
                return small[:, at:at + n * e].rearrange("p (t e) -> p t e", t=n)

            def wide(a, n):
                return a.unsqueeze(2).broadcast_to((P, NT, n))

            iota32 = rc[:, R_IOTA32:R_IOTA32 + EXPERTS]
            bank = filled(dve, "logit")
            dve.wait_ge(sem("route_in"), 16)
            logit = tmp(0, NT, 36)
            dve.tensor_copy(logit, bank[:, 0:128].rearrange("p (t e) -> p t e", t=NT)[:, :, 0:36]) \
                .then_inc(read("logit"), 1)
            moved(dve, "logit")
            gmax, m1, m2, mn = small[:, 72:74], small[:, 74:76], small[:, 76:78], small[:, 78:80]

            def first_max(values, n, most, flags, cand, picked):
                then(dve.tensor_reduce(most, values, AX.X, ALU.max))
                then(dve.tensor_tensor(flags, values, wide(most, n), ALU.is_equal))
                for t in range(NT):
                    ins = dve.scalar_tensor_tensor(out=cand[:, t, :], in0=flags[:, t, :], scalar=-64.0,
                                                   in1=iota32[:, 0:n], op0=ALU.mult, op1=ALU.add)
                    if t < NT - 1:
                        ins.then_inc(sem("first_half"), 1)
                        first[0] += 1
                then(ins)
                dve.wait_ge(sem("first_half"), first[0])
                then(dve.tensor_reduce(mn, cand, AX.X, ALU.min))
                then(dve.tensor_tensor(picked, cand, wide(mn, n), ALU.is_equal))

            first = [0]
            flags, cand = tmp(128, NT, 32), tmp(192, NT, 32)
            oh1, oh2, picked, em = tmp(256, NT, 32), tmp(320, NT, 32), tmp(384, NT, 32), tmp(448, NT, 32)
            glog, elog = logit[:, :, 0:GROUPS], logit[:, :, GROUPS:36]
            ohg, gflag, gcand = tmp(96, NT, 4), tmp(104, NT, 4), tmp(112, NT, 4)
            first_max(glog, GROUPS, gmax, gflag, gcand, ohg)
            dve.tensor_tensor(tmp(80, NT, 4), glog, wide(gmax, 4), ALU.subtract).then_inc(sem("group_shifted"), 1)
            pen = tmp(120, NT, 4)
            then(dve.tensor_scalar(pen, ohg, BIG, -BIG, ALU.mult, ALU.add))
            for t in range(NT):
                then(dve.tensor_tensor(em[:, t, :].rearrange("p (g e) -> p g e", g=GROUPS),
                                       elog[:, t, :].rearrange("p (g e) -> p g e", g=GROUPS),
                                       pen[:, t, :].unsqueeze(2).broadcast_to((P, GROUPS, PER_GROUP)), ALU.add))
            first_max(em, EXPERTS, m1, flags, cand, oh1)
            then(dve.scalar_tensor_tensor(out=em.rearrange("p t e -> p (t e)"),
                                          in0=oh1.rearrange("p t e -> p (t e)"), scalar=-3 * BIG,
                                          in1=em.rearrange("p t e -> p (t e)"), op0=ALU.mult, op1=ALU.add))
            first_max(em, EXPERTS, m2, flags, cand, oh2)
            dve.tensor_tensor(picked, oh1, oh2, ALU.add).then_inc(sem("chosen"), 1)
            dve.tensor_tensor(small[:, 88:90], m2, m1, ALU.subtract).then_inc(sem("pair_shifted"), 1)
            dve.wait_ge(sem("group_exp"), 1)
            gsum, gp, es, w1, w2 = (small[:, 520:522], small[:, 522:524], small[:, 524:526],
                                    small[:, S_W1:S_W1 + 2], small[:, S_W2:S_W2 + 2])
            then(dve.tensor_reduce(gsum, tmp(80, NT, 4), AX.X, ALU.add))
            then(dve.reciprocal(gp, gsum))
            dve.wait_ge(sem("pair_exp"), 1)
            then(dve.tensor_scalar(es, small[:, 88:90], 1.0, None, ALU.add))
            then(dve.reciprocal(es, es))
            then(dve.tensor_tensor(w1, es, gp, ALU.mult))
            then(dve.tensor_tensor(w2, w1, small[:, 88:90], ALU.mult))
            bank = filled(dve, "rank")
            cnt = small[:, 530:562]
            incl, start = small[:, 562:594], small[:, 594:626]
            then(dve.tensor_copy(cnt, bank[:, 64:96]))
            then(dve.tensor_tensor_scan(incl, ones[:, 0:EXPERTS], cnt, 0.0, ALU.mult, ALU.add))
            then(dve.tensor_tensor(start, incl, cnt, ALU.subtract))
            pos = tmp(640, NT, 32)
            dve.tensor_tensor(pos, bank[:, 0:64].rearrange("p (t e) -> p t e", t=NT),
                              start.unsqueeze(1).broadcast_to((P, NT, EXPERTS)), ALU.add).then_inc(read("rank"), 1)
            moved(dve, "rank")
            then(dve.tensor_tensor(flags, oh1, pos, ALU.mult))
            then(dve.tensor_reduce(small[:, S_P1:S_P1 + 2], flags, AX.X, ALU.add))
            then(dve.tensor_tensor(flags, oh2, pos, ALU.mult))
            dve.tensor_reduce(small[:, S_P2:S_P2 + 2], flags, AX.X, ALU.add).then_inc(sem("slots_known"), 1)
            dve.wait_ge(sem("slots_known"), 1)
            iota = rc[:, R_IOTA:R_IOTA + SLOTS_A]
            for t in range(NT):
                then(dve.tensor_scalar(sel[:, t, :], iota, small[:, S_P1 + t:S_P1 + t + 1], None, ALU.is_equal))
                dve.scalar_tensor_tensor(out=sel[:, t, :], in0=iota, scalar=small[:, S_P2 + t:S_P2 + t + 1],
                                         in1=sel[:, t, :], op0=ALU.is_equal, op1=ALU.add) \
                    .then_inc(sem("sel_ready"), 1)
            for t in range(NT):
                then(dve.tensor_scalar(em[:, t, :], oh1[:, t, :], w1[:, t:t + 1], None, ALU.mult))
                then(dve.scalar_tensor_tensor(out=em[:, t, :], in0=oh2[:, t, :], scalar=w2[:, t:t + 1],
                                              in1=em[:, t, :], op0=ALU.mult, op1=ALU.add))
            then(dve.tensor_tensor(pos, pos, start.unsqueeze(1).broadcast_to((P, NT, EXPERTS)), ALU.subtract))
            then(dve.scalar_tensor_tensor(out=pos.rearrange("p t e -> p (t e)"),
                                          in0=pos.rearrange("p t e -> p (t e)"), scalar=1.0,
                                          in1=picked.rearrange("p t e -> p (t e)"), op0=ALU.add, op1=ALU.mult))
            for r in range(4):
                if r < 3:
                    then(dve.tensor_copy(small[:, P * r + 64:P * r + 128], small[:, 448:512]))
                then(dve.tensor_scalar(small[:, P * r:P * r + 64], pos.rearrange("p t e -> p (t e)"),
                                       -1.0 - WIN * r, None, ALU.add))
            row = tmp(740, 1, 132)[0:1, 0, :]
            then(dve.tensor_copy(row[:, 0:EXPERTS], start[0:1, :]))
            then(dve.memset(row[:, EXPERTS:EXPERTS + 4], 0.0))
            then(dve.tensor_reduce(row[:, EXPERTS:EXPERTS + 1], cnt[0:1, :], AX.X, ALU.max))
            for r in range(1, 4):
                lo = EXPERTS + 4 + EXPERTS * (r - 1)
                then(dve.tensor_scalar(row[:, lo:lo + EXPERTS], start[0:1, :], float(WIN * r), float(NOWHERE),
                                       ALU.add, ALU.min))
            dve.tensor_copy(table[0:1, :], row).then_inc(sem("table_ready"), 1)
            for j in range(1, KD, 2):
                bank = filled(dve, ("gather", j))
                dve.tensor_copy(xg[:, j, 0:SLOTS_A], bank[:, :]).then_inc(read(("gather", j)), 1)

            def gated(done):
                dve.tensor_tensor(hid, GU_BANK[0:WIN, :], silu_g, ALU.mult).then_inc(done, 1)

            def move_result(done):
                dve.tensor_copy(y_e, Y_BANK[:, :]).then_inc(done, 1)

            dve.wait_ge(silu_done, 1)
            gated(hid_ready)
            with dve.Fori(1, EXPERTS) as e:
                dve.wait_ge(silu_done, e + 1)
                dve.wait_ge(t_full, e + C_T)
                gated(hid_ready)
                dve.wait_ge(y_full, e)
                move_result(y_moved)
            dve.wait_ge(y_full, EXPERTS)
            move_result(y_moved)
            dve.wait_ge(sem("combined"), 1)
            with dve.If(overflow(dve)):
                with dve.Fori(0, 3 * EXPERTS) as n:
                    dve.wait_ge(sem("over_silu"), n + 1)
                    gated(sem("over_hidden"))
                    dve.wait_ge(sem("over_down"), n + 1)
                    move_result(sem("over_down_moved"))
                dve.wait_ge(sem("over_done"), 3 * EXPERTS + 1)
            for j in range(KD):
                bank = ACC[j // 2]
                dve.scalar_tensor_tensor(out=xT[:, j, :], in0=bank[:, (j % 2) * T:(j % 2 + 1) * T],
                                         scalar=mod[:, 40 + j:41 + j], in1=xT[:, j, :],
                                         op0=ALU.mult, op1=ALU.add).then_inc(read(("acc", j // 2)), 1)
            rstd = rstd_of("ms3")
            for j in range(KD):
                moved(dve, ("acc", j // 2))
                dve.scalar_tensor_tensor(out=xT[:, j, :], in0=xT[:, j, :], scalar=col("final_g", j), in1=rstd,
                                         op0=ALU.mult, op1=ALU.mult).then_inc(sem("x_normed"), 1)

            for j in range(KQ + KKV):
                bank = filled(dve, ("cq", j))
                dve.tensor_copy(cq[:, j, :], bank[:, 0:T]).then_inc(read(("cq", j)), 1)
            rq = rstd_of("msq")
            for j in range(KQ):
                moved(dve, ("cq", j))
                dve.scalar_tensor_tensor(out=cq[:, j, :], in0=cq[:, j, :], scalar=col("mla_q_norm_2", j), in1=rq,
                                         op0=ALU.mult, op1=ALU.mult).then_inc(sem("latent_ready"), 1)
            rkv = rstd_of("mskv")
            for j in range(KKV):
                moved(dve, ("cq", KQ + j))
                dve.scalar_tensor_tensor(out=cq[:, KQ + j, :], in0=cq[:, KQ + j, :],
                                         scalar=col("mla_kv_norm_2", j), in1=rkv,
                                         op0=ALU.mult, op1=ALU.mult).then_inc(sem("latent_ready"), 1)
            swap = [(i + ROPE // 2) % ROPE for i in range(ROPE)]
            cosA = ac[NOPE:QK, A_COS:A_COS + T]
            sinA = ac[NOPE:QK, A_SIN:A_SIN + T]
            dve.wait_ge(sem("mla_in"), 16)
            moved(dve, "krope")
            k_raw, k_turn = raw[NOPE:QK, 3, 0:T], raw[NOPE:QK, 3, T:2 * T]
            then(dve.stream_shuffle(k_turn, k_raw, swap))
            then(dve.tensor_tensor(k_turn, k_turn, sinA, ALU.mult))
            then(dve.tensor_tensor(k_raw, k_raw, cosA, ALU.mult))
            dve.tensor_tensor(k_raw, k_raw, k_turn, ALU.add).then_inc(sem("krope_ready"), 1)
            for t in range(NT):
                name = ("v1", t, 1)
                bank = filled(dve, name)
                dve.tensor_copy(v[:, t, 512:D], bank[:, :]).then_inc(read(name), 1)
            for p in range(1, HEADS // 2, 2):
                name = ("kn", p)
                bank = filled(dve, name)
                dve.tensor_copy(kh[0:NOPE, 2 * p:2 * p + 2, :], bank[0:NOPE, :].rearrange("p (h n) -> p h n", h=2)) \
                    .then_inc(read(name), 1)
            sin2 = sinA.unsqueeze(1).broadcast_to((ROPE, 2, T))
            for p in range(HEADS // 2):
                moved(dve, ("q", p))
                turn = raw[NOPE:QK, p % 2, :].rearrange("p (h n) -> p h n", h=2)
                q = qh[NOPE:QK, 2 * p:2 * p + 2, :]
                dve.stream_shuffle(turn, q, swap).then_inc(sem("q_shuffled"), 1)
                dve.wait_ge(sem("q_shuffled"), p + 1)
                then(dve.tensor_tensor(turn, turn, sin2, ALU.mult))
                dve.wait_ge(sem("q_cos"), p + 1)
                dve.tensor_tensor(q, q, turn, ALU.add).then_inc(sem("q_ready"), 1)

            mask = ac[:, A_MASK:A_MASK + T]

            def attention(layer, scale):
                for i in range(HEADS + 4):
                    if i < HEADS:
                        b = i % 4
                        name = ("s", layer, i)
                        bank = filled(dve, name)
                        if i >= 4:
                            filled(dve, ("pt", layer, i - 4))
                        dve.tensor_tensor_reduce(out=prob[:, b, 0:P], in0=bank[:, 0:P], in1=mask[:, P:T],
                                                 scale=-scale, scalar=3e38, op0=ALU.add, op1=ALU.min,
                                                 accum_out=smin[:, b, 0:1]).then_inc(sem("scores_part"), 1)
                        dve.wait_ge(sem("scores_part"), HEADS * layer + i + 1)
                        dve.tensor_tensor_reduce(out=prob[:, b, P:3 * P], in0=bank[:, P:3 * P], in1=mask,
                                                 scale=-scale, scalar=3e38, op0=ALU.add, op1=ALU.min,
                                                 accum_out=smin[:, b, 1:2]).then_inc(read(name), 1)
                    if 1 <= i <= HEADS:
                        b = (i - 1) % 4
                        dve.wait_ge(sem("exp_done"), 2 * (HEADS * layer + i))
                        dve.reciprocal(srec[:, b, :], ssum[:, b, :]).then_inc(sem("sum_inverse"), 1)
                    if i >= 5 and (i - 5) % 2 == 0 and (i - 5) // 2 < HEADS // 2:
                        merge(layer, (i - 5) // 2)

            def merge(layer, p):
                name = ("o", layer, p)
                bank = filled(dve, name)
                dve.tensor_tensor(o[:, p, :], bank[:, 0:T], gate[:, p, :], ALU.mult).then_inc(read(name), 1)

            def out_norm(layer):
                for j in range(KD):
                    name = ("proj2", layer, j)
                    bank = filled(dve, name)
                    dve.scalar_tensor_tensor(out=xT[:, j, :], in0=xT[:, j, :], scalar=ALPHA, in1=bank[:, 0:T],
                                             op0=ALU.mult, op1=ALU.add).then_inc(read(name), 1)
                name = ("mean2", layer)
                bank = filled(dve, name)
                for j in range(KD):
                    dve.scalar_tensor_tensor(out=xT[:, j, :], in0=bank[:, 0:T], scalar=-1.0 / D, in1=xT[:, j, :],
                                             op0=ALU.mult, op1=ALU.add).then_inc(sem("centred2"), 1)
                dve.wait_ge(sem("centred2"), KD * (layer + 1))
                rs = rstd_of(("var2", layer))
                for j in range(KD):
                    dve.scalar_tensor_tensor(out=xT[:, j, :], in0=xT[:, j, :], scalar=col("ln_g_2", KD * layer + j),
                                             in1=rs, op0=ALU.mult, op1=ALU.mult).then_inc(sem("normed2"), 1)

            attention(0, SCALE_A)
            out_norm(0)
            dve.wait_ge(sem("moba_in"), 16)
            for n in range(2):
                for j in range(KD):
                    name = ("rot", n, j)
                    bank = filled(dve, name)
                    dve.tensor_tensor(turned[:, j, :], bank[:, 0:T], bc[:, B_SIN:B_SIN + T], ALU.mult) \
                        .then_inc(read(name), 1)
                    moved(dve, name)
                    dve.wait_ge(sem("raw_cos"), KD * n + j + 1)
                    to = qb if n else kb
                    dve.tensor_tensor(to[:, j, :], raw_b[:, j, :], turned[:, j, :], ALU.add) \
                        .then_inc(sem("turned"), 1)
            attention(1, SCALE_B)
            out_norm(1)
            for t in range(NT):
                name = ("out", t, 0)
                bank = filled(dve, name)
                dve.tensor_copy(out_tok[:, t, 0:512], bank[:, :]).then_inc(sem(f"out_ready{t}"), 1)


_USED = ["x", "c", "ada_w", "ada_b", "norm_mix_g", "norm_ffn_g", "final_g", "conv_w_in", "conv_b_in",
         "conv_w_dw", "conv_b_dw", "conv_ln_g", "conv_ln_b", "conv_w_out", "moe_w_rg", "moe_b_rg",
         "moe_w_re", "moe_b_re", "moe_w_gate", "moe_w_up", "moe_w_down", "mla_w_in_2", "mla_q_norm_2",
         "mla_kv_norm_2", "mla_w_uq_2", "mla_w_ukv_2", "mla_w_o_2", "moba_w_kv_2", "moba_w_in_2",
         "moba_w_o_2", "ln_g_2", "ln_b_2"]


def shape_constants():
    base = np.concatenate([np.eye(P), np.ones((P, P))], 1)
    i = np.arange(P)
    route = np.concatenate([i[:, None] < i[None, :],
                            np.broadcast_to(np.arange(SLOTS_A), (P, SLOTS_A)),
                            np.broadcast_to(np.arange(P) % WIN, (P, P))], 1)
    mask = np.concatenate([np.zeros((P, P)), np.where(i[None, :] <= i[:, None], 0.0, -BIG)], 1)

    def tables(dim):
        inv = np.float32(10000.0) ** (-np.arange(0, dim, 2, dtype=np.float32) / np.float32(dim))
        ang = np.arange(T, dtype=np.float32)[None, :] * inv.astype(np.float32)[:, None]
        ang = np.concatenate([ang, ang], 0)
        return np.cos(ang), np.sin(ang)

    cos, sin = tables(ROPE)
    sign = np.where(np.arange(ROPE) < ROPE // 2, -1.0, 1.0)[:, None]
    mla = np.zeros((P, A_COLS))
    mla[:, 0:T] = mask
    mla[NOPE:QK, A_COS:A_COS + T] = cos
    mla[NOPE:QK, A_SIN:A_SIN + T] = sin * sign
    cos, sin = tables(HD)
    rot = np.zeros((P, P))
    for m in range(P):
        if m % HD < HD // 2:
            rot[m + HD // 2, m] = -1.0
        else:
            rot[m - HD // 2, m] = 1.0
    moba = np.concatenate([np.tile(cos, (2, 1)), np.tile(sin, (2, 1)), rot], 1)
    return {"k_base": base, "k_route": route, "k_mla": mla, "k_moba": moba}


def kernel(**inputs):
    import concourse.bacc as bacc
    from concourse.bass_utils import run_bass_kernel_spmd

    nc = bacc.Bacc("TRN2", target_bir_lowering=False, num_devices=1)
    arrays, A = {}, {}
    given = {name: np.ascontiguousarray(inputs[name]) for name in _USED}
    for name, a in shape_constants().items():
        given[name] = np.ascontiguousarray(a.astype(np.float32))
    for name, a in given.items():
        arrays[f"in_{name}"] = a
        A[name] = nc.dram_tensor(f"in_{name}", a.shape, mybir.dt.from_np(a.dtype), kind="ExternalInput").ap()
    out = nc.dram_tensor("out_0", (1, T, D), F32, kind="ExternalOutput").ap()
    two_blocks(nc, A, out)
    r = run_bass_kernel_spmd(nc, [arrays], core_ids=[0])
    return r.results[0]["out_0"]
```

```python
from contextlib import ExitStack

import numpy as np
import concourse.bass as bass
from concourse import mybir

ALU = mybir.AluOpType
ACT = mybir.ActivationFunctionType
F32 = mybir.dt.float32
I32 = mybir.dt.int32
AX = mybir.AxisListType

P = 128
T = 256
NT = T // P
D = 1024
KD = D // P
TAPS = 31
EXPERTS = 32
GROUPS = 4
PER_GROUP = EXPERTS // GROUPS
CHOICES = GROUPS + EXPERTS
HIDDEN = 512
KF = HIDDEN // P
SLOTS_A = 2 * T
WIN = 64
PADDED = SLOTS_A + WIN
NOWHERE = SLOTS_A
BIG = 1e30
EPS = 1e-6
LN_EPS = 1e-5
ALPHA = 4 ** 0.25

HEADS = 16
NOPE, ROPE = 64, 32
QK = NOPE + ROPE
HD = 64
KQ = 768 // P
KKV = 256 // P
SCALE_A = QK ** -0.5
SCALE_B = HD ** -0.5

SLOT = 4096
RING = 9
RING_C = 7
BODY = 3
LOOPS = EXPERTS // BODY
PEELED = EXPERTS - LOOPS * BODY
PE_TAPS = 7
DIAGS = 8
SPLIT = 640
ROWS_AT = 13
GATES_AT = 13

C_IDENT, C_ONES = 0, P
R_STRICT, R_IOTA = 0, P
R_IOTA32 = R_IOTA
R_IOTA2 = P + SLOTS_A
R_COLS = 2 * P + SLOTS_A
A_MASK, A_COS, A_SIN = 0, T, 2 * T
A_COLS = 3 * T
B_COLS = 2 * T

LOT0 = [("ada_b", 48), ("conv_b_in", 16), ("norm_mix_g", 8), ("norm_ffn_g", 8), ("final_g", 8),
        ("conv_b_dw", 8), ("conv_ln_g", 8), ("conv_ln_b", 8), ("c", 8)]
LOT1 = [("mla_q_norm_2", 6), ("mla_kv_norm_2", 2), ("ln_g_2", 16), ("ln_b_2", 16)]
COL = {}
_at = 0
for _name, _n in LOT0 + LOT1:
    COL[_name] = _at
    _at += _n
LOT0_ROWS = sum(n for _, n in LOT0)
LOT1_ROWS = sum(n for _, n in LOT1)
COL["dw"] = _at
PAR = _at + TAPS * KD
DW_ROWS = TAPS * KD // 2


def two_blocks(nc, A, out):
    with ExitStack() as ctx:
        def sb(name, shape, dt=F32):
            return ctx.enter_context(nc.sbuf_tensor(name, shape, dt))

        sems = {}

        def sem(name):
            if name not in sems:
                sems[name] = ctx.enter_context(nc.semaphore(name))
            return sems[name]

        R0 = RING * SLOT
        R = R0 + KD * T
        arena = sb("arena", [P, R + 13312])
        consts = sb("consts", [P, 2 * P])
        par = sb("par", [P, PAR])
        mod = sb("mod", [P, 48])
        der = sb("der", [P, 40])
        brow = sb("brow", [1, GROUPS + EXPERTS])
        table = sb("table", [1, 4 * EXPERTS + 4], I32)
        ps = [ctx.enter_context(nc.psum_tensor(f"bank{i}", [P, 512], F32)) for i in range(8)]

        def area(off, k, n):
            return arena[:, off:off + k * n].rearrange("p (k n) -> p k n", k=k)

        ident = consts[:, C_IDENT:C_IDENT + P]
        ones = consts[:, C_ONES:C_ONES + P]

        def col(name, j=0):
            return par[:, COL[name] + j:COL[name] + j + 1]

        a1, a2 = der[:, 8:16], der[:, 16:24]
        own = der[:, 28:40].rearrange("p (b q) -> p b q", b=BODY)
        eps6, eps5 = der[:, 24:25], der[:, 25:26]

        xT = area(R0, KD, T)
        x_tok = area(R, NT, D)
        sq = area(R + 2048, KD, T)
        h = area(R + 4096, KD, T)
        u = area(R + 6144, KD, TAPS - 1 + T)
        y = area(R + 8432, KD, T)
        sg = area(R + 10480, 4, T)
        diag = area(R + 11504, DIAGS, P)
        rows = area(R + 12528, 4, P)
        cact = area(R + 13040, KD, 32)
        ada_rows = arena[:, R + 12528:R + 13040]
        std = arena[:, R + 6144:R + 6144 + T]
        scaled = x_tok.rearrange("p a b -> p (a b)").rearrange("p (k n) -> p k n", k=KD)
        h2 = area(R + 4608, KD, T)
        h2_tok = area(R + 6656, NT, D)
        small = arena[:, R + 9216:R + 10240]
        sel = area(R + 10240, NT, SLOTS_A)
        rc = arena[:, R + 12528:R + 12528 + R_COLS]
        wr = arena[:, R + 8704:R + 8704 + KD * CHOICES].rearrange("p (k n) -> p k n", k=KD)
        logit_rows = small[0:CHOICES, 640:640 + T]
        xg = area(R, KD, PADDED)
        xw = [area(R + 4608 + b * KD * WIN, KD, WIN) for b in range(BODY)]
        weighted = [area(R + 6144 + b * NT * P, NT, P) for b in range(BODY)]
        silu_g = arena[0:WIN, R + 6912:R + 6912 + HIDDEN]
        hid = arena[0:WIN, R + 7424:R + 7424 + HIDDEN]
        turned_e = [arena[:, R + 10240 + b * 512:R + 10752 + b * 512] for b in range(BODY)]
        hid_t = [a[:, 0:KF * WIN].rearrange("p (f n) -> p f n", f=KF) for a in turned_e]
        comb = [a[:, KF * WIN:512] for a in turned_e]
        y_e = arena[:, R + 11776:R + 12288]
        qh = area(RING_C * SLOT, HEADS, T)
        kh = area((RING_C + 1) * SLOT, HEADS, T)
        cq = area(R, KQ + KKV, T)
        gate = area(R + 2048, KD, T)
        v = area(R + 4096, NT, D)
        o = area(R + 6144, KD, T)
        sq2 = o
        raw = area(R + 6144, 4, 2 * T)
        prob = area(R + 8192, 4, 3 * P)
        prob_t = area(R + 9728, 4, 3 * P)
        ac = arena[:, R + 11264:R + 11264 + A_COLS]
        std2 = arena[:, R + 12032:R + 12288]
        smin = area(R + 12288, 4, 2)
        ssum = area(R + 12296, 4, 2)
        srec = area(R + 12304, 4, 2)
        wrope = area(R + 12352, KD, ROPE)
        qb = area(RING_C * SLOT, KD, T)
        kb = area(RING_C * SLOT + 2048, KD, T)
        raw_b = area((RING_C + 1) * SLOT, KD, T)
        turned = area((RING_C + 1) * SLOT + 2048, KD, T)
        x_rows = area(R, NT, D)
        affine = area((RING_C + 1) * SLOT, 4, D)
        stats = area(R + 12312, NT, 20)

        def slot(s, k=KD, n=512):
            return arena[:, s * SLOT:s * SLOT + k * n].rearrange("p (k n) -> p k n", k=k)

        use, fills, reads = {}, [0] * 8, [0] * 8

        def plan(name, b, readers=1, counted=1):
            use[name] = (b, fills[b], reads[b], reads[b] + readers)
            fills[b] += counted
            reads[b] += readers

        for j in range(KD):
            plan(("x", j), j % 4)
        plan("par", 4)
        plan("ms1", 7)
        plan(("ada", 0), 6)
        plan(("mod", 0), 5)
        for j in range(KD):
            plan(("glu_a", j), 2 * (j % 2))
            plan(("glu_g", j), 2 * (j % 2) + 1)
        for pair in range(KD // 2):
            plan(("conv", pair), 4 + pair % 2, readers=2, counted=0)
        for g in (1, 2):
            plan(("ada", g), 5 + g)
            plan(("mod", g), g - 1)
        plan("mean1", 6, readers=0)
        plan("var1", 7)
        for j in range(KD):
            plan(("proj1", j), j % 4)
        plan("ms2", 7)
        plan("logit_rows", 4)
        plan("logit", 5)
        for t in range(NT):
            for half in range(2):
                plan(("h2tok", t, half), 2 * t + half)
        plan("rank", 4, 1)
        for j in range(KD):
            plan(("gather", j), j % 4)
        BEFORE_EXPERTS = list(reads)
        for n in range(4):
            plan(("acc", n), 4 + n, readers=2, counted=0)
        plan("ms3", 7)
        for j in range(KQ + KKV):
            plan(("cq", j), j % 4)
        plan("msq", 7)
        plan("mskv", 6)
        plan("krope", 4)
        for j in range(KD // 2):
            plan(("gate", 0, j), j % 4)
        for t in range(NT):
            for n in range(2):
                plan(("v1", t, n), 2 * t + n)
        for g in range(HEADS // 4):
            plan(("kn", g), g % 4, readers=2)
        for g in range(HEADS // 4):
            plan(("qn", g), g % 2, readers=2)
            plan(("qr", g), 2 + g % 2)
        for layer in (0, 1):
            if layer:
                for n in range(2):
                    for j in range(KD):
                        plan(("raw", n, j), j % 4, readers=2)
                    for w in range(4):
                        plan(("gate", 1, w) if n else ("v2", w // 2, w % 2), w % 4)
            for half in range(2):
                plan(("gates", layer, half), 6 + half)
            for i in range(HEADS + 3):
                if i < HEADS:
                    plan(("s", layer, i), i % 2)
                if 0 <= i - 2 < HEADS:
                    plan(("pt", layer, i - 2), 2 + i % 2)
                if 0 <= i - 3 and (i - 3) % 2 == 0:
                    plan(("o", layer, (i - 3) // 2), 4 + (i - 3) // 2 % 2)
            for t in range(NT):
                for half in range(2):
                    if layer == 0:
                        plan(("rows", t, half), 6 + half)
            for t in range(NT):
                for half in range(2):
                    plan(("out", layer, t, half), 2 * t + half)
            for t in range(NT):
                for half in range(2):
                    if layer == 0:
                        plan(("back", t, half), 4 + 2 * t + half, readers=4)

        def may_fill(pe, name):
            b, _, before, _ = use[name]
            if before:
                pe.wait_ge(sem(f"bank{b}_read"), before)
            return ps[b]

        def filled(eng, name):
            b, n, _, _ = use[name]
            eng.wait_ge(sem(f"bank{b}_full"), n + 1)
            return ps[b]

        def full(name):
            return sem(f"bank{use[name][0]}_full")

        def read(name):
            return sem(f"bank{use[name][0]}_read")

        def moved(eng, name):
            b, _, _, after = use[name]
            eng.wait_ge(sem(f"bank{b}_read"), after)

        def partly_moved(eng, name, n):
            b, _, before, _ = use[name]
            eng.wait_ge(sem(f"bank{b}_read"), before + n)

        def cols(w, lo, n, k=KD):
            return w[:, lo:lo + n].rearrange("(k p) n -> p k n", p=P)

        chunks = []

        def chunk(name, s, parts, last):
            chunks.append((name, s, parts, last))

        aw = A["ada_w"][0]
        win = A["conv_w_in"][0]
        order = [("ada", i) for i in range(4)] + [("glu", i) for i in range(4)] \
            + [("ada", i) for i in range(4, 12)] + [("proj1", 0), ("proj1", 1)]
        for i, (kind, n) in enumerate(order):
            s = i % RING
            if kind == "ada":
                chunk((kind, n), s, [(slot(s), cols(aw, 512 * n, 512))], ("ada", n // 4))
            elif kind == "glu":
                w = arena[:, s * SLOT:(s + 1) * SLOT].rearrange("p (k n) -> p k n", k=KD)
                chunk((kind, n), s, [(w[:, :, 0:256], cols(win, 256 * n, 256)),
                                     (w[:, :, 256:512], cols(win, D + 256 * n, 256))], ("glu_g", 2 * n + 1))
            else:
                chunk((kind, n), s, [(slot(s), cols(A["conv_w_out"][0], 512 * n, 512))], ("proj1", 4 * n + 3))
        CHUNKS_A = len(chunks)
        assert CHUNKS_A % RING == 0

        def next_c():
            return (RING_C - 1 + len(chunks) - CHUNKS_A) % RING_C

        mw = A["mla_w_in_2"][0]
        for n in range(2):
            s = next_c()
            chunk(("cq", n), s, [(slot(s), cols(mw, 512 * n, 512))], ("cq", 4 * n + 3))
        for n in range(2):
            s = next_c()
            chunk(("gate", 0, n), s, [(slot(s), cols(mw, D + ROPE + 512 * n, 512))],
                  ("gates", 0, 1) if n else ("gate", 0, 3))
        s = next_c()
        chunk("ukv", s, [(slot(s, KKV, 2048), cols(A["mla_w_ukv_2"][0], 0, 2048))], ("kn", HEADS // 4 - 1))
        for n in range(4):
            s = next_c()
            chunk(("uq", n), s, [(slot(s, KQ, 384), cols(A["mla_w_uq_2"][0], 384 * n, 384))], ("qr", n))
        for n in range(2):
            s = next_c()
            chunk(("wo", 0, n), s, [(slot(s), cols(A["mla_w_o_2"][0], 512 * n, 512))], ("out", 0, 1, n))
        for kind, w in (("kv", A["moba_w_kv_2"]), ("in", A["moba_w_in_2"][0])):
            for n in range(4):
                s = next_c()
                if n < 2:
                    last = ("raw", int(kind == "in"), 4 * n + 3)
                else:
                    last = ("v2", 1, n - 2) if kind == "kv" else ("gate", 1, 3) if n == 2 else ("gates", 1, 1)
                chunk((kind, n), s, [(slot(s), cols(w, 512 * n, 512))], last)
        for n in range(2):
            s = next_c()
            chunk(("wo", 1, n), s, [(slot(s), cols(A["moba_w_o_2"][0], 512 * n, 512))], ("out", 1, 1, n))

        landed, place, count = {}, {}, [0] * RING
        for i, (name, s, parts, _) in enumerate(chunks):
            if i == CHUNKS_A:
                EXPERT_BASE = list(count)
                for e in range(EXPERTS):
                    for m in range(3):
                        count[3 * (e % BODY) + m] += 16
            count[s] += 16 * len(parts)
            landed[name], place[name] = count[s], s

        def arrived(eng, name):
            eng.wait_ge(sem(f"slot{place[name]}"), landed[name])
            return place[name]

        gu_full, silu_done, hid_ready = sem("gate_up_full"), sem("silu_done"), sem("hidden_ready")
        t_full, t_moved = sem("turned_full"), sem("turned_moved")
        y_full, y_moved, win_ready = sem("down_full"), sem("down_moved"), sem("window_ready")
        GU_BANK, Y_BANK, T_BANK = ps[0], ps[1], ps[2]
        ACC = ps[4:8]
        C_T = BODY

        expert_w = [A["moe_w_gate"][0], A["moe_w_up"][0], A["moe_w_down"][0]]

        def overflow(eng):
            eng.wait_ge(sem("table_ready"), 1)
            most = eng.value_load(table[0:1, EXPERTS:EXPERTS + 1], min_val=0, max_val=T)
            return most > WIN

        S_P1, S_P2, S_W1, S_W2 = 1000, 1002, 1004, 1006

        block = ctx.enter_context(nc.Block())

        @block.sync
        def _(sp):
            sp.dma_start(x_tok, A["x"][0].rearrange("(t p) n -> p t n", p=P)).then_inc(sem("x_in"), 16)
            def load(i):
                _, s, parts, _ = chunks[i]
                for dst, src in parts:
                    sp.dma_start(dst, src).then_inc(sem(f"slot{s}"), 16)

            for i in range(CHUNKS_A):
                if i >= RING:
                    filled(sp, chunks[i - RING][3])
                load(i)
                if i == 0:
                    sp.wait_ge(sem("rows_in"), 16 * (len(LOT0) + len(LOT1) + 2))

            def load_matrix(e, b, m):
                s = 3 * b + m
                dst = slot(s) if m < 2 else slot(s, KF, D)
                src = expert_w[m][bass.ds(e, 1)].rearrange("e (k p) n -> p (e k) n", p=P)
                sp.dma_start(dst, src).then_inc(sem(f"slot{s}"), 16)

            for e in range(BODY):
                for m in range(3):
                    filled(sp, chunks[CHUNKS_A - RING + 3 * e + m][3])
                    load_matrix(e, e, m)
            with sp.Fori(0, LOOPS - 1) as it:
                for b in range(BODY):
                    sp.wait_ge(gu_full, it * BODY + (b + 1))
                    load_matrix(it * BODY + (BODY + b), b, 0)
                    load_matrix(it * BODY + (BODY + b), b, 1)
                    sp.wait_ge(y_full, it * BODY + (b + 1))
                    load_matrix(it * BODY + (BODY + b), b, 2)
            for b in range(PEELED):
                e = LOOPS * BODY + b
                sp.wait_ge(gu_full, e - BODY + 1)
                load_matrix(e, b, 0)
                load_matrix(e, b, 1)
                sp.wait_ge(y_full, e - BODY + 1)
                load_matrix(e, b, 2)
            with sp.If(overflow(sp)):
                sp.wait_ge(y_full, EXPERTS)
                with sp.Fori(0, EXPERTS) as e:
                    sp.wait_ge(sem("over_done"), e * 3 + 1)
                    for m in range(3):
                        dst = slot(m) if m < 2 else slot(m, KF, D)
                        sp.dma_start(dst, expert_w[m][bass.ds(e, 1)].rearrange("e (k p) n -> p (e k) n", p=P)) \
                            .then_inc(sem("over_in"), 16)
                sp.wait_ge(sem("over_done"), 3 * EXPERTS + 1)
            for i in range(CHUNKS_A, len(chunks)):
                n = i - CHUNKS_A
                s = chunks[i][1]
                if n >= RING_C:
                    filled(sp, chunks[i - RING_C][3])
                elif s == RING_C - 1:
                    sp.wait_ge(gu_full, LOOPS * BODY)
                elif s < 3 * PEELED:
                    e = LOOPS * BODY + s // 3
                    sp.wait_ge(gu_full if s % 3 < 2 else y_full, e + 1)
                load(i)
            sp.wait_ge(sem("turned"), 2 * KD)
            for layer in range(2):
                for at, name in ((0, "ln_g_2"), (1, "ln_b_2")):
                    sp.dma_start(affine[:, 2 * layer + at, :], A[name][layer:layer + 1, :].broadcast_to((P, D))) \
                        .then_inc(sem("affine_in"), 16)
            for t in range(NT):
                for side, lo, hi in (("left", 0, SPLIT), ("right", SPLIT, D)):
                    sp.wait_ge(sem(f"out_{side}"), t + 1)
                    sp.dma_start(out[0, t * P:(t + 1) * P, lo:hi], x_rows[:, t, lo:hi]) \
                        .then_inc(sem("out_done"), 16)
            sp.wait_ge(sem("out_done"), 16 * 2 * NT)

        @block.gpsimd
        def _(pool):
            pool.wait_ge(sem("consts_in"), 16)
            moved(pool, "par")
            made = 0
            for j in range(KD):
                for w in range(PE_TAPS):
                    if made >= DIAGS:
                        pool.wait_ge(sem("diag_used"), made - DIAGS + 1)
                    pool.tensor_scalar(diag[:, made % DIAGS, :], ident, col("dw", w * KD + j), 0.0,
                                       ALU.mult, ALU.add).then_inc(sem("diag_ready"), 1)
                    made += 1

            pool.wait_ge(sem("diag_used"), made)
            pool.memset(y_e, 0.0).then_inc(sem("zeros_ready"), 1)
            pool.wait_ge(sem("h2_ready"), KD)
            pool.memset(xg[:, :, SLOTS_A:PADDED], 0.0).then_inc(sem("pad_ready"), 1)
            pool.wait_ge(sem("pad_ready"), 1)
            pool.wait_ge(sem("table_ready"), 1)

            def window(e, r, b, ready):
                place = e if r == 0 else e + (4 + EXPERTS * r)
                ranks = small[:, P * r:P * (r + 1)].rearrange("p (q e) -> p q e", q=2 * NT)
                pool.tensor_copy(own[:, b, :].unsqueeze(2), ranks[:, :, bass.ds(e, 1)]).then_inc(sem("own_ready"), 1)
                pool.wait_ge(sem("own_ready"), e + 1 if r == 0 else e * 3 + (EXPERTS + r))
                at = pool.value_load(table[0:1, bass.ds(place, 1)], min_val=0, max_val=SLOTS_A)
                for t in range(NT):
                    pool.tensor_scalar(weighted[b][:, t, :], rc[:, R_IOTA2:R_IOTA2 + P], own[:, b, t:t + 1],
                                             own[:, b, NT + t:NT + t + 1], ALU.is_equal, ALU.mult)
                if b == 0 and r == 0:
                    for j in range(KD - 4, KD):
                        moved(pool, ("gather", j))
                pool.tensor_copy(xw[b], xg[:, :, bass.ds(at, WIN)]).then_inc(ready, 1)

            with pool.Fori(0, LOOPS) as it:
                for b in range(BODY):
                    pool.wait_ge(t_full, it * BODY + (b + 1))
                    window(it * BODY + b, 0, b, win_ready)
            for b in range(PEELED):
                pool.wait_ge(t_full, LOOPS * BODY + b + 1)
                window(LOOPS * BODY + b, 0, b, win_ready)
            pool.sem_inc(sem("over_done"), 1)
            with pool.If(overflow(pool)):
                pool.wait_ge(sem("combined"), 1)
                with pool.Fori(0, EXPERTS) as e:
                    for r in range(1, 4):
                        pool.wait_ge(sem("over_done"), e * 3 + r)
                        window(e, r, 0, sem("over_window"))

            pool.wait_ge(sem("krope_ready"), 1)
            src = raw[NOPE:QK, 3, 0:T].unsqueeze(1).broadcast_to((ROPE, HEADS, T))
            pool.tensor_copy(kh[NOPE:QK, :, :], src).then_inc(sem("krope_spread"), 1)
            pool.wait_ge(sem("krope_spread"), 1)
            for g in range(HEADS // 4):
                pool.wait_ge(sem("q_shuffled"), g + 1)
                pool.tensor_tensor(raw[:, g % 2, 0:T], raw[:, g % 2, 0:T], ac[:, A_COS:A_COS + T],
                                   ALU.mult).then_inc(sem("q_cos"), 1)

            def scale_probs(n):
                pool.wait_ge(sem("sum_inverse"), n + 1)
                b = n % 4
                pool.tensor_scalar(prob[:, b, 0:P], prob[:, b, 0:P], srec[:, b, 0:1], 0.0, ALU.mult, ALU.add)
                pool.tensor_scalar(prob[:, b, P:3 * P], prob[:, b, P:3 * P], srec[:, b, 1:2], 0.0,
                                   ALU.mult, ALU.add).then_inc(sem("probs_ready"), 1)

            for i in range(HEADS):
                scale_probs(i)
            for n in range(2):
                for j in range(KD):
                    partly_moved(pool, ("raw", n, j), 1)
                    if n == j == 0:
                        pool.wait_ge(sem("moba_in"), 16)
                    pool.tensor_tensor(raw_b[:, j, :], raw_b[:, j, :], ac[:, A_COS:A_COS + T], ALU.mult) \
                        .then_inc(sem("raw_cos"), 1)
            pool.wait_ge(sem("affine_in"), 64)
            for t in range(NT):
                for half in range(2):
                    filled(pool, ("back", t, half))
            for i in range(2):
                for t in range(NT):
                    if i:
                        pool.wait_ge(sem("rows_scaled"), t + 1)
                    pool.tensor_tensor(x_rows[:, t, :], x_rows[:, t, :], affine[:, i, :], ALU.add if i else ALU.mult) \
                        .then_inc(sem("rows_shifted" if i else "rows_scaled"), 1)
            for i in range(HEADS):
                scale_probs(HEADS + i)
            for t in range(NT):
                x = x_rows[:, t, SPLIT:D]
                pool.wait_ge(sem("row_inverse"), NT + t + 1)
                pool.tensor_scalar(x, x, stats[:, t, 12:13], stats[:, t, 15:16], ALU.subtract, ALU.mult) \
                    .then_inc(sem("right_step"), 1)
                pool.wait_ge(sem("right_step"), 2 * t + 1)
                pool.tensor_tensor(x, x, affine[:, 2, SPLIT:D], ALU.mult).then_inc(sem("right_step"), 1)
                pool.wait_ge(sem("right_step"), 2 * t + 2)
                pool.tensor_tensor(x, x, affine[:, 3, SPLIT:D], ALU.add).then_inc(sem("out_right"), 1)

        @block.scalar
        def _(act):
            def rows_of(name):
                a = A[name]
                n = len(a.shape)
                flat = a if n == 1 else a.rearrange("a b -> (a b)")
                return flat.rearrange("(r n) -> r n", n=P)

            act.dma_start(consts[:, :], A["k_base"]).then_inc(sem("consts_in"), 16)
            for lot, names in ((0, LOT0), (1, LOT1)):
                at = 0
                for name, n in names:
                    act.dma_start(rows[at:at + n, lot, :], rows_of(name)).then_inc(sem("rows_in"), 16)
                    at += n
            dwr = A["conv_w_dw"][0].rearrange("w (k n) -> (w k) n", n=P)
            for half in range(2):
                act.dma_start(rows[0:DW_ROWS, 2 + half, :], dwr[half * DW_ROWS:(half + 1) * DW_ROWS, :]) \
                    .then_inc(sem("rows_in"), 16)
            act.dma_start(brow[:, 0:GROUPS], A["moe_b_rg"]).then_inc(sem("router_in"), 16)
            act.dma_start(brow[:, GROUPS:GROUPS + EXPERTS], A["moe_b_re"]).then_inc(sem("router_in"), 16)

            def norm_std(name, n, eps):
                bank = filled(act, name)
                to = std if name in ("ms1", "var1", "ms2") else std2
                act.activation(to, bank[:, 0:T], ACT.Sqrt, bias=eps, scale=1.0 / n).then_inc(read(name), 1)

            for j in range(KD):
                moved(act, ("x", j))
                act.activation(sq[:, j, :], xT[:, j, :], ACT.Square).then_inc(sem("squared0"), 1)
            moved(act, "par")
            act.activation(cact[:, :, :], par[:, COL["c"]:COL["c"] + 8].unsqueeze(2).broadcast_to((P, KD, 32)),
                           ACT.Silu).then_inc(sem("c_ready"), 1)
            act.wait_ge(sem("eps_ready"), 2)
            norm_std("ms1", D, eps6)
            moved(act, ("mod", 0))
            for j in range(KD):
                act.wait_ge(sem("h_scaled"), j + 1)
                act.activation(h[:, j, :], h[:, j, :], ACT.Identity, bias=mod[:, j:j + 1]) \
                    .then_inc(sem("h_ready"), 1)

            def sigmoid(j):
                bank = filled(act, ("glu_g", j))
                if j >= 4:
                    moved(act, ("glu_a", j - 4))
                act.activation(sg[:, j % 4, :], bank[:, 0:T], ACT.Sigmoid, bias=col("conv_b_in", KD + j)) \
                    .then_inc(read(("glu_g", j)), 1)

            def convolved(pair):
                act.wait_ge(sem("conv_done"), 2 * pair + 2)
                bank = ps[use[("conv", pair)][0]]
                for c in range(2):
                    j = 2 * pair + c
                    act.activation(y[:, j, :], bank[:, c * T:(c + 1) * T], ACT.Identity, bias=col("conv_b_dw", j)) \
                        .then_inc(read(("conv", pair)), 1)

            for j in range(5):
                sigmoid(j)
            convolved(0)
            sigmoid(5)
            sigmoid(6)
            convolved(1)
            sigmoid(7)
            convolved(2)
            convolved(3)
            for j in range(KD):
                act.wait_ge(sem("centred1"), j + 1)
                act.activation(sq[:, j, :], y[:, j, :], ACT.Square).then_inc(sem("squared1"), 1)
            norm_std("var1", D, eps6)
            for j in range(KD):
                act.wait_ge(sem("normed1"), j + 1)
                act.activation(h[:, j, :], y[:, j, :], ACT.Silu, bias=col("conv_ln_b", j)) \
                    .then_inc(sem("act_ready"), 1)
            for j in range(KD):
                moved(act, ("proj1", j))
                act.activation(sq[:, j, :], xT[:, j, :], ACT.Square).then_inc(sem("squared2"), 1)
                if j == 0:
                    act.dma_start(rc, A["k_route"]).then_inc(sem("route_in"), 16)
                    act.dma_start(wr[:, :, 0:GROUPS], cols(A["moe_w_rg"][0], 0, GROUPS)) \
                        .then_inc(sem("router_in"), 16)
                    act.dma_start(wr[:, :, GROUPS:CHOICES], cols(A["moe_w_re"][0], 0, EXPERTS)) \
                        .then_inc(sem("router_in"), 16)
            norm_std("ms2", D, eps6)
            for j in range(KD):
                act.wait_ge(sem("h2_scaled"), j + 1)
                act.activation(h2[:, j, :], scaled[:, j, :], ACT.Identity, bias=mod[:, 24 + j:25 + j]) \
                    .then_inc(sem("h2_ready"), 1)
            for t in range(NT):
                for half in range(2):
                    name = ("h2tok", t, half)
                    bank = filled(act, name)
                    act.activation(h2_tok[:, t, half * 512:(half + 1) * 512], bank[:, :], ACT.Copy) \
                        .then_inc(read(name), 1)
            act.wait_ge(sem("group_shifted"), 1)
            act.activation(small[:, 80:88], small[:, 80:88], ACT.Exp).then_inc(sem("group_exp"), 1)
            act.wait_ge(sem("pair_shifted"), 1)
            act.activation(small[:, 88:90], small[:, 88:90], ACT.Exp).then_inc(sem("pair_exp"), 1)
            for j in range(0, KD, 2):
                bank = filled(act, ("gather", j))
                act.activation(xg[:, j, 0:SLOTS_A], bank[:, :], ACT.Copy).then_inc(read(("gather", j)), 1)

            def silu(full_sem, n, done):
                act.wait_ge(full_sem, n)
                act.activation(silu_g, GU_BANK[WIN:2 * WIN, :], ACT.Silu).then_inc(done, 1)

            def move_turned(full_sem, n, b, done):
                act.wait_ge(full_sem, n)
                act.activation(turned_e[b], T_BANK[:, :], ACT.Copy).then_inc(done, 1)

            silu(gu_full, 1, silu_done)
            with act.Fori(0, LOOPS) as it:
                for b in range(BODY):
                    move_turned(t_full, it * BODY + (C_T + b + 1), b, t_moved)
                    silu(gu_full, it * BODY + (b + 2), silu_done)
            for e in range(LOOPS * BODY + 1, EXPERTS + 1):
                move_turned(t_full, C_T + e, (e - 1) % BODY, t_moved)
                if e < EXPERTS:
                    silu(gu_full, e + 1, silu_done)
            more = overflow(act)
            act.wait_ge(sem("combined"), 1)
            with act.If(more):
                with act.Fori(0, 3 * EXPERTS) as n:
                    silu(sem("over_gate_up"), n + 1, sem("over_silu"))
                    move_turned(sem("over_turned"), n + 1, 0, sem("over_turned_moved"))
                act.wait_ge(sem("over_done"), 3 * EXPERTS + 1)
            for j in range(KD):
                moved(act, ("acc", j // 2))
                act.activation(sq2[:, j, :], xT[:, j, :], ACT.Square).then_inc(sem("squared3"), 1)
            act.dma_start(ac, A["k_mla"]).then_inc(sem("mla_in"), 16)
            act.dma_start(wrope, cols(mw, D, ROPE)).then_inc(sem("wrope_in"), 16)
            norm_std("ms3", D, eps6)
            for j in range(KQ + KKV):
                moved(act, ("cq", j))
                act.activation(sq2[:, j, :], cq[:, j, :], ACT.Square).then_inc(sem("squared5"), 1)
            norm_std("msq", KQ * P, eps6)
            act.wait_ge(sem("rstd_ready"), 5)
            norm_std("mskv", KKV * P, eps6)
            bank = filled(act, "krope")
            act.activation(raw[NOPE:QK, 3, 0:T], bank[NOPE:QK, 0:T], ACT.Copy).then_inc(read("krope"), 1)
            for j in range(KD // 2):
                name = ("gate", 0, j)
                bank = filled(act, name)
                act.activation(gate[:, j, :], bank[:, 0:T], ACT.Silu).then_inc(read(name), 1)
            for t in range(NT):
                name = ("v1", t, 0)
                bank = filled(act, name)
                act.activation(v[:, t, 0:512], bank[:, :], ACT.Copy).then_inc(read(name), 1)
            for g in range(HEADS // 4):
                name = ("kn", g)
                bank = filled(act, name)
                act.activation(kh[0:NOPE, 4 * g:4 * g + 4:2, :], bank[0:NOPE, :].rearrange("p (h n) -> p h n", h=2),
                               ACT.Copy).then_inc(read(name), 1)
            for g in range(HEADS // 4):
                name = ("qn", g)
                bank = filled(act, name)
                act.activation(qh[0:NOPE, 4 * g:4 * g + 4:2, :], bank[0:NOPE, :].rearrange("p (h n) -> p h n", h=2),
                               ACT.Copy).then_inc(read(name), 1)
                name = ("qr", g)
                bank = filled(act, name)
                if g >= 2:
                    act.wait_ge(sem("q_ready"), g - 1)
                act.activation(raw[:, g % 2, 0:T], bank[:, 0:T], ACT.Copy).then_inc(read(name), 1)

            def attention(layer):
                for i in range(HEADS + 2):
                    if i == GATES_AT:
                        for half in range(2):
                            name = ("gates", layer, half)
                            bank = filled(act, name)
                            to = gate[:, 4 + 2 * half:6 + 2 * half, :].rearrange("p j n -> p (j n)")
                            act.activation(to, bank[:, :], ACT.Silu).then_inc(read(name), 1)
                    if i < HEADS:
                        b = i % 4
                        moved(act, ("s", layer, i))
                        act.activation(prob[:, b, 0:P], prob[:, b, 0:P], ACT.Exp, bias=smin[:, b, 0:1],
                                       scale=-1.0, accum_out=ssum[:, b, 0:1]).then_inc(sem("exp_done"), 1)
                        act.activation(prob[:, b, P:3 * P], prob[:, b, P:3 * P], ACT.Exp, bias=smin[:, b, 1:2],
                                       scale=-1.0, accum_out=ssum[:, b, 1:2]).then_inc(sem("exp_done"), 1)
                    if i >= 2:
                        n = i - 2
                        name = ("pt", layer, n)
                        bank = filled(act, name)
                        if n >= 4:
                            filled(act, ("o", layer, (n - 4) // 2))
                        act.activation(prob_t[:, n % 4, :], bank[:, 0:3 * P], ACT.Copy).then_inc(read(name), 1)

            def out_norm(layer):
                for t in range(NT):
                    act.wait_ge(sem("moments_ready"), NT * layer + t + 1)
                    act.activation(stats[:, t, 14:15], stats[:, t, 13:14], ACT.Sqrt, bias=eps5) \
                        .then_inc(sem("row_deviation"), 1)

            def turned_back(t):
                name = ("back", t, 0)
                bank = filled(act, name)
                for j in range(KD // 2):
                    act.activation(xT[:, j, t * P:(t + 1) * P], bank[:, j * P:(j + 1) * P], ACT.Identity,
                                   bias=col("ln_b_2", j), scale=col("ln_g_2", j)).then_inc(read(name), 1)

            attention(0)
            act.dma_start(ac[:, A_COS:A_COS + B_COLS], A["k_moba"]).then_inc(sem("moba_in"), 16)
            out_norm(0)
            for t in range(NT):
                turned_back(t)
            for n in range(2):
                for j in range(KD):
                    name = ("raw", n, j)
                    bank = filled(act, name)
                    if n:
                        act.wait_ge(sem("turned"), j + 1)
                    act.activation(raw_b[:, j, :], bank[:, 0:T], ACT.Copy).then_inc(read(name), 1)
                for w in range(4):
                    name = ("gate", 1, w) if n else ("v2", w // 2, w % 2)
                    bank = filled(act, name)
                    if n:
                        act.activation(gate[:, w, :], bank[:, 0:T], ACT.Silu).then_inc(read(name), 1)
                    else:
                        act.activation(v[:, w // 2, (w % 2) * 512:(w % 2 + 1) * 512], bank[:, :], ACT.Copy) \
                            .then_inc(read(name), 1)
            attention(1)
            out_norm(1)

        @block.tensor
        def _(pe):
            pe.sem_inc(t_full, C_T)
            pe.wait_ge(sem("consts_in"), 16)
            pe.wait_ge(sem("x_in"), 16)
            for j in range(KD):
                bank = may_fill(pe, ("x", j))
                for t in range(NT):
                    mm = pe.transpose(bank[:, t * P:(t + 1) * P], x_tok[:, t, j * P:(j + 1) * P], ident)
                mm.then_inc(full(("x", j)), 1)
            pe.wait_ge(sem("rows_in"), 16 * (len(LOT0) + len(LOT1) + 2))
            bank = may_fill(pe, "par")
            for lot, n, at in ((0, LOT0_ROWS, 0), (1, LOT1_ROWS, LOT0_ROWS), (2, DW_ROWS, COL["dw"]),
                               (3, DW_ROWS, COL["dw"] + DW_ROWS)):
                mm = pe.transpose(bank[:, at:at + n], rows[0:n, lot, :], ident[0:n, 0:n])
            mm.then_inc(full("par"), 1)

            def total(name, src, tiles, ready):
                bank = may_fill(pe, name)
                for k in range(tiles):
                    ready(k)
                    mm = pe.matmul(bank[:, 0:T], ones, src[:, k, :], start=(k == 0), stop=(k == tiles - 1))
                mm.then_inc(full(name), 1)

            def project(name, w, lo, m, rhs, k0=0, n=T, at=0, part=0, tiles=KD, done=True, ready=None):
                bank = ps[use[name][0]]
                for k in range(tiles):
                    if ready:
                        ready(k)
                    mm = pe.matmul(bank[part:part + m, at:at + n], w[:, k, lo:lo + m], rhs[:, k0 + k, :],
                                   start=(k == 0), stop=(k == tiles - 1))
                if done:
                    mm.then_inc(full(name), 1)

            total("ms1", sq, KD, lambda k: pe.wait_ge(sem("squared0"), k + 1))

            def ada(g):
                pe.wait_ge(sem("c_ready"), 1)
                bank = may_fill(pe, ("ada", g))
                for i in range(4):
                    w = slot(arrived(pe, ("ada", 4 * g + i)))
                    for k in range(KD):
                        for c in range(4):
                            mm = pe.matmul(bank[32 * c:32 * c + 32, i * P:(i + 1) * P], cact[:, k, :],
                                           w[:, k, c * P:(c + 1) * P], start=(k == 0), stop=(k == KD - 1),
                                           skip_group_check=True)
                mm.then_inc(full(("ada", g)), 1)

            def ada_columns(g):
                bank = may_fill(pe, ("mod", g))
                moved(pe, ("ada", g))
                for i in range(4):
                    mm = pe.transpose(bank[:, i * P:(i + 1) * P], ada_rows[:, i * P:(i + 1) * P], ident)
                mm.then_inc(full(("mod", g)), 1)

            ada(0)
            ada_columns(0)

            def glu(j):
                w = slot(arrived(pe, ("glu", j // 2)))
                may_fill(pe, ("glu_a", j))
                project(("glu_a", j), w, (j % 2) * P, P, h,
                        ready=(lambda k: pe.wait_ge(sem("h_ready"), k + 1)) if j == 0 else None)
                may_fill(pe, ("glu_g", j))
                project(("glu_g", j), w, 256 + (j % 2) * P, P, h)

            def convolve(j):
                bank = may_fill(pe, ("conv", j // 2))
                pe.wait_ge(sem("u_edge"), 1)
                moved(pe, ("glu_a", j))
                for w in range(PE_TAPS):
                    made = j * PE_TAPS + w
                    pe.wait_ge(sem("diag_ready"), made + 1)
                    mm = pe.matmul(bank[:, (j % 2) * T:(j % 2 + 1) * T], diag[:, made % DIAGS, :],
                                   u[:, j, w:w + T], start=(w == 0), stop=(w == PE_TAPS - 1))
                    mm.then_inc(sem("diag_used"), 1)

            glu(0)
            for j in range(1, KD + 1):
                if j < KD:
                    glu(j)
                convolve(j - 1)
            ada(1)
            ada(2)
            ada_columns(1)
            ada_columns(2)
            total("mean1", y, KD, lambda k: moved(pe, ("conv", k // 2)))
            total("var1", sq, KD, lambda k: pe.wait_ge(sem("squared1"), k + 1))
            for n in range(2):
                w = slot(arrived(pe, ("proj1", n)))
                for j in range(4 * n, 4 * n + 4):
                    may_fill(pe, ("proj1", j))
                    project(("proj1", j), w, (j % 4) * P, P, h,
                            ready=(lambda k: pe.wait_ge(sem("act_ready"), k + 1)) if j == 0 else None)
            total("ms2", sq, KD, lambda k: pe.wait_ge(sem("squared2"), k + 1))

            pe.wait_ge(sem("router_in"), 64)
            bank = may_fill(pe, "logit_rows")
            for k in range(KD):
                pe.wait_ge(sem("h2_ready"), k + 1)
                pe.matmul(bank[0:CHOICES, 0:T], wr[:, k, :], h2[:, k, :], start=(k == 0), stop=False)
            for t in range(NT):
                mm = pe.matmul(bank[0:CHOICES, t * P:(t + 1) * P], brow[0:1, :], ones[0:1, :],
                               start=False, stop=(t == NT - 1))
            mm.then_inc(full("logit_rows"), 1)

            def token_major(t, half):
                name = ("h2tok", t, half)
                bank = may_fill(pe, name)
                for j in range(4):
                    mm = pe.transpose(bank[:, j * P:(j + 1) * P], h2[:, 4 * half + j, t * P:(t + 1) * P], ident)
                mm.then_inc(full(name), 1)

            token_major(0, 0)
            bank = may_fill(pe, "logit")
            moved(pe, "logit_rows")
            for t in range(NT):
                mm = pe.transpose(bank[:, t * 64:t * 64 + CHOICES], logit_rows[:, t * P:(t + 1) * P],
                                  ident[0:CHOICES, 0:CHOICES])
            mm.then_inc(full("logit"), 1)
            token_major(0, 1)
            token_major(1, 0)
            token_major(1, 1)

            def open_sums(n):
                pe.wait_ge(sem(f"bank{4 + n}_read"), BEFORE_EXPERTS[4 + n])
                pe.matmul(ACC[n][:, :], ones[0:1, :], y_e[0:1, :], start=True, stop=False, skip_group_check=True)

            pe.wait_ge(sem("zeros_ready"), 1)
            for n in (2, 3, 1):
                open_sums(n)
            pe.wait_ge(sem("chosen"), 1)
            pe.wait_ge(sem("route_in"), 16)
            bank = may_fill(pe, "rank")
            strict = rc[:, R_STRICT:R_STRICT + P]
            picked = small[:, 384:448].rearrange("p (t e) -> p t e", t=NT)
            pe.matmul(bank[:, 0:32], strict, picked[:, 0, :], start=True, stop=True)
            pe.matmul(bank[:, 32:64], ones, picked[:, 0, :], start=True, stop=False)
            pe.matmul(bank[:, 32:64], strict, picked[:, 1, :], start=False, stop=True)
            pe.matmul(bank[:, 64:96], ones, picked[:, 0, :], start=True, stop=False)
            pe.matmul(bank[:, 64:96], ones, picked[:, 1, :], start=False, stop=True).then_inc(full("rank"), 1)
            open_sums(0)
            for j in range(KD):
                name = ("gather", j)
                bank = may_fill(pe, name)
                for t in range(NT):
                    pe.wait_ge(sem("sel_ready"), t + 1)
                    moved(pe, ("h2tok", t, j // 4))
                    mm = pe.matmul(bank[:, :], h2_tok[:, t, j * P:(j + 1) * P], sel[:, t, :],
                                   start=(t == 0), stop=(t == NT - 1))
                mm.then_inc(full(name), 1)
            for b in range(4):
                if BEFORE_EXPERTS[b]:
                    pe.wait_ge(sem(f"bank{b}_read"), BEFORE_EXPERTS[b])

            def gate_up(b, wu, wg):
                for k in range(KD):
                    for half, w in ((0, wu), (1, wg)):
                        mm = pe.matmul(GU_BANK[half * WIN:(half + 1) * WIN, :], xw[b][:, k, :], w[:, k, :],
                                       start=(k == 0), stop=(k == KD - 1), skip_group_check=True)
                return mm

            def turn(b):
                for t in range(NT):
                    lo = KF * WIN + t * P
                    pe.transpose(T_BANK[:, lo:lo + P], weighted[b][:, t, :], ident)
                for f in range(KF):
                    mm = pe.transpose(T_BANK[:, f * WIN:(f + 1) * WIN], hid[:, f * P:(f + 1) * P],
                                      ident[0:WIN, 0:WIN])
                return mm

            def down(b, w):
                for f in range(KF):
                    for half in range(2):
                        mm = pe.matmul(Y_BANK[half * WIN:(half + 1) * WIN, :], hid_t[b][:, f, :],
                                       w[:, f, half * 512:(half + 1) * 512], start=(f == 0), stop=(f == KF - 1),
                                       skip_group_check=True)
                return mm

            def combine(b):
                for j in range(4):
                    for half in range(2):
                        rows_ = slice(half * WIN, (half + 1) * WIN)
                        mm = pe.matmul(ACC[2 * half + j // 2][:, (j % 2) * T:(j % 2 + 1) * T],
                                       y_e[rows_, j * P:(j + 1) * P], comb[b][rows_, :],
                                       start=False, stop=False, skip_group_check=True)
                return mm

            def begin(e, b, uses, first=False):
                pe.wait_ge(win_ready, e + 1)
                pe.wait_ge(sem(f"slot{3 * b}"), uses(3 * b, 0))
                pe.wait_ge(sem(f"slot{3 * b + 1}"), uses(3 * b + 1, 0))
                if not first:
                    pe.wait_ge(hid_ready, e)
                gate_up(b, slot(3 * b + 1), slot(3 * b)).then_inc(gu_full, 1)

            def finish(e, b, uses, second=False):
                b1, b2 = (b - 1) % BODY, (b - 2) % BODY
                pe.wait_ge(hid_ready, e)
                turn(b1).then_inc(t_full, 1)
                if not second:
                    pe.wait_ge(y_moved, e - 1)
                    combine(b2)
                pe.wait_ge(sem(f"slot{3 * b1 + 2}"), uses(3 * b1 + 2, -1 if b == 0 else 0))
                pe.wait_ge(t_moved, e)
                down(b1, slot(3 * b1 + 2, KF, D)).then_inc(y_full, 1)

            def last_uses(s, back):
                return (LOOPS + 1 + back) * 16 + EXPERT_BASE[s]

            for e in range(BODY):
                begin(e, e, lambda s, back: EXPERT_BASE[s] + 16, first=e == 0)
                if e:
                    finish(e, e, lambda s, back: EXPERT_BASE[s] + 16, second=e == 1)
            with pe.Fori(1, LOOPS) as it:
                for b in range(BODY):
                    for part in (begin, finish):
                        part(it * BODY + b, b, lambda s, back: it * 16 + (EXPERT_BASE[s] + 16 + 16 * back))
            for b in range(PEELED):
                e = LOOPS * BODY + b
                finish(e, b, last_uses)
                begin(e, b, last_uses)
            more = overflow(pe)
            finish(EXPERTS, EXPERTS % BODY, last_uses)
            pe.wait_ge(y_moved, EXPERTS)
            combine((EXPERTS - 1) % BODY).then_inc(sem("combined"), 1)
            with pe.If(more):
                with pe.Fori(0, EXPERTS) as e:
                    pe.wait_ge(sem("over_in"), e * 48 + 48)
                    for r in range(3):
                        n = e * 3 + (r + 1)
                        pe.wait_ge(sem("over_window"), n)
                        gate_up(0, slot(1), slot(0)).then_inc(sem("over_gate_up"), 1)
                        pe.wait_ge(sem("over_hidden"), n)
                        turn(0).then_inc(sem("over_turned"), 1)
                        pe.wait_ge(sem("over_turned_moved"), n)
                        down(0, slot(2, KF, D)).then_inc(sem("over_down"), 1)
                        pe.wait_ge(sem("over_down_moved"), n)
                        combine(0).then_inc(sem("over_done"), 1)

            total("ms3", sq2, KD, lambda k: pe.wait_ge(sem("squared3"), k + 1))
            for n in range(2):
                w = slot(arrived(pe, ("cq", n)))
                for j in range(4 * n, 4 * n + 4):
                    may_fill(pe, ("cq", j))
                    project(("cq", j), w, (j % 4) * P, P, xT,
                            ready=(lambda k: pe.wait_ge(sem("x_normed"), k + 1)) if j == 0 else None)
            total("msq", sq2, KQ, lambda k: pe.wait_ge(sem("squared5"), k + 1))
            bank = may_fill(pe, "mskv")
            for k in range(KKV):
                pe.wait_ge(sem("squared5"), KQ + k + 1)
                mm = pe.matmul(bank[:, 0:T], ones, sq2[:, KQ + k, :], start=(k == 0), stop=(k == KKV - 1))
            mm.then_inc(full("mskv"), 1)
            pe.wait_ge(sem("wrope_in"), 16)
            may_fill(pe, "krope")
            project("krope", wrope, 0, ROPE, xT, part=NOPE)
            w = slot(arrived(pe, ("gate", 0, 0)))
            for j in range(4):
                may_fill(pe, ("gate", 0, j))
                project(("gate", 0, j), w, j * P, P, xT)
            w = slot(arrived(pe, "ukv"), KKV, 2048)
            wv = w.rearrange("p k (h c) -> p k h c", c=P)
            for t in range(NT):
                for n in range(2):
                    name = ("v1", t, n)
                    bank = may_fill(pe, name)
                    for k in range(KKV):
                        pe.wait_ge(sem("latent_ready"), KQ + k + 1)
                        mm = pe.matmul(bank[:, :].rearrange("p (h c) -> p h c", c=HD), cq[:, KQ + k, t * P:(t + 1) * P], wv[:, k, 8 * n:8 * n + 8, NOPE:P],
                                       start=(k == 0), stop=(k == KKV - 1))
                    mm.then_inc(full(name), 1)

            def pairs(name, w, heads, lo, rhs, k0, tiles):
                bank = may_fill(pe, name)
                for c in range(2):
                    for k in range(tiles):
                        for half in range(2):
                            mm = pe.matmul(bank[half * NOPE:(half + 1) * NOPE, c * T:(c + 1) * T],
                                           w[:, k, heads + 2 * c + half, lo:lo + NOPE], rhs[:, k0 + k, :],
                                           start=(k == 0), stop=(k == tiles - 1), skip_group_check=True)
                mm.then_inc(full(name), 1)

            for g in range(HEADS // 4):
                pairs(("kn", g), wv, 4 * g, 0, cq, KQ, KKV)
            for g in range(HEADS // 4):
                w = slot(arrived(pe, ("uq", g)), KQ, 384).rearrange("p k (h c) -> p k h c", c=QK)
                pairs(("qn", g), w, 0, 0, cq, 0, KQ)
                name = ("qr", g)
                bank = may_fill(pe, name)
                for k in range(KQ):
                    for c in range(4):
                        mm = pe.matmul(bank[ROPE * c:ROPE * (c + 1), 0:T], w[:, k, c, NOPE:QK], cq[:, k, :],
                                       start=(k == 0), stop=(k == KQ - 1), skip_group_check=True)
                mm.then_inc(full(name), 1)

            def more_gates(layer, w, i):
                tile = i // 3
                name = ("gates", layer, tile // 2)
                bank = may_fill(pe, name) if i % 6 == 0 else ps[use[name][0]]
                for k in range(3 * (i % 3), min(3 * (i % 3) + 3, KD)):
                    mm = pe.matmul(bank[:, (tile % 2) * T:(tile % 2 + 1) * T], w[:, k, tile * P:(tile + 1) * P],
                                   xT[:, k, :], start=(k == 0), stop=(k == KD - 1), skip_group_check=True)
                if i % 6 == 5:
                    mm.then_inc(full(name), 1)

            def attention(layer, q_of, k_of, ready, w):
                for i in range(HEADS + 3):
                    if i < HEADS:
                        ready(i)
                        name = ("s", layer, i)
                        bank = may_fill(pe, name)
                        q, k = q_of(i), k_of(i)
                        pe.matmul(bank[:, 0:P], q[:, 0:P], k[:, 0:P], start=True, stop=True)
                        pe.matmul(bank[:, P:3 * P], q[:, P:T], k[:, 0:T], start=True, stop=True) \
                            .then_inc(full(name), 1)
                    if i < 12:
                        more_gates(layer, w, i)
                    if 0 <= i - 2 < HEADS:
                        n = i - 2
                        name = ("pt", layer, n)
                        bank = may_fill(pe, name)
                        pe.wait_ge(sem("probs_ready"), HEADS * layer + n + 1)
                        for c in range(3):
                            mm = pe.transpose(bank[:, c * P:(c + 1) * P], prob[:, n % 4, c * P:(c + 1) * P], ident)
                        mm.then_inc(full(name), 1)
                    if i >= 3:
                        n = i - 3
                        name = ("o", layer, n // 2)
                        at = HD * (n % 2)
                        bank = may_fill(pe, name) if n % 2 == 0 else ps[use[name][0]]
                        moved(pe, ("pt", layer, n))
                        pe.matmul(bank[at:at + HD, 0:T], v[:, 0, n * HD:(n + 1) * HD], prob_t[:, n % 4, 0:T],
                                  start=True, stop=False, skip_group_check=True)
                        mm = pe.matmul(bank[at:at + HD, P:T], v[:, 1, n * HD:(n + 1) * HD],
                                       prob_t[:, n % 4, T:3 * P], start=False, stop=True, skip_group_check=True)
                        if n % 2:
                            mm.then_inc(full(name), 1)
                    if layer == 0 and 0 <= i - ROWS_AT < 2 * NT:
                        t, half = divmod(i - ROWS_AT, 2)
                        name = ("rows", t, half)
                        bank = may_fill(pe, name)
                        for j in range(4):
                            mm = pe.transpose(bank[:, j * P:(j + 1) * P], xT[:, 4 * half + j, t * P:(t + 1) * P], ident)
                        mm.then_inc(full(name), 1)

            def out_layer(layer):
                ws = [slot(arrived(pe, ("wo", layer, half))) for half in range(2)]
                for t in range(NT):
                    for half in range(2):
                        name = ("out", layer, t, half)
                        bank = may_fill(pe, name)
                        for k in range(KD):
                            if t == half == 0:
                                moved(pe, ("o", layer, k))
                            mm = pe.matmul(bank[:, :], o[:, k, t * P:(t + 1) * P], ws[half][:, k, :],
                                           start=(k == 0), stop=(k == KD - 1))
                        mm.then_inc(full(name), 1)
                        if layer == 0 and t == 1:
                            turn_back(half)

            def turn_back(t):
                pe.wait_ge(sem("row_normed"), t + 1)
                for half in range(2):
                    name = ("back", t, half)
                    bank = may_fill(pe, name)
                    for j in range(4):
                        mm = pe.transpose(bank[:, j * P:(j + 1) * P],
                                          x_rows[:, t, (4 * half + j) * P:(4 * half + j + 1) * P], ident)
                    mm.then_inc(full(name), 1)

            def ready_a(i):
                if i == 0:
                    pe.wait_ge(sem("krope_spread"), 1)
                    for g in range(HEADS // 4):
                        moved(pe, ("kn", g))
                    pe.wait_ge(sem("mla_in"), 16)
                    for t in range(NT):
                        for n in range(2):
                            moved(pe, ("v1", t, n))
                moved(pe, ("qn", i // 4))
                pe.wait_ge(sem("q_ready"), i // 4 + 1)

            attention(0, lambda i: qh[0:QK, i, :], lambda i: kh[0:QK, i, :], ready_a,
                      slot(arrived(pe, ("gate", 0, 1))))
            out_layer(0)

            def layer_ready(k):
                for t in range(NT):
                    partly_moved(pe, ("back", t, k // 4), k % 4 + 1)

            for n, kind in enumerate(("kv", "in")):
                for j in range(KD):
                    if j % 4 == 0:
                        w = slot(arrived(pe, (kind, j // 4)))
                    may_fill(pe, ("raw", n, j))
                    project(("raw", n, j), w, (j % 4) * P, P, xT,
                            ready=layer_ready if n == j == 0 else None)
                if n == 0:
                    ws = [slot(arrived(pe, (kind, 2))), slot(arrived(pe, (kind, 3)))]
                    for t in range(NT):
                        for half in range(2):
                            name = ("v2", t, half)
                            bank = may_fill(pe, name)
                            for k in range(KD):
                                mm = pe.matmul(bank[:, :], xT[:, k, t * P:(t + 1) * P], ws[half][:, k, :],
                                               start=(k == 0), stop=(k == KD - 1))
                            mm.then_inc(full(name), 1)
                else:
                    w = slot(arrived(pe, (kind, 2)))
                    for j in range(4):
                        may_fill(pe, ("gate", 1, j))
                        project(("gate", 1, j), w, j * P, P, xT)

            def ready_b(i):
                if i == 0:
                    for t in range(NT):
                        for n in range(2):
                            moved(pe, ("v2", t, n))
                pe.wait_ge(sem("turned"), KD + i // 2 + 1)

            attention(1, lambda i: qb[HD * (i % 2):HD * (i % 2) + HD, i // 2, :],
                      lambda i: kb[HD * (i % 2):HD * (i % 2) + HD, i // 2, :], ready_b,
                      slot(arrived(pe, ("in", 3))))
            out_layer(1)

        @block.vector
        def _(dve):
            steps = [0]

            def then(ins):
                steps[0] += 1
                ins.then_inc(sem("vector_step"), 1)
                dve.wait_ge(sem("vector_step"), steps[0])

            rstd_count = [0]

            def inverse(name, parked):
                moved(dve, name)
                dve.reciprocal(parked, std if name in ("ms1", "var1", "ms2") else std2) \
                    .then_inc(sem("rstd_ready"), 1)
                rstd_count[0] += 1
                dve.wait_ge(sem("rstd_ready"), rstd_count[0])
                return parked

            def rstd_of(name):
                return inverse(name, ps[use[name][0]][:, T:2 * T])

            dve.memset(eps6, EPS).then_inc(sem("eps_ready"), 1)
            dve.memset(eps5, LN_EPS).then_inc(sem("eps_ready"), 1)
            for j in range(KD):
                bank = filled(dve, ("x", j))
                dve.tensor_copy(xT[:, j, :], bank[:, 0:T]).then_inc(read(("x", j)), 1)
            bank = filled(dve, "par")
            dve.tensor_copy(par[:, :], bank[:, 0:PAR]).then_inc(read("par"), 1)
            rstd = rstd_of("ms1")
            dve.memset(u[:, :, 0:TAPS - 1], 0.0).then_inc(sem("u_edge"), 1)
            moved(dve, "par")

            def ada_row(g):
                bank = filled(dve, ("ada", g))
                dve.tensor_copy(ada_rows, bank[:, :]).then_inc(read(("ada", g)), 1)

            def modulation(g):
                bank = filled(dve, ("mod", g))
                dve.tensor_tensor(mod[:, 16 * g:16 * g + 16].rearrange("p (i c) -> p i c", i=4),
                                  bank[:, :].rearrange("p (i c n) -> p i c n", i=4, c=4)[:, :, :, 0],
                                  par[:, 16 * g:16 * g + 16].rearrange("p (i c) -> p i c", i=4),
                                  ALU.add).then_inc(read(("mod", g)), 1)
                moved(dve, ("mod", g))

            ada_row(0)
            modulation(0)
            then(dve.scalar_tensor_tensor(out=a1, in0=mod[:, 8:16], scalar=1.0,
                                          in1=par[:, COL["norm_mix_g"]:COL["norm_mix_g"] + 8],
                                          op0=ALU.add, op1=ALU.mult))
            for j in range(KD):
                moved(dve, ("x", j))
                dve.scalar_tensor_tensor(out=h[:, j, :], in0=xT[:, j, :], scalar=a1[:, j:j + 1], in1=rstd,
                                         op0=ALU.mult, op1=ALU.mult).then_inc(sem("h_scaled"), 1)

            def merge_glu(j):
                bank = filled(dve, ("glu_a", j))
                moved(dve, ("glu_g", j))
                dve.scalar_tensor_tensor(out=u[:, j, TAPS - 1:], in0=bank[:, 0:T], scalar=col("conv_b_in", j),
                                         in1=sg[:, j % 4, :], op0=ALU.add, op1=ALU.mult) \
                    .then_inc(read(("glu_a", j)), 1)

            taps = TAPS - PE_TAPS

            def tap(pair, first_tap, last_tap):
                bank = ps[use[("conv", pair)][0]]
                for w in range(first_tap, last_tap):
                    for c in range(2):
                        j = 2 * pair + c
                        if w == 0:
                            moved(dve, ("glu_a", j))
                            dve.wait_ge(sem("diag_used"), PE_TAPS * (2 * pair + 2))
                        else:
                            dve.wait_ge(sem("tap_done"), pair * 2 * (taps - 1) + 2 * (w - 1) + c + 1)
                        done = sem("conv_done") if w == taps - 1 else sem("tap_done")
                        to = bank[:, c * T:(c + 1) * T]
                        dve.scalar_tensor_tensor(out=to, in0=u[:, j, PE_TAPS + w:PE_TAPS + w + T],
                                                 scalar=col("dw", (PE_TAPS + w) * KD + j), in1=to,
                                                 op0=ALU.mult, op1=ALU.add).then_inc(done, 1)

            dve.wait_ge(sem("u_edge"), 1)
            merge_glu(0)
            merge_glu(1)
            for pair in range(KD // 2):
                if pair < KD // 2 - 1:
                    merge_glu(2 * pair + 2)
                    tap(pair, 0, taps // 2)
                    merge_glu(2 * pair + 3)
                    tap(pair, taps // 2, taps)
                else:
                    tap(pair, 0, taps * 2 // 3)
                    ada_row(1)
                    tap(pair, taps * 2 // 3, taps)
            modulation(1)
            ada_row(2)
            modulation(2)
            then(dve.scalar_tensor_tensor(out=a2, in0=mod[:, 32:40], scalar=1.0,
                                          in1=par[:, COL["norm_ffn_g"]:COL["norm_ffn_g"] + 8],
                                          op0=ALU.add, op1=ALU.mult))
            bank = filled(dve, "mean1")
            for j in range(KD):
                moved(dve, ("conv", j // 2))
                dve.scalar_tensor_tensor(out=y[:, j, :], in0=bank[:, 0:T], scalar=-1.0 / D, in1=y[:, j, :],
                                         op0=ALU.mult, op1=ALU.add).then_inc(sem("centred1"), 1)
            dve.wait_ge(sem("centred1"), KD)
            rstd = rstd_of("var1")
            for j in range(KD):
                dve.scalar_tensor_tensor(out=y[:, j, :], in0=y[:, j, :], scalar=col("conv_ln_g", j), in1=rstd,
                                         op0=ALU.mult, op1=ALU.mult).then_inc(sem("normed1"), 1)
            for j in range(KD):
                bank = filled(dve, ("proj1", j))
                dve.scalar_tensor_tensor(out=xT[:, j, :], in0=bank[:, 0:T], scalar=mod[:, 16 + j:17 + j],
                                         in1=xT[:, j, :], op0=ALU.mult, op1=ALU.add) \
                    .then_inc(read(("proj1", j)), 1)
            rstd = rstd_of("ms2")
            for j in range(KD):
                moved(dve, ("proj1", j))
                dve.scalar_tensor_tensor(out=scaled[:, j, :], in0=xT[:, j, :], scalar=a2[:, j:j + 1], in1=rstd,
                                         op0=ALU.mult, op1=ALU.mult).then_inc(sem("h2_scaled"), 1)

            def tmp(at, n, e):
                return small[:, at:at + n * e].rearrange("p (t e) -> p t e", t=n)

            def wide(a, n):
                return a.unsqueeze(2).broadcast_to((P, NT, n))

            iota32 = rc[:, R_IOTA32:R_IOTA32 + EXPERTS]
            bank = filled(dve, "logit_rows")
            dve.tensor_copy(logit_rows, bank[0:CHOICES, 0:T]).then_inc(read("logit_rows"), 1)
            bank = filled(dve, "logit")
            dve.wait_ge(sem("route_in"), 16)
            logit = tmp(0, NT, CHOICES)
            dve.tensor_copy(logit, bank[:, 0:128].rearrange("p (t e) -> p t e", t=NT)[:, :, 0:CHOICES]) \
                .then_inc(read("logit"), 1)
            moved(dve, "logit")
            gmax, m1, m2, mn = small[:, 72:74], small[:, 74:76], small[:, 76:78], small[:, 78:80]

            def first_max(values, n, most, flags, cand, picked):
                then(dve.tensor_reduce(most, values, AX.X, ALU.max))
                then(dve.tensor_tensor(flags, values, wide(most, n), ALU.is_equal))
                for t in range(NT):
                    ins = dve.scalar_tensor_tensor(out=cand[:, t, :], in0=flags[:, t, :], scalar=-64.0,
                                                   in1=iota32[:, 0:n], op0=ALU.mult, op1=ALU.add)
                    if t < NT - 1:
                        ins.then_inc(sem("first_half"), 1)
                        first[0] += 1
                then(ins)
                dve.wait_ge(sem("first_half"), first[0])
                then(dve.tensor_reduce(mn, cand, AX.X, ALU.min))
                then(dve.tensor_tensor(picked, cand, wide(mn, n), ALU.is_equal))

            first = [0]
            flags, cand = tmp(128, NT, 32), tmp(192, NT, 32)
            oh1, oh2, picked, em = tmp(256, NT, 32), tmp(320, NT, 32), tmp(384, NT, 32), tmp(448, NT, 32)
            glog, elog = logit[:, :, 0:GROUPS], logit[:, :, GROUPS:CHOICES]
            ohg, gflag, gcand = tmp(96, NT, 4), tmp(104, NT, 4), tmp(112, NT, 4)
            first_max(glog, GROUPS, gmax, gflag, gcand, ohg)
            dve.tensor_tensor(tmp(80, NT, 4), glog, wide(gmax, 4), ALU.subtract).then_inc(sem("group_shifted"), 1)
            pen = tmp(120, NT, 4)
            then(dve.tensor_scalar(pen, ohg, BIG, -BIG, ALU.mult, ALU.add))
            for t in range(NT):
                then(dve.tensor_tensor(em[:, t, :].rearrange("p (g e) -> p g e", g=GROUPS),
                                       elog[:, t, :].rearrange("p (g e) -> p g e", g=GROUPS),
                                       pen[:, t, :].unsqueeze(2).broadcast_to((P, GROUPS, PER_GROUP)), ALU.add))
            first_max(em, EXPERTS, m1, flags, cand, oh1)
            then(dve.scalar_tensor_tensor(out=em.rearrange("p t e -> p (t e)"),
                                          in0=oh1.rearrange("p t e -> p (t e)"), scalar=-3 * BIG,
                                          in1=em.rearrange("p t e -> p (t e)"), op0=ALU.mult, op1=ALU.add))
            first_max(em, EXPERTS, m2, flags, cand, oh2)
            dve.tensor_tensor(picked, oh1, oh2, ALU.add).then_inc(sem("chosen"), 1)
            dve.tensor_tensor(small[:, 88:90], m2, m1, ALU.subtract).then_inc(sem("pair_shifted"), 1)
            dve.wait_ge(sem("group_exp"), 1)
            gsum, gp, es, w1, w2 = (small[:, 520:522], small[:, 522:524], small[:, 524:526],
                                    small[:, S_W1:S_W1 + 2], small[:, S_W2:S_W2 + 2])
            then(dve.tensor_reduce(gsum, tmp(80, NT, 4), AX.X, ALU.add))
            then(dve.reciprocal(gp, gsum))
            dve.wait_ge(sem("pair_exp"), 1)
            then(dve.tensor_scalar(es, small[:, 88:90], 1.0, None, ALU.add))
            then(dve.reciprocal(es, es))
            then(dve.tensor_tensor(w1, es, gp, ALU.mult))
            then(dve.tensor_tensor(w2, w1, small[:, 88:90], ALU.mult))
            bank = filled(dve, "rank")
            cnt = small[:, 530:562]
            incl, start = small[:, 562:594], small[:, 594:626]
            then(dve.tensor_copy(cnt, bank[:, 64:96]))
            then(dve.tensor_tensor_scan(incl, ones[:, 0:EXPERTS], cnt, 0.0, ALU.mult, ALU.add))
            then(dve.tensor_tensor(start, incl, cnt, ALU.subtract))
            pos = tmp(640, NT, 32)
            dve.tensor_tensor(pos, bank[:, 0:64].rearrange("p (t e) -> p t e", t=NT),
                              start.unsqueeze(1).broadcast_to((P, NT, EXPERTS)), ALU.add).then_inc(read("rank"), 1)
            moved(dve, "rank")
            then(dve.tensor_tensor(flags, oh1, pos, ALU.mult))
            then(dve.tensor_reduce(small[:, S_P1:S_P1 + 2], flags, AX.X, ALU.add))
            then(dve.tensor_tensor(flags, oh2, pos, ALU.mult))
            dve.tensor_reduce(small[:, S_P2:S_P2 + 2], flags, AX.X, ALU.add).then_inc(sem("slots_known"), 1)
            dve.wait_ge(sem("slots_known"), 1)
            iota = rc[:, R_IOTA:R_IOTA + SLOTS_A]
            for t in range(NT):
                then(dve.tensor_scalar(sel[:, t, :], iota, small[:, S_P1 + t:S_P1 + t + 1], None, ALU.is_equal))
                dve.scalar_tensor_tensor(out=sel[:, t, :], in0=iota, scalar=small[:, S_P2 + t:S_P2 + t + 1],
                                         in1=sel[:, t, :], op0=ALU.is_equal, op1=ALU.add) \
                    .then_inc(sem("sel_ready"), 1)
            for t in range(NT):
                then(dve.tensor_scalar(em[:, t, :], oh1[:, t, :], w1[:, t:t + 1], None, ALU.mult))
                then(dve.scalar_tensor_tensor(out=em[:, t, :], in0=oh2[:, t, :], scalar=w2[:, t:t + 1],
                                              in1=em[:, t, :], op0=ALU.mult, op1=ALU.add))
            then(dve.tensor_tensor(pos, pos, start.unsqueeze(1).broadcast_to((P, NT, EXPERTS)), ALU.subtract))
            then(dve.scalar_tensor_tensor(out=pos.rearrange("p t e -> p (t e)"),
                                          in0=pos.rearrange("p t e -> p (t e)"), scalar=1.0,
                                          in1=picked.rearrange("p t e -> p (t e)"), op0=ALU.add, op1=ALU.mult))
            for r in range(4):
                if r < 3:
                    then(dve.tensor_copy(small[:, P * r + 64:P * r + 128], small[:, 448:512]))
                then(dve.tensor_scalar(small[:, P * r:P * r + 64], pos.rearrange("p t e -> p (t e)"),
                                       -1.0 - WIN * r, None, ALU.add))
            row = tmp(740, 1, 132)[0:1, 0, :]
            then(dve.tensor_copy(row[:, 0:EXPERTS], start[0:1, :]))
            then(dve.memset(row[:, EXPERTS:EXPERTS + 4], 0.0))
            then(dve.tensor_reduce(row[:, EXPERTS:EXPERTS + 1], cnt[0:1, :], AX.X, ALU.max))
            for r in range(1, 4):
                lo = EXPERTS + 4 + EXPERTS * (r - 1)
                then(dve.tensor_scalar(row[:, lo:lo + EXPERTS], start[0:1, :], float(WIN * r), float(NOWHERE),
                                       ALU.add, ALU.min))
            dve.tensor_copy(table[0:1, :], row).then_inc(sem("table_ready"), 1)
            for j in range(1, KD, 2):
                bank = filled(dve, ("gather", j))
                dve.tensor_copy(xg[:, j, 0:SLOTS_A], bank[:, :]).then_inc(read(("gather", j)), 1)

            def gated(done):
                dve.tensor_tensor(hid, GU_BANK[0:WIN, :], silu_g, ALU.mult).then_inc(done, 1)

            def move_result(done):
                dve.tensor_copy(y_e, Y_BANK[:, :]).then_inc(done, 1)

            dve.wait_ge(silu_done, 1)
            gated(hid_ready)
            with dve.Fori(1, EXPERTS) as e:
                dve.wait_ge(silu_done, e + 1)
                dve.wait_ge(t_full, e + C_T)
                gated(hid_ready)
                dve.wait_ge(y_full, e)
                move_result(y_moved)
            more = overflow(dve)
            dve.wait_ge(y_full, EXPERTS)
            move_result(y_moved)
            dve.wait_ge(sem("combined"), 1)
            with dve.If(more):
                with dve.Fori(0, 3 * EXPERTS) as n:
                    dve.wait_ge(sem("over_silu"), n + 1)
                    gated(sem("over_hidden"))
                    dve.wait_ge(sem("over_down"), n + 1)
                    move_result(sem("over_down_moved"))
                dve.wait_ge(sem("over_done"), 3 * EXPERTS + 1)
            for j in range(KD):
                bank = ACC[j // 2]
                dve.scalar_tensor_tensor(out=xT[:, j, :], in0=bank[:, (j % 2) * T:(j % 2 + 1) * T],
                                         scalar=mod[:, 40 + j:41 + j], in1=xT[:, j, :],
                                         op0=ALU.mult, op1=ALU.add).then_inc(read(("acc", j // 2)), 1)
            rstd = rstd_of("ms3")
            for j in range(KD):
                moved(dve, ("acc", j // 2))
                dve.scalar_tensor_tensor(out=xT[:, j, :], in0=xT[:, j, :], scalar=col("final_g", j), in1=rstd,
                                         op0=ALU.mult, op1=ALU.mult).then_inc(sem("x_normed"), 1)

            for j in range(KQ + KKV):
                bank = filled(dve, ("cq", j))
                dve.tensor_copy(cq[:, j, :], bank[:, 0:T]).then_inc(read(("cq", j)), 1)
            rq = rstd_of("msq")
            for j in range(KQ):
                moved(dve, ("cq", j))
                dve.scalar_tensor_tensor(out=cq[:, j, :], in0=cq[:, j, :], scalar=col("mla_q_norm_2", j), in1=rq,
                                         op0=ALU.mult, op1=ALU.mult).then_inc(sem("latent_ready"), 1)
            rkv = rstd_of("mskv")
            for j in range(KKV):
                moved(dve, ("cq", KQ + j))
                dve.scalar_tensor_tensor(out=cq[:, KQ + j, :], in0=cq[:, KQ + j, :],
                                         scalar=col("mla_kv_norm_2", j), in1=rkv,
                                         op0=ALU.mult, op1=ALU.mult).then_inc(sem("latent_ready"), 1)
            swap = [(i + ROPE // 2) % ROPE for i in range(ROPE)]
            cosA = ac[NOPE:QK, A_COS:A_COS + T]
            sinA = ac[NOPE:QK, A_SIN:A_SIN + T]
            dve.wait_ge(sem("mla_in"), 16)
            moved(dve, "krope")
            k_raw, k_turn = raw[NOPE:QK, 3, 0:T], raw[NOPE:QK, 3, T:2 * T]
            then(dve.stream_shuffle(k_turn, k_raw, swap))
            then(dve.tensor_tensor(k_turn, k_turn, sinA, ALU.mult))
            then(dve.tensor_tensor(k_raw, k_raw, cosA, ALU.mult))
            dve.tensor_tensor(k_raw, k_raw, k_turn, ALU.add).then_inc(sem("krope_ready"), 1)
            for t in range(NT):
                name = ("v1", t, 1)
                bank = filled(dve, name)
                dve.tensor_copy(v[:, t, 512:D], bank[:, :]).then_inc(read(name), 1)
            for g in range(HEADS // 4):
                name = ("kn", g)
                bank = filled(dve, name)
                dve.tensor_copy(kh[0:NOPE, 4 * g + 1:4 * g + 4:2, :],
                                bank[NOPE:2 * NOPE, :].rearrange("p (h n) -> p h n", h=2)).then_inc(read(name), 1)
            for g in range(HEADS // 4):
                name = ("qn", g)
                bank = filled(dve, name)
                dve.tensor_copy(qh[0:NOPE, 4 * g + 1:4 * g + 4:2, :],
                                bank[NOPE:2 * NOPE, :].rearrange("p (h n) -> p h n", h=2)).then_inc(read(name), 1)
                moved(dve, ("qr", g))
                q, turn = raw[:, g % 2, 0:T], raw[:, g % 2, T:2 * T]
                dve.stream_shuffle(turn, q, swap).then_inc(sem("q_shuffled"), 1)
                dve.wait_ge(sem("q_shuffled"), g + 1)
                then(dve.tensor_tensor(turn, turn, ac[:, A_SIN:A_SIN + T], ALU.mult))
                dve.wait_ge(sem("q_cos"), g + 1)
                for c in range(4):
                    part = slice(ROPE * c, ROPE * (c + 1))
                    ins = dve.tensor_tensor(qh[NOPE:QK, 4 * g + c, :], q[part], turn[part], ALU.add)
                ins.then_inc(sem("q_ready"), 1)

            mask = ac[:, A_MASK:A_MASK + T]

            def attention(layer, scale):
                for i in range(HEADS + 4):
                    if i < HEADS:
                        b = i % 4
                        name = ("s", layer, i)
                        bank = filled(dve, name)
                        if i >= 4:
                            filled(dve, ("pt", layer, i - 4))
                        dve.tensor_tensor_reduce(out=prob[:, b, 0:P], in0=bank[:, 0:P], in1=mask[:, P:T],
                                                 scale=-scale, scalar=3e38, op0=ALU.add, op1=ALU.min,
                                                 accum_out=smin[:, b, 0:1]).then_inc(sem("scores_part"), 1)
                        dve.wait_ge(sem("scores_part"), HEADS * layer + i + 1)
                        dve.tensor_tensor_reduce(out=prob[:, b, P:3 * P], in0=bank[:, P:3 * P], in1=mask,
                                                 scale=-scale, scalar=3e38, op0=ALU.add, op1=ALU.min,
                                                 accum_out=smin[:, b, 1:2]).then_inc(read(name), 1)
                    if 1 <= i <= HEADS:
                        b = (i - 1) % 4
                        dve.wait_ge(sem("exp_done"), 2 * (HEADS * layer + i))
                        dve.reciprocal(srec[:, b, :], ssum[:, b, :]).then_inc(sem("sum_inverse"), 1)
                    if i >= 5 and (i - 5) % 2 == 0 and (i - 5) // 2 < HEADS // 2:
                        merge(layer, (i - 5) // 2)
                    if layer == 0 and 0 <= i - ROWS_AT - 1 < 2 * NT:
                        t, half = divmod(i - ROWS_AT - 1, 2)
                        bank = filled(dve, ("rows", t, half))
                        dve.tensor_copy(x_rows[:, t, half * 512:(half + 1) * 512], bank[:, :]) \
                            .then_inc(read(("rows", t, half)), 1)

            def merge(layer, p):
                name = ("o", layer, p)
                bank = filled(dve, name)
                moved(dve, ("gate", layer, p) if p < 4 else ("gates", layer, (p - 4) // 2))
                dve.tensor_tensor(o[:, p, :], bank[:, 0:T], gate[:, p, :], ALU.mult).then_inc(read(name), 1)

            def out_norm(layer):
                for t in range(NT):
                    for half in range(2):
                        name = ("out", layer, t, half)
                        if layer == 0:
                            moved(dve, ("rows", t, half))
                        elif half == 0:
                            dve.wait_ge(sem("rows_shifted"), t + 1)
                        bank = filled(dve, name)
                        x = x_rows[:, t, half * 512:(half + 1) * 512]
                        dve.scalar_tensor_tensor(out=x, in0=x, scalar=ALPHA, in1=bank[:, :],
                                                 op0=ALU.mult, op1=ALU.add).then_inc(read(name), 1)
                        moved(dve, name)
                        then(dve.bn_stats(stats[:, t, 6 * half:6 * half + 6], x))
                    dve.bn_aggr(stats[:, t, 12:14], stats[:, t, 0:12]).then_inc(sem("moments_ready"), 1)
                    dve.wait_ge(sem("row_deviation"), NT * layer + t + 1)
                    dve.reciprocal(stats[:, t, 15:16], stats[:, t, 14:15]).then_inc(sem("row_inverse"), 1)
                    if layer == 0:
                        dve.wait_ge(sem("row_inverse"), t + 1)
                        dve.tensor_scalar(x_rows[:, t, :], x_rows[:, t, :], stats[:, t, 12:13],
                                          stats[:, t, 15:16], ALU.subtract, ALU.mult).then_inc(sem("row_normed"), 1)
                    else:
                        x = x_rows[:, t, 0:SPLIT]
                        then(dve.scalar_tensor_tensor(out=x, in0=x, scalar=stats[:, t, 12:13],
                                                      in1=affine[:, 2, 0:SPLIT], op0=ALU.subtract, op1=ALU.mult))
                        dve.wait_ge(sem("row_inverse"), NT + t + 1)
                        dve.scalar_tensor_tensor(out=x, in0=x, scalar=stats[:, t, 15:16], in1=affine[:, 3, 0:SPLIT],
                                                 op0=ALU.mult, op1=ALU.add).then_inc(sem("out_left"), 1)

            attention(0, SCALE_A)
            out_norm(0)
            for t in range(NT):
                name = ("back", t, 1)
                bank = filled(dve, name)
                for j in range(KD // 2):
                    dve.tensor_scalar(xT[:, 4 + j, t * P:(t + 1) * P], bank[:, j * P:(j + 1) * P],
                                      col("ln_g_2", 4 + j), col("ln_b_2", 4 + j), ALU.mult, ALU.add) \
                        .then_inc(read(name), 1)
            dve.wait_ge(sem("moba_in"), 16)
            half_hd = HD // 2
            for n in range(2):
                for j in range(KD):
                    name = ("raw", n, j)
                    bank = filled(dve, name)
                    partly_moved(dve, name, 1)
                    for lo in range(0, P, half_hd):
                        to = lo + half_hd if lo % HD == 0 else lo - half_hd
                        ins = dve.tensor_tensor(turned[to:to + half_hd, j, :], bank[lo:lo + half_hd, 0:T],
                                                ac[lo:lo + half_hd, A_SIN:A_SIN + T], ALU.mult)
                        if lo < P - half_hd:
                            steps[0] += 1
                            ins.then_inc(sem("vector_step"), 1)
                    ins.then_inc(read(name), 1)
                    moved(dve, name)
                    dve.wait_ge(sem("vector_step"), steps[0])
                    dve.wait_ge(sem("raw_cos"), KD * n + j + 1)
                    to = qb if n else kb
                    dve.tensor_tensor(to[:, j, :], raw_b[:, j, :], turned[:, j, :], ALU.add) \
                        .then_inc(sem("turned"), 1)
            attention(1, SCALE_B)
            out_norm(1)


_USED = ["x", "c", "ada_w", "ada_b", "norm_mix_g", "norm_ffn_g", "final_g", "conv_w_in", "conv_b_in",
         "conv_w_dw", "conv_b_dw", "conv_ln_g", "conv_ln_b", "conv_w_out", "moe_w_rg", "moe_b_rg",
         "moe_w_re", "moe_b_re", "moe_w_gate", "moe_w_up", "moe_w_down", "mla_w_in_2", "mla_q_norm_2",
         "mla_kv_norm_2", "mla_w_uq_2", "mla_w_ukv_2", "mla_w_o_2", "moba_w_kv_2", "moba_w_in_2",
         "moba_w_o_2", "ln_g_2", "ln_b_2"]


def shape_constants():
    base = np.concatenate([np.eye(P), np.ones((P, P))], 1)
    i = np.arange(P)
    route = np.concatenate([i[:, None] < i[None, :],
                            np.broadcast_to(np.arange(SLOTS_A), (P, SLOTS_A)),
                            np.broadcast_to(np.arange(P) % WIN, (P, P))], 1)
    mask = np.concatenate([np.zeros((P, P)), np.where(i[None, :] <= i[:, None], 0.0, -BIG)], 1)

    def tables(dim):
        inv = np.float32(10000.0) ** (-np.arange(0, dim, 2, dtype=np.float32) / np.float32(dim))
        ang = np.arange(T, dtype=np.float32)[None, :] * inv.astype(np.float32)[:, None]
        ang = np.concatenate([ang, ang], 0)
        return np.cos(ang), np.sin(ang)

    cos, sin = tables(ROPE)
    sign = np.where(np.arange(ROPE) < ROPE // 2, -1.0, 1.0)[:, None]
    mla = np.zeros((P, A_COLS))
    mla[:, 0:T] = mask
    mla[:, A_COS:A_COS + T] = np.tile(cos, (P // ROPE, 1))
    mla[:, A_SIN:A_SIN + T] = np.tile(sin * sign, (P // ROPE, 1))
    cos, sin = tables(HD)
    away = np.where(np.arange(HD) < HD // 2, 1.0, -1.0)[:, None]
    moba = np.concatenate([np.tile(cos, (2, 1)), np.tile(sin * away, (2, 1))], 1)
    return {"k_base": base, "k_route": route, "k_mla": mla, "k_moba": moba}


def kernel(**inputs):
    import concourse.bacc as bacc
    from concourse.bass_utils import run_bass_kernel_spmd

    nc = bacc.Bacc("TRN2", target_bir_lowering=False, num_devices=1)
    arrays, A = {}, {}
    given = {name: np.ascontiguousarray(inputs[name]) for name in _USED}
    for name, a in shape_constants().items():
        given[name] = np.ascontiguousarray(a.astype(np.float32))
    for name, a in given.items():
        arrays[f"in_{name}"] = a
        A[name] = nc.dram_tensor(f"in_{name}", a.shape, mybir.dt.from_np(a.dtype), kind="ExternalInput").ap()
    out = nc.dram_tensor("out_0", (1, T, D), F32, kind="ExternalOutput").ap()
    two_blocks(nc, A, out)
    r = run_bass_kernel_spmd(nc, [arrays], core_ids=[0])
    return r.results[0]["out_0"]
```
